# Optimizing a Trainium2 kernel written in Bass

```python
import jax, jax.numpy as jnp
from jax import lax
import numpy as np

D_MODEL = 1024
BATCH = 1
SEQ = 128
DEPTH = 2
DEC_BATCH = 1
DEC_SEQ = 512
PAST_LEN = 128

GRID_W = 64
N_MIXERS = 2
N_ML = (DEPTH + 1) // 2
N_MLA = DEPTH // 2
D_FF = 2816
EPS = 1e-6
ML_DI = 2 * D_MODEL
ML_NH = 4
ML_DH = ML_DI // ML_NH
ML_CONV_K = 5
ML_QKV_BLOCK = 4
ML_CHUNK = 64
MLA_NH = 8
MLA_NOPE = 128
MLA_ROPE = 64
MLA_DV = 128
MLA_QK = MLA_NOPE + MLA_ROPE
MLA_Q_LORA = 256
MLA_KV_LORA = 128
ROPE_THETA = 10000.0
ATTN_QBLOCK = 128

kernel_name = 'hybrid_mlstm_mla_flow_trunk'

def rms_norm(x, g):
    xf = x.astype(jnp.float32)
    y = xf * lax.rsqrt(jnp.mean(xf * xf, axis=-1, keepdims=True) + EPS)
    return (y * g.astype(jnp.float32)).astype(x.dtype)

def modulate(x, g, shift, scale):
    return rms_norm(x, g) * (1 + scale) + shift

def swiglu(x, w_in, w_out):
    a, b = jnp.split(x @ w_in, 2, axis=-1)
    return (jax.nn.silu(a) * b) @ w_out

def trunk_layer(x, mod, g3, w_in2, w_out2, mixer):
    sh1, sc1, ga1, sh2, sc2, ga2, sh3, sc3, ga3 = jnp.split(mod, 9, axis=-1)
    x = x + 0.5 * ga1 * swiglu(modulate(x, g3[0], sh1, sc1), w_in2[0], w_out2[0])
    y, aux = mixer(modulate(x, g3[1], sh2, sc2))
    x = x + ga2 * y
    x = x + 0.5 * ga3 * swiglu(modulate(x, g3[2], sh3, sc3), w_in2[1], w_out2[1])
    return x, aux

def grid_rope(n_tokens):
    rows = n_tokens // GRID_W
    r = jnp.repeat(jnp.arange(rows, dtype=jnp.float32), GRID_W)
    col = jnp.tile(jnp.arange(GRID_W, dtype=jnp.float32), rows)
    n_f = MLA_ROPE // 4
    freqs = jnp.power(ROPE_THETA, -jnp.arange(n_f, dtype=jnp.float32) / n_f)
    ang = jnp.concatenate([r[:, None] * freqs, col[:, None] * freqs], axis=-1)
    return jnp.cos(ang), jnp.sin(ang)

def apply_rope(x, cos, sin):
    x1, x2 = jnp.split(x, 2, axis=-1)
    cs = cos[None, :, None, :].astype(x.dtype)
    sn = sin[None, :, None, :].astype(x.dtype)
    return jnp.concatenate([x1 * cs - x2 * sn, x1 * sn + x2 * cs], axis=-1)

def block_attention(q, k, v):
    B, Tq, H, dk = q.shape
    nb = Tq // ATTN_QBLOCK
    qb = jnp.moveaxis(q.reshape(B, nb, ATTN_QBLOCK, H, dk), 1, 0)
    scale = dk ** -0.5

    def one_block(qi):
        s = jnp.einsum('bqhd,bkhd->bhqk', qi, k).astype(jnp.float32) * scale
        p = jax.nn.softmax(s, axis=-1).astype(v.dtype)
        return jnp.einsum('bhqk,bkhd->bqhd', p, v)

    o = lax.map(one_block, qb)
    return jnp.moveaxis(o, 0, 1).reshape(B, Tq, H, v.shape[-1])

def mla_queries(cq, q_norm_g, w_uq, q_g, rope):
    B, T, _ = cq.shape
    q = (rms_norm(cq, q_norm_g) @ w_uq).reshape(B, T, MLA_NH, MLA_QK)
    q = rms_norm(q, q_g)
    if rope is not None:
        q = jnp.concatenate([q[..., :MLA_NOPE], apply_rope(q[..., MLA_NOPE:], *rope)], axis=-1)
    return q

def mla_entry(kvr, kv_norm_g):
    return jnp.concatenate([rms_norm(kvr[..., :MLA_KV_LORA], kv_norm_g), kvr[..., MLA_KV_LORA:]], axis=-1)

def mla_keys_values(entry, w_ukv, k_g, rope):
    B, T, _ = entry.shape
    kv = (entry[..., :MLA_KV_LORA] @ w_ukv).reshape(B, T, MLA_NH, MLA_NOPE + MLA_DV)
    kr = jnp.broadcast_to(entry[:, :, None, MLA_KV_LORA:], (B, T, MLA_NH, MLA_ROPE))
    k = rms_norm(jnp.concatenate([kv[..., :MLA_NOPE], kr], axis=-1), k_g)
    if rope is not None:
        k = jnp.concatenate([k[..., :MLA_NOPE], apply_rope(k[..., MLA_NOPE:], *rope)], axis=-1)
    return k, kv[..., MLA_NOPE:]

def mla_mixer(xn, w_in, q_norm_g, w_uq, kv_norm_g, w_ukv, qk_g, w_o, ctx_entry, rope):
    B, T, _ = xn.shape
    h = xn @ w_in
    q = mla_queries(h[..., :MLA_Q_LORA], q_norm_g, w_uq, qk_g[0], rope)
    entry = mla_entry(h[..., MLA_Q_LORA:], kv_norm_g)
    k, v = mla_keys_values(entry, w_ukv, qk_g[1], rope)
    if ctx_entry is not None:
        kc, vc = mla_keys_values(ctx_entry, w_ukv, qk_g[1], None)
        k = jnp.concatenate([k, kc], axis=1)
        v = jnp.concatenate([v, vc], axis=1)
    o = block_attention(q, k, v).reshape(B, T, MLA_NH * MLA_DV)
    return o @ w_o, entry

def centred_dwconv(x, w, b):
    kw = w.shape[0]
    y = lax.conv_general_dilated(x, w[:, None, :], window_strides=(1,), padding=[(kw // 2, kw // 2)],
                                 dimension_numbers=('NWC', 'WIO', 'NWC'), feature_group_count=x.shape[-1])
    return y + b

def headwise(x, w):
    B, T, _ = x.shape
    return jnp.einsum('btni,nio->btno', x.reshape(B, T, -1, ML_QKV_BLOCK), w).reshape(B, T, ML_DI)

def to_heads(x):
    B, T, _ = x.shape
    return x.reshape(B, T, ML_NH, ML_DH).transpose(0, 2, 1, 3).astype(jnp.float32)

def mlstm_scan(q, k, v, ig, lf, C0, n0, m0):
    B, H, T, DH = q.shape
    nc = T // ML_CHUNK

    def chunks(a):
        return jnp.moveaxis(a.reshape(a.shape[:2] + (nc, ML_CHUNK) + a.shape[3:]), 2, 0)

    causal = jnp.tril(jnp.ones((ML_CHUNK, ML_CHUNK), dtype=bool))

    def step(carry, inp):
        C, n, m = carry
        qc, kc, vc, ic, fc = inp
        b = jnp.cumsum(fc, axis=-1)
        dlog = jnp.where(causal, b[..., :, None] - b[..., None, :] + ic[..., None, :], -jnp.inf)
        inter = b + m[..., None]
        m_row = jnp.maximum(jnp.max(dlog, axis=-1), inter)
        s = jnp.einsum('bhjd,bhtd->bhjt', qc, kc) * jnp.exp(dlog - m_row[..., None])
        decay = jnp.exp(inter - m_row)
        num = decay[..., None] * jnp.einsum('bhvk,bhjk->bhjv', C, qc) + jnp.einsum('bhjt,bhtv->bhjv', s, vc)
        den = decay * jnp.einsum('bhk,bhjk->bhj', n, qc) + jnp.sum(s, axis=-1)
        h = num / jnp.maximum(jnp.abs(den), jnp.exp(-m_row))[..., None]
        b_last = b[..., -1]
        wlog = b_last[..., None] - b + ic
        m_new = jnp.maximum(b_last + m, jnp.max(wlog, axis=-1))
        w = jnp.exp(wlog - m_new[..., None])
        carry_decay = jnp.exp(b_last + m - m_new)
        C_new = carry_decay[..., None, None] * C + jnp.einsum('bhtv,bhtk->bhvk', vc * w[..., None], kc)
        n_new = carry_decay[..., None] * n + jnp.einsum('bht,bhtk->bhk', w, kc)
        return (C_new, n_new, m_new), h

    init = (C0.astype(jnp.float32), n0.astype(jnp.float32), m0.astype(jnp.float32))
    (C, n, m), h = lax.scan(step, init, (chunks(q), chunks(k), chunks(v), chunks(ig), chunks(lf)))
    h = jnp.moveaxis(h, 0, 2).reshape(B, H, T, DH)
    return h, C, n, m

def mlstm_mixer(xn, w_up, conv_w, conv_b, w_qkv, w_gate, b_gate, head_g, skip, w_down, init):
    B, T, _ = xn.shape
    xm, z = jnp.split(xn @ w_up, 2, axis=-1)
    xc = jax.nn.silu(centred_dwconv(xm, conv_w, conv_b))
    q = headwise(xc, w_qkv[0])
    k = headwise(xc, w_qkv[1])
    v = headwise(xm, w_qkv[2])
    g = jnp.einsum('btc,dcg->dbtg', jnp.concatenate([q, k, v], axis=-1), w_gate) + b_gate[:, None, None, :]
    g = jnp.moveaxis(g.astype(jnp.float32), -1, 2)
    ig = g[:, :, :ML_NH]
    lf = jax.nn.log_sigmoid(g[:, :, ML_NH:])
    qh = to_heads(q) * ML_DH ** -0.5
    kh = to_heads(k)
    vh = to_heads(v)
    C0, n0, m0 = init
    h_f, Cf, nf, mf = mlstm_scan(qh, kh, vh, ig[0], lf[0], C0[:, 0], n0[:, 0], m0[:, 0])
    flip = lambda a: jnp.flip(a, axis=2)
    h_b, Cb, nb, mb = mlstm_scan(flip(qh), flip(kh), flip(vh), flip(ig[1]), flip(lf[1]), C0[:, 1], n0[:, 1], m0[:, 1])
    h = (h_f + flip(h_b)).transpose(0, 2, 1, 3)
    h = rms_norm(h, head_g.reshape(ML_NH, ML_DH)).reshape(B, T, ML_DI).astype(xn.dtype)
    out = ((h + skip * xc) * jax.nn.silu(z)) @ w_down
    return out, (jnp.stack([Cf, Cb], axis=1), jnp.stack([nf, nb], axis=1), jnp.stack([mf, mb], axis=1))

def setup_inputs(seed: int = 0) -> dict:
    key = jax.random.key(seed)
    ks = iter(jax.random.split(key, 40))

    def nrm(shape, scale):
        return jax.random.normal(next(ks), shape, jnp.float32) * scale

    def gain(shape):
        return 1.0 + nrm(shape, 0.02)

    b_gate = jnp.concatenate([nrm((N_ML, 2, ML_NH), 0.1),
                              jnp.linspace(3.0, 6.0, ML_NH, dtype=jnp.float32) + nrm((N_ML, 2, ML_NH), 0.1)], axis=-1)
    return {
        'x_prompt': nrm((BATCH, SEQ, D_MODEL), 1.0),
        'x_sample': nrm((DEC_BATCH, DEC_SEQ, D_MODEL), 1.0),
        'state_mlstm_C': nrm((DEC_BATCH, N_ML, 2, ML_NH, ML_DH, ML_DH), 0.05),
        'state_mlstm_n': nrm((DEC_BATCH, N_ML, 2, ML_NH, ML_DH), 0.1),
        'state_mlstm_m': nrm((DEC_BATCH, N_ML, 2, ML_NH), 1.0),
        'cache_mla': nrm((DEC_BATCH, N_MLA, PAST_LEN, MLA_KV_LORA + MLA_ROPE), 1.0),
        'c': nrm((DEC_BATCH, D_MODEL), 1.0),
        'c_ctx': nrm((D_MODEL,), 1.0),
        'w_mod': nrm((DEPTH, D_MODEL, 9 * D_MODEL), 0.5 * D_MODEL ** -0.5),
        'b_mod': nrm((DEPTH, 9 * D_MODEL), 0.02),
        'norm_g': gain((DEPTH, 3, D_MODEL)),
        'ffn_w_in': nrm((DEPTH, 2, D_MODEL, 2 * D_FF), D_MODEL ** -0.5),
        'ffn_w_out': nrm((DEPTH, 2, D_FF, D_MODEL), D_FF ** -0.5),
        'ml_w_up': nrm((N_ML, D_MODEL, 2 * ML_DI), D_MODEL ** -0.5),
        'ml_conv_w': nrm((N_ML, ML_CONV_K, ML_DI), ML_CONV_K ** -0.5),
        'ml_conv_b': nrm((N_ML, ML_DI), 0.01),
        'ml_w_qkv': nrm((N_ML, 3, ML_DI // ML_QKV_BLOCK, ML_QKV_BLOCK, ML_QKV_BLOCK), ML_QKV_BLOCK ** -0.5),
        'ml_w_gate': nrm((N_ML, 2, 3 * ML_DI, 2 * ML_NH), (3 * ML_DI) ** -0.5),
        'ml_b_gate': b_gate,
        'ml_head_g': gain((N_ML, ML_DI)),
        'ml_skip': gain((N_ML, ML_DI)),
        'ml_w_down': nrm((N_ML, ML_DI, D_MODEL), ML_DI ** -0.5),
        'mla_w_in': nrm((N_MLA, D_MODEL, MLA_Q_LORA + MLA_KV_LORA + MLA_ROPE), D_MODEL ** -0.5),
        'mla_q_norm_g': gain((N_MLA, MLA_Q_LORA)),
        'mla_w_uq': nrm((N_MLA, MLA_Q_LORA, MLA_NH * MLA_QK), MLA_Q_LORA ** -0.5),
        'mla_kv_norm_g': gain((N_MLA, MLA_KV_LORA)),
        'mla_w_ukv': nrm((N_MLA, MLA_KV_LORA, MLA_NH * (MLA_NOPE + MLA_DV)), MLA_KV_LORA ** -0.5),
        'mla_qk_g': gain((N_MLA, 2, MLA_QK)),
        'mla_w_o': nrm((N_MLA, MLA_NH * MLA_DV, D_MODEL), (MLA_NH * MLA_DV) ** -0.5),
    }

def reference(x_prompt, x_sample, state_mlstm_C, state_mlstm_n, state_mlstm_m, cache_mla, c, c_ctx,
              w_mod, b_mod, norm_g, ffn_w_in, ffn_w_out,
              ml_w_up, ml_conv_w, ml_conv_b, ml_w_qkv, ml_w_gate, ml_b_gate, ml_head_g, ml_skip, ml_w_down,
              mla_w_in, mla_q_norm_g, mla_w_uq, mla_kv_norm_g, mla_w_ukv, mla_qk_g, mla_w_o):
    rope = grid_rope(x_sample.shape[1])
    b_ctx = x_prompt.shape[0]
    zero_state = (jnp.zeros((b_ctx, 2, ML_NH, ML_DH, ML_DH), jnp.float32),
                  jnp.zeros((b_ctx, 2, ML_NH, ML_DH), jnp.float32),
                  jnp.zeros((b_ctx, 2, ML_NH), jnp.float32))
    yp, ys = x_prompt, x_sample
    new_C, new_n, new_m, new_kv = [], [], [], []
    for i in range(DEPTH):
        j = i // N_MIXERS
        mod_ctx = (jax.nn.silu(c_ctx) @ w_mod[i] + b_mod[i])[None, None, :]
        mod_lat = (jax.nn.silu(c) @ w_mod[i] + b_mod[i])[:, None, :]
        if i % N_MIXERS == 0:
            ml_args = (ml_w_up[j], ml_conv_w[j], ml_conv_b[j], ml_w_qkv[j], ml_w_gate[j], ml_b_gate[j],
                       ml_head_g[j], ml_skip[j], ml_w_down[j])
            lat_init = (state_mlstm_C[:, j], state_mlstm_n[:, j], state_mlstm_m[:, j])
            yp, st = trunk_layer(yp, mod_ctx, norm_g[i], ffn_w_in[i], ffn_w_out[i],
                                 lambda xn: mlstm_mixer(xn, *ml_args, zero_state))
            ys, _ = trunk_layer(ys, mod_lat, norm_g[i], ffn_w_in[i], ffn_w_out[i],
                                lambda xn: mlstm_mixer(xn, *ml_args, lat_init))
            new_C.append(st[0])
            new_n.append(st[1])
            new_m.append(st[2])
        else:
            mla_args = (mla_w_in[j], mla_q_norm_g[j], mla_w_uq[j], mla_kv_norm_g[j], mla_w_ukv[j], mla_qk_g[j], mla_w_o[j])
            yp, entry = trunk_layer(yp, mod_ctx, norm_g[i], ffn_w_in[i], ffn_w_out[i],
                                    lambda xn: mla_mixer(xn, *mla_args, None, None))
            ys, _ = trunk_layer(ys, mod_lat, norm_g[i], ffn_w_in[i], ffn_w_out[i],
                                lambda xn: mla_mixer(xn, *mla_args, cache_mla[:, j], rope))
            new_kv.append(entry)
    return (yp, ys, jnp.stack(new_C, axis=1), jnp.stack(new_n, axis=1), jnp.stack(new_m, axis=1), jnp.stack(new_kv, axis=1))


_drawn_inputs = setup_inputs


def setup_inputs(seed=0):
    import zlib

    import numpy as np

    out = dict(_drawn_inputs(seed))
    spreads = {}
    factors = {'state_mlstm_C': 8.0,
     'state_mlstm_n': 8.0,
     'state_mlstm_m': 8.0,
     'cache_mla': 6.436,
     'ml_conv_b': 3.425,
     'ml_head_g': 8.0,
     'ml_skip': 8.0,
     'mla_q_norm_g': 8.0,
     'mla_kv_norm_g': 3.911,
     'mla_qk_g': 8.0}
    for name, (base, spread) in spreads.items():
        noise = np.random.default_rng([zlib.crc32(name.encode()), seed]).standard_normal(out[name].shape)
        drawn = base * np.exp(spread * noise) if base else spread * noise
        out[name] = __import__('jax').numpy.asarray(drawn.astype(out[name].dtype))
    for name, factor in factors.items():
        out[name] = (out[name] * factor).astype(out[name].dtype)
    return out
```

```python
from contextlib import ExitStack

import concourse.bass as bass
from concourse import mybir
import numpy as np

F32 = mybir.dt.float32
F32R = mybir.dt.float32r
ALU = mybir.AluOpType
ACT = mybir.ActivationFunctionType
AX_X = mybir.AxisListType.X

P = 128
D = 1024
KD = D // P
NP_ = 128
NL = 512
T = NP_ + NL
TH = T // 2
FF = 2816
MF = FF // P
HALVES = (12, MF - 12)
PIECE = 16 * P
DI = 2048
NT = DI // P
NH = 4
DH = DI // NH
HT = DH // P
CONV = 5
GAP = CONV // 2
TG = T + GAP
AH = 8
QK = 192
QL = 256
KV = 128
PAST = 128
TK = T + PAST
EPS = 1e-6
N_MOD = 36
N_FIRST = 5
SEG = ((0, NP_, 0), (NP_, T, 1))


def mm3(pe, out, w_hi, w_lo, x_hi, x_lo, first, last):
    pe.matmul(out, w_hi, x_hi, start=first, stop=False)
    pe.matmul(out, w_hi, x_lo, start=False, stop=False)
    return pe.matmul(out, w_lo, x_hi, start=False, stop=last)


def plan():
    seq = []
    q = c = n_norm = n_hid = n_mod = 0

    def add(kind, pieces, mods=0, **kw):
        nonlocal q, c, n_mod
        seq.append(dict(kind=kind, q=q, n=pieces, c=c, mods=mods, mod=n_mod, off=c - q // 2, **kw))
        q += pieces
        c += pieces // 2 + mods
        n_mod += mods

    def norm(sub, early=True):
        nonlocal n_norm
        add("norm", 0, 0, sub=sub, at=n_norm, early=early)
        n_norm += 1

    def ffn(f, sub, with_mod):
        nonlocal n_hid
        for half, tiles in enumerate(HALVES):
            k = 0
            for n, mods in ((2 * with_mod[half], with_mod[half]), (tiles - 2 * with_mod[half], 0)):
                if n:
                    add("in", n, mods, f=f, pair=(half * HALVES[0] + k) // 2, k0=k, hid=n_hid, norm=n_norm - 1)
                    n_hid += n
                    k += n
            add("out", KD, f=f, half=half, tiles=tiles, sub=sub, hid=n_hid, stats=n_norm if half else None)

    add("mod", 0, N_FIRST)
    norm(0)
    ffn(0, 0, (6, 5))
    norm(1)
    add("up", NT)
    add("gates", 0)
    add("heads", 2 * NH, sub=1)
    norm(2, early=False)
    ffn(1, 2, (6, 5))
    norm(3)
    ffn(2, 3, (6, 3))
    norm(4)
    add("attn_in", 2)
    add("attn_q", 2)
    add("attn_kv", 2)
    add("attn", 0)
    add("attn_out", 4, sub=4, stats=n_norm)
    norm(5)
    ffn(3, 5, (0, 0))
    seq[-1]["stats"] = None
    assert n_mod == N_MOD
    return seq


SIZE = {"in": PIECE, "up": PIECE, "heads": PIECE, "attn_in": PIECE, "attn_q": 12 * P,
        "attn_kv": 8 * P, "attn_out": PIECE}


def size_of(phase):
    return phase["tiles"] * P if phase["kind"] == "out" else SIZE[phase["kind"]]


def build(nc, t, stop=None):
    with ExitStack() as ctx:
        def sb(name, shape, dt=F32):
            return ctx.enter_context(nc.sbuf_tensor(name, shape, dt))

        def sem(name):
            return ctx.enter_context(nc.semaphore(name))

        seq = plan()
        if stop is not None:
            seq = seq[:stop]
        for n, ph in enumerate(seq):
            after = seq[n + 1] if n + 1 < len(seq) else None
            ph["next"] = size_of(after) if after and after["n"] else None
            ph["next_c"] = after["c"] if after else None
            ph["next_mod"] = after["mod"] if after and after["mods"] else None
            ph["after_norm"] = n > 0 and seq[n - 1]["kind"] == "norm"
            if ph["kind"] in ("up", "heads", "gates"):
                ph["next"] = None

        x = sb("x", [P, KD, T])
        w_hi = sb("w_hi", [P, 2, PIECE], F32R)
        w_lo = sb("w_lo", [P, 2, PIECE], F32R)
        mod = sb("mod", [P, 2 * 72, 2])
        bmod = sb("bmod", [P, 2 * 72, 2])
        norm_g = sb("norm_g", [P, 48, 2])
        cvec = sb("cvec", [P, KD, 2])
        csilu = sb("csilu", [P, KD, 2])
        c4 = sb("c4", [P, KD, 4], F32R)
        mod_rows = sb("mod_rows", [36, 2 * P])
        scale_v = sb("scale_v", [P, KD, 2])
        gate_v = sb("gate_v", [P, KD, 2])
        eps_v = sb("eps_v", [P, 1])
        ones = sb("ones", [P, P])
        cst = sb("cst", [P, 8 * P + 36])
        ident, upto, downto, bias_f, bias_b, sel_a, sel_b, rot = (cst[:, i * P:(i + 1) * P] for i in range(8))
        bdmask = cst[:, 8 * P:8 * P + 32]
        sum_parts = cst[0:36, 8 * P + 32:]
        mlp = sb("mlp", [P, NT * (CONV + 3)])
        conv_w = mlp[:, 0:NT * CONV].rearrange("p (t k) -> p t k", k=CONV)
        conv_b, head_g, skip = (mlp[:, NT * (CONV + i):NT * (CONV + i + 1)] for i in range(3))
        wq3 = sb("wq3", [P, 3, NT, 4])
        bgate = sb("bgate", [P, 16])
        m0 = sb("m0", [P, 8])
        n0 = sb("n0", [P, NH, 8])
        m0row = sb("m0row", [4, 2])
        a_col = sb("a_col", [P, 5, 2, 4])
        attn_g = sb("attn_g", [P, 8])
        soft = sb("soft", [P, 8])
        psum = ctx.enter_context(nc.psum_tensor("psum", [P, 8, 512], F32))

        base = (nc.sbuf_base + 31) // 32 * 32
        raw = nc.alloc_sbuf_tensor_at("raw", [P, 2, 2, PIECE], F32, offset=base)
        raw_lo = nc.alloc_sbuf_tensor_at("raw_lo", [P, 2, 2, PIECE], F32R, offset=base)
        base += 16 * PIECE
        arena_kb = (nc.sbuf_usable_end - base) // 1024

        def at(name, kb, shape, dt=F32):
            size = 4
            for n in shape[1:]:
                size *= n
            assert kb * 1024 + size <= arena_kb * 1024, (name, arena_kb)
            return nc.alloc_sbuf_tensor_at(name, shape, dt, offset=base + int(kb * 1024))

        xn_hi = at("xn_hi", 0, [P, KD, T], F32R)
        xn_lo = at("xn_lo", 20, [P, KD, T], F32R)
        hid_hi = at("hid_hi", 40, [P, HALVES[0], T], F32R)
        hid_lo = at("hid_lo", 70, [P, HALVES[0], T], F32R)
        hid_f = at("hid_f", 70, [P, HALVES[0], T])
        silu_s = at("silu_s", 100, [P, 2, T])
        mod_hi = at("mod_hi", 105, [P, PIECE], F32R)
        sq = at("sq", 100, [P, 2, T])
        acc = at("acc", 0, [P, T])
        root = at("root", 45, [P, T])
        rstd = at("rstd", 47.5, [P, T])
        nrm = at("nrm", 50, [P, 2, T])
        wgr = at("wgr", 64, [P, 3, 2, NT, 32])
        gate_w = at("gate_w", 80, [P, 2, NT, 16])
        gtmp = at("gtmp", 76, [P, NT, 16])
        xm_pad = at("xm_pad", 40, [P, 2, TG + 2 * GAP])
        conv = at("conv", 46, [P, 2, TG])
        xc_s = at("xc_s", 52, [P, 2, T])
        z_s = at("z_s", 57, [P, 2, T])
        gt = at("gt", 64, [P, 10, 8])
        g_abs = at("g_abs", 65, [P, 10, 4])
        g_exp = at("g_exp", 66, [P, 10, 4])
        g_ln = at("g_ln", 67, [P, 10, 4])
        logf = at("logf", 68, [P, 10, 4])
        b_col = at("b_col", 69, [P, 10, 4])
        a_row = at("a_row", 70, [4, 2, T])
        b_row = at("b_row", 75, [4, 2, T])
        m_row = at("m_row", 80, [4, 2, T])
        s_row = at("s_row", 85, [4, 2, T])
        rows = at("rows", 90, [4, 4, T])
        m_new = at("m_new", 100, [4, 2])
        xm_h = at("xm_h", 0, [P, HT, T])
        alpha = at("alpha", 0, [P, 2, NL])
        rden = at("rden", 4, [P, 2, T])
        se_p = at("se_p", 9, [P, 2, P])
        xc_h = at("xc_h", 10, [P, HT, T])
        w_tok = at("w_tok", 20, [P, 2])
        vw = at("vw", 22, [P, 2, DH])
        nq_d = at("nq_d", 22, [P, 2, NL])
        k_tok = at("k_tok", 26, [P, DH])
        h_tmp = at("h_tmp", 26, [P, NL])
        q_t = at("q_t", 28, [P, HT, T])
        k_t = at("k_t", 38, [P, HT, T])
        y_hi = at("y_hi", 28, [P, HT, T], F32R)
        y_lo = at("y_lo", 38, [P, HT, T], F32R)
        v_tok = at("v_tok", 48, [P, 5, DH])
        c_out = at("c_out", 58, [P, 2, DH])
        se_f = at("se_f", 58, [P, 4, NL])
        se_b = at("se_b", 66, [P, 4, NL])
        zs_h = at("zs_h", 66, [P, HT, T])
        c_t = at("c_t", 76, [P, 2, HT, DH])
        h_sq = at("h_sq", 76, [P, 2, T])
        h_root = at("h_root", 81, [P, T])
        h_rstd = at("h_rstd", 83.5, [P, T])
        h_t = at("h_t", 92, [P, HT, T])
        bd = at("bd", 92, [P, 3, HT, P])
        n_bc = at("n_bc", 98, [P, 8, P])
        bc = at("bc", 102, [P, 4, T])
        c_sq = at("c_sq", 40, [P, 2, T])
        pt = at("pt", 0, [P, 5, NL])
        prob = at("prob", 10, [P, 2, T])
        v_h = at("v_h", 15, [P, 6, P])
        qs = at("qs", 18, [P, T])
        ks = at("ks", 20.5, [P, TK])
        kn_raw = at("kn_raw", 24, [P, AH, TK])
        qn_raw = at("qn_raw", 48, [P, AH, T])
        qr_raw = at("qr_raw", 68, [P, AH // 2, T])
        cq = at("cq", 78, [P, 2, T])
        ent = at("ent", 83, [P, TK])
        kr = at("kr", 86, [P, TK])
        cq_hi = at("cq_hi", 89, [P, 2, T], F32R)
        cq_lo = at("cq_lo", 94, [P, 2, T], F32R)
        ent_hi = at("ent_hi", 99, [P, TK], F32R)
        ent_lo = at("ent_lo", 102, [P, TK], F32R)
        k_rot = at("k_rot", 105, [P, TK])
        kr_ss = at("kr_ss", 108, [P, TK])
        a_sq = at("a_sq", 78, [P, TK])
        a_root = at("a_root", 81, [P, TK])
        r_q = at("r_q", 84, [P, T])
        r_k = at("r_k", 86.5, [P, TK])
        ropes = at("ropes", 89.5, [P, 2, NL])
        krs = at("krs", 93.5, [P, TK])
        qrs = at("qrs", 96.5, [P, T])
        o_hi = at("o_hi", 48, [P, AH, T], F32R)
        o_lo = at("o_lo", 24, [P, AH, T], F32R)

        xm_d = nc.dram_tensor("xm_d", (NT, P, T), F32, kind="Internal").ap()
        xc_d = nc.dram_tensor("xc_d", (NT, P, T), F32, kind="Internal").ap()
        z_d = nc.dram_tensor("z_d", (NT, P, T), F32, kind="Internal").ap()
        rows_d = nc.dram_tensor("rows_d", (NH, 4, T), F32, kind="Internal").ap()

        raw_in, mod_in, hi_done, lo_done, used, freed = (sem(n) for n in ("raw_in", "mod_in", "hi_done", "lo_done", "used", "freed"))
        mod_hi_done, mod_lo_done, mod_used, mod_copied, mod_turned, mod_freed = (
            sem(n) for n in ("mod_hi_done", "mod_lo_done", "mod_used", "mod_copied", "mod_turned", "mod_freed"))
        rows_set = sem("rows_set")
        in_c, in_bmod, in_cst, in_x = sem("in_c"), sem("in_bmod"), sem("in_cst"), sem("in_x")
        eps_set, ones_set, c_act, c_ready = sem("eps_set"), sem("ones_set"), sem("c_act"), sem("c_ready")
        vec_ready, gate_ready, sq_ready, acc_set, acc_ready = (
            sem(n) for n in ("vec_ready", "gate_ready", "sq_ready", "acc_set", "acc_ready"))
        ss_ready, root_ready, rstd_ready, nrm_ready = sem("ss_ready"), sem("root_ready"), sem("rstd_ready"), sem("nrm_ready")
        xhi_ready, xn_ready = sem("xhi_ready"), sem("xn_ready")
        silu_ready, mul_ready, hid_ready = sem("silu_ready"), sem("mul_ready"), sem("hid_ready")
        y_out = sem("y_out")

        def bank2(b):
            return psum[:, b:b + 2, 0:TH]

        def half(ap, n):
            return ap[..., n * TH:(n + 1) * TH]

        def two(ap):
            return ap.rearrange("p (h n) -> p h n", h=2)

        PARTS = ((0, 0, NP_, 0), (0, NP_, TH, 1), (1, 0, TH, 1))

        leaves = []
        for ph in seq:
            for i in range(max(ph["n"] // 2, ph["mods"])):
                if ph["n"]:
                    leaves.append(("w", ph["q"] + 2 * i + 2))
                if ph["mods"]:
                    leaves.append(("mod", 2 * (ph["mod"] + i) + 2))

        in_wgr, gw_tmp = sem("in_wgr"), sem("gw_tmp")
        xm_acc, xm_ready, z_ready, conv_ready, xc_ready = sem("xm_acc"), sem("xm_ready"), sem("z_ready"), sem("conv_ready"), sem("xc_ready")
        pad_set, gate_mm = sem("pad_set"), sem("gate_mm")
        xm_out, xc_out, z_out = ([sem(f"{n}_out{par}") for par in range(2)] for n in ("xm", "xc", "z"))
        conv_tap = sem("conv_tap")
        g_dve, g_act, g_pe, rows_out, m_out = sem("g_dve"), sem("g_act"), sem("g_pe"), sem("rows_out"), sem("m_out")
        in_xm, in_xc, in_bc, in_ct, in_z = sem("in_xm"), sem("in_xc"), sem("in_bc"), sem("in_ct"), sem("in_z")
        bd_ready, qk_mm, qk_ev, kt_mm, kt_ev, v_mm, v_ev = (sem(n) for n in ("bd_ready", "qk_mm", "qk_ev", "kt_mm", "kt_ev", "v_mm", "v_ev"))
        wt_ready, vw_ready, cn_mm, cn_ev = (sem(n) for n in ("wt_ready", "vw_ready", "cn_mm", "cn_ev"))
        cn_out = [sem("cn_out0"), sem("cn_out1")]
        s_mm, nq_mm, nq_ev, arg_ready, e_ready, dec_ready, se_ready = (sem(n) for n in ("s_mm", "nq_mm", "nq_ev", "arg_ready", "e_ready", "dec_ready", "se_ready"))
        den_mm, den_step, w_ready, g_mm, g_ev, h_step = (sem(n) for n in ("den_mm", "den_step", "w_ready", "g_mm", "g_ev", "h_step"))
        h_mm, h_ready, hsq_ready, hsq_used, hroot_ready, hrstd_ready = (sem(n) for n in ("h_mm", "h_ready", "hsq_ready", "hsq_used", "hroot_ready", "hrstd_ready"))
        y_step, y_ready, wd_mm, wd_ev = sem("y_step"), sem("y_ready"), sem("wd_mm"), sem("wd_ev")

        S_ML = float(DH) ** -0.5
        cn_slots = (2, NH * 10)

        def gated_tile(buf, par):
            return buf[:, par, :]

        def lat(j):
            return slice(j * P, (j + 1) * P)

        def pe_up(pe, ph):
            q0, n_at = ph["q"], 1

            def gate_sums(tt, first, last_):
                pe.wait_ge(xc_ready, tt + 1)
                for j in range(5):
                    a, b = j * P, (j + 1) * P
                    g = a + (GAP if j else 0) + GAP
                    for src, (lhs, w) in enumerate(((xc_s[:, first % 2, a:b], 0), (xm_pad[:, first % 2, g:g + P], 1))):
                        last = pe.matmul(psum[:, 4, 16 * j:16 * j + 16], lhs, gate_w[:, w, tt, :],
                                         start=(first == 0 and j == 0 and src == 0), stop=(last_ and src == 1),
                                         skip_group_check=True)
                last.then_inc(gate_mm, 1)

            def tile(q, par, tt):
                pe.wait_ge(lo_done, q + 1)
                for side in range(2):
                    if side == 0:
                        if not isinstance(tt, int) or tt:
                            pe.wait_ge(xm_ready, tt)
                    else:
                        pe.wait_ge(freed, q)
                        if isinstance(tt, int):
                            pe.wait_ge(mod_freed, ph["mod"])
                    for k in range(KD):
                        if side == 0:
                            pe.wait_ge(xn_ready, KD * n_at + k + 1)
                        s = slice((k * 2 + side) * P, (k * 2 + side + 1) * P)
                        for n in range(2):
                            last = mm3(pe, psum[:, 2 * side + n, 0:TH], w_hi[:, par, s], w_lo[:, par, s],
                                       half(xn_hi[:, k, :], n), half(xn_lo[:, k, :], n), k == 0, k == KD - 1)
                    last.then_inc(xm_acc if side == 0 else used, 1)

            tile(q0, 0, 0)
            tile(q0 + 1, 1, 1)
            pe.wait_ge(gw_tmp, 44)
            gate_sums(0, 0, False)
            with pe.Fori(1, NT // 2) as i:
                tile(2 * i + q0, 0, 2 * i)
                gate_sums(2 * i - 1, 3, False)
                tile(2 * i + (q0 + 1), 1, 2 * i + 1)
                gate_sums(2 * i, 2, False)
            gate_sums(NT - 1, NT - 1, True)

        def pe_gates(pe, ph):
            pe.wait_ge(g_dve, 4)
            for j in range(5):
                for d, tri in enumerate((upto, downto)):
                    out = psum[:, 5, 8 * j + 4 * d:8 * j + 4 * d + 4]
                    others = [] if j == 0 else [s for s in range(1, 5) if (s < j if d == 0 else s > j)]
                    last = pe.matmul(out, tri, logf[:, 2 * j + d, :], start=True, stop=not others)
                    for s in others:
                        last = pe.matmul(out, ones[:], logf[:, 2 * s + d, :], start=False, stop=(s == others[-1]))
            last.then_inc(g_pe, 1)
            pe.wait_ge(g_dve, 6)
            for src, col in enumerate((a_col, b_col)):
                for d in range(2):
                    for j in range(5):
                        c_in = a_col[:, j, d, :] if src == 0 else b_col[:, 2 * j + d, :]
                        out = psum[0:4, 2 * src + d, (j - 1) * P:j * P] if j else psum[0:4, 6, (2 * src + d) * P:(2 * src + d + 1) * P]
                        last = pe.transpose(out, c_in, ident)
            last.then_inc(g_pe, 1)

        def pe_heads(pe, ph):
            q0 = ph["q"]
            with pe.Fori(0, NH) as h:
                pe.wait_ge(freed, 2 * h + q0)
                pe.wait_ge(bd_ready, h + 1)
                pe.wait_ge(in_xc, 16 * h + 16)
                for n in range(2 * HT):
                    if n >= 2:
                        pe.wait_ge(qk_ev, 2 * HT * h + (n - 1))
                    for b in range(2):
                        last = pe.matmul(psum[:, 2 * (n % 2) + b, 0:TH], bd[:, n // HT, n % HT, :],
                                         half(xc_h[:, n % HT, :], b), start=True, stop=True)
                    last.then_inc(qk_mm, 1)
                for k in range(HT):
                    last = pe.matmul(psum[:, 6, k * P:(k + 1) * P], xc_h[:, k, 0:P], bd[:, 1, k, :], start=True, stop=True)
                last.then_inc(kt_mm, 1)
                pe.wait_ge(in_xm, 16 * h + 16)
                for j in range(5):
                    if j >= 2:
                        pe.wait_ge(v_ev, 5 * h + (j - 1))
                    for k in range(HT):
                        last = pe.matmul(psum[:, 4 + j % 2, k * P:(k + 1) * P], xm_h[:, k, j * P:(j + 1) * P],
                                         bd[:, 2, k, :], start=True, stop=True)
                    last.then_inc(v_mm, 1)
                pe.wait_ge(vw_ready, h + 1)
                pe.wait_ge(kt_ev, h + 1)
                for n in range(10):
                    if n >= 2:
                        pe.wait_ge(cn_ev, 10 * h + (n - 1))
                    if n < 8:
                        last = pe.matmul(psum[:, 6 + n % 2, :], vw[:, n // HT, (n % HT) * P:(n % HT + 1) * P],
                                         k_tok[:], start=True, stop=True)
                    else:
                        last = pe.matmul(psum[0:1, 6 + n % 2, :], w_tok[:, n - 8:n - 7], k_tok[:], start=True, stop=True)
                    last.then_inc(cn_mm, 1)
                pe.wait_ge(qk_ev, 2 * HT * h + 2 * HT)
                for j in range(4):
                    for k in range(HT):
                        last = pe.matmul(psum[:, j, :], k_t[:, k, lat(j + 1)], q_t[:, k, NP_:T], start=(k == 0), stop=(k == HT - 1))
                pe.wait_ge(cn_ev, 10 * h + 10)
                for k in range(HT):
                    last = pe.matmul(psum[:, 6, 0:P], k_t[:, k, 0:P], q_t[:, k, 0:P], start=(k == 0), stop=(k == HT - 1))
                last.then_inc(s_mm, 1)
                pe.wait_ge(v_ev, 5 * h + 5)
                for d in range(2):
                    for k in range(HT):
                        last = pe.matmul(psum[:, 4 + d, :], n_bc[:, HT * d + k, :], q_t[:, k, NP_:T], start=(k == 0), stop=(k == HT - 1))
                last.then_inc(nq_mm, 1)
                pe.wait_ge(nq_ev, h + 1)
                pe.wait_ge(se_ready, h + 1)
                for k in range(4):
                    pe.matmul(psum[:, 4, k * P:NL], ones[:], se_f[:, k, k * P:NL], start=(k == 0), stop=(k == 3))
                for k in (3, 2, 1, 0):
                    pe.matmul(psum[:, 5, 0:(k + 1) * P], ones[:], se_b[:, k, 0:(k + 1) * P], start=(k == 3), stop=(k == 0))
                for d in range(2):
                    last = pe.matmul(psum[:, 6, d * P:(d + 1) * P], ones[:], se_p[:, d, :], start=True, stop=True)
                last.then_inc(den_mm, 1)
                pe.wait_ge(in_ct, 16 * h + 16)
                for n in range(8):
                    if n >= 4:
                        pe.wait_ge(g_ev, 8 * h + (n - 3))
                    for k in range(HT):
                        last = pe.matmul(psum[:, n % 4, :], c_t[:, n % 2, k, (n // 2) * P:(n // 2 + 1) * P],
                                         q_t[:, k, NP_:T], start=(k == 0), stop=(k == HT - 1))
                    last.then_inc(g_mm, 1)
                pe.wait_ge(w_ready, h + 1)
                for n in range(HT):
                    for k in range(4):
                        last = pe.matmul(psum[:, 4 + n, :], v_tok[:, k + 1, n * P:(n + 1) * P], se_f[:, k, :], start=(k == 0), stop=(k == 3))
                    pe.wait_ge(g_ev, 8 * h + min(8, 5 + n))
                    last = pe.matmul(psum[:, n, 0:P], v_tok[:, 0, n * P:(n + 1) * P], se_p[:, 0, :], start=True, stop=True)
                    last.then_inc(h_mm, 1)
                pe.wait_ge(h_ready, HT * h + HT)
                for k in range(HT):
                    pe.wait_ge(hsq_ready, HT * h + (k + 1))
                    for b in range(2):
                        last = pe.matmul(psum[:, b, 0:TH], ones[:], half(h_sq[:, k % 2, :], b), start=(k == 0), stop=(k == HT - 1))
                    last.then_inc(hsq_used, 1)
                pe.wait_ge(hroot_ready, h + 1)
                for p in range(2):
                    pe.wait_ge(lo_done, 2 * h + (q0 + p + 1))
                    for m in range(4):
                        n = 4 * p + m
                        if n - 2 in (3, 7):
                            pe.wait_ge(freed, 2 * h + (q0 + (n - 2) // 4 + 1))
                        elif n >= 2:
                            pe.wait_ge(wd_ev, 6 * h + (n - 2 - (n - 2) // 4 + 1))
                        for k in range(HT):
                            if n == 0:
                                pe.wait_ge(y_ready, HT * h + (HT + k + 1))
                            s = slice((m * HT + k) * P, (m * HT + k + 1) * P)
                            for b in range(2):
                                last = mm3(pe, psum[:, 2 * (n % 2) + b, 0:TH], w_hi[:, p, s], w_lo[:, p, s],
                                           half(y_hi[:, k, :], b), half(y_lo[:, k, :], b), k == 0, k == HT - 1)
                        last.then_inc(used if m == 3 else wd_mm, 1)

        def act_up(act, ph):
            q0 = ph["q"]

            def tile(q, par, tt, use, split=True):
                first = isinstance(use, int) and use == 0
                if split:
                    act_hi(act, q + 1, PIECE, 1 - par, ph["off"])
                act.wait_ge(xm_acc, tt + 1)
                if first:
                    act.wait_ge(pad_set, 1)
                else:
                    act.wait_ge(gate_mm, tt - 1)
                    act.wait_ge(xm_out[par], use * 32)
                nc.scalar.activation(xm_pad[:, par, GAP:GAP + NP_], psum[:, 0, 0:NP_], ACT.Copy)
                nc.scalar.activation(xm_pad[:, par, 2 * GAP + NP_:2 * GAP + TH], psum[:, 0, NP_:TH], ACT.Copy)
                nc.scalar.activation(xm_pad[:, par, 2 * GAP + TH:2 * GAP + T], psum[:, 1, 0:TH], ACT.Copy).then_inc(xm_ready, 1)
                act.wait_ge(xm_ready, tt + 1)
                act.dma_start(xm_d[tt, :, 0:NP_], xm_pad[:, par, GAP:GAP + NP_]).then_inc(xm_out[par], 16)
                act.dma_start(xm_d[tt, :, NP_:T], xm_pad[:, par, 2 * GAP + NP_:2 * GAP + T]).then_inc(xm_out[par], 16)
                act.wait_ge(used, q + 1)
                if not first:
                    act.wait_ge(z_out[par], use * 16)
                nc.scalar.activation(two(z_s[:, par, :]), bank2(2), ACT.Silu).then_inc(freed, 1)
                act.wait_ge(freed, q + 1)
                act.dma_start(z_d[tt], z_s[:, par, :]).then_inc(z_out[par], 16)
                act.wait_ge(conv_ready, tt + 1)
                if not first:
                    act.wait_ge(xc_out[par], use * 16)
                for a, b, off in ((0, NP_, 0), (NP_, T, GAP)):
                    last = nc.scalar.activation(xc_s[:, par, a:b], conv[:, par, a + off:b + off], ACT.Silu,
                                                bias=conv_b[:, bass.ds(tt, 1)])
                last.then_inc(xc_ready, 1)
                act.wait_ge(xc_ready, tt + 1)
                act.dma_start(xc_d[tt], xc_s[:, par, :]).then_inc(xc_out[par], 16)

            tile(q0, 0, 0, 0)
            tile(q0 + 1, 1, 1, 0)
            with act.Fori(1, NT // 2 - 1) as i:
                tile(2 * i + q0, 0, 2 * i, i)
                tile(2 * i + (q0 + 1), 1, 2 * i + 1, i)
            tile(q0 + NT - 2, 0, NT - 2, NT // 2 - 1)
            tile(q0 + NT - 1, 1, NT - 1, NT // 2 - 1, split=False)

        def act_gates(act, ph):
            act.wait_ge(g_dve, 2)
            nc.scalar.activation(g_exp[:], g_abs[:], ACT.Exp, scale=-1.0).then_inc(g_act, 1)
            act.wait_ge(g_act, 1)
            nc.scalar.activation(g_ln[:], g_exp[:], ACT.Ln, bias=ones[:, 0:1]).then_inc(g_act, 1)
            act.wait_ge(g_dve, 14)
            nc.scalar.activation(rows[:, 2:4, :], s_row[:], ACT.Exp, scale=-1.0).then_inc(g_act, 1)

        def act_heads(act, ph):
            q0 = ph["q"]
            with act.Fori(0, NH) as h:
                act_hi(act, 2 * h + q0, PIECE, 0, ph["off"])
                act_hi(act, 2 * h + (q0 + 1), PIECE, 1, ph["off"])
                act.wait_ge(in_bc, 16 * h + 16)
                for d in range(2):
                    edge = NP_ - 1 if d == 0 else 0
                    last = nc.scalar.activation(w_tok[:, d:d + 1], a_col[:, 0, d, bass.ds(h, 1)], ACT.Exp,
                                                bias=bc[:, d, edge:edge + 1])
                last.then_inc(wt_ready, 1)
                for n in range(2 * HT):
                    act.wait_ge(qk_mm, 2 * HT * h + (n + 1))
                    dst = q_t if n < HT else k_t
                    nc.scalar.activation(two(dst[:, n % HT, :]), bank2(2 * (n % 2)), ACT.Copy).then_inc(qk_ev, 1)
                for n in range(10):
                    act.wait_ge(cn_mm, 10 * h + (n + 1))
                    if n >= 2:
                        act.wait_ge(cn_out[n % 2], 80 * h + 16 * (n // 2))
                    used_rows = P if n < 8 else 1
                    nc.scalar.activation(c_out[0:used_rows, n % 2, :], psum[0:used_rows, 6 + n % 2, :], ACT.Copy).then_inc(cn_ev, 1)
                    act.wait_ge(cn_ev, 10 * h + (n + 1))
                    if n < 8:
                        dst = t["new_c"][h, n // HT, (n % HT) * P:(n % HT + 1) * P, :]
                    else:
                        dst = t["new_n"][h, n - 8]
                    act.dma_start(dst, c_out[0:used_rows, n % 2, :]).then_inc(cn_out[n % 2], 16)
                act.wait_ge(arg_ready, h + 1)
                for j in range(4):
                    diag = slice(j * P, (j + 1) * P)
                    nc.scalar.activation(se_f[:, j, diag], se_f[:, j, diag], ACT.Exp)
                    nc.scalar.activation(se_b[:, j, diag], se_b[:, j, diag], ACT.Exp)
                    if j < 3:
                        nc.scalar.activation(se_f[:, j, (j + 1) * P:NL], bc[:, 0, NP_ + (j + 1) * P:T], ACT.Exp,
                                             bias=a_col[:, j + 1, 0, bass.ds(h, 1)])
                    if j > 0:
                        nc.scalar.activation(se_b[:, j, 0:j * P], bc[:, 1, NP_:NP_ + j * P], ACT.Exp,
                                             bias=a_col[:, j + 1, 1, bass.ds(h, 1)])
                nc.scalar.activation(se_p[:], se_p[:], ACT.Exp).then_inc(e_ready, 1)
                for d in range(2):
                    last = nc.scalar.activation(alpha[:, d, :], bc[:, d, NP_:T], ACT.Exp, bias=m0[:, bass.ds(h + 4 * d, 1)])
                last.then_inc(dec_ready, 1)
                for k in range(HT):
                    act.wait_ge(h_ready, HT * h + (k + 1))
                    if k == 0:
                        act.wait_ge(g_mm, 8 * h + 8)
                    if k >= 2:
                        act.wait_ge(hsq_used, HT * h + (k - 1))
                    nc.scalar.activation(h_sq[:, k % 2, :], h_t[:, k, :], ACT.Square).then_inc(hsq_ready, 1)
                act.wait_ge(hsq_used, HT * h + HT)
                nc.scalar.activation(two(h_root[:]), bank2(0), ACT.Sqrt, bias=eps_v[:], scale=1.0 / DH).then_inc(hroot_ready, 1)

        def dve_up(dve, ph):
            q0 = ph["q"]
            nc.vector.memset(xm_pad[:], 0.0).then_inc(pad_set, 1)
            dve.wait_ge(in_wgr, 16)
            steps = 0
            for dst in range(2):
                parts = (0, 1) if dst == 0 else (2,)
                for d in range(2):
                    out = gate_w[:, dst, :, 8 * d:8 * d + 8]
                    for n, (s, o) in enumerate((s, o) for s in parts for o in range(4)):
                        a = wgr[:, s, d, :, 8 * o:8 * o + 8]
                        b = wq3[:, s, :, o:o + 1].to_broadcast([P, NT, 8])
                        tmp = gtmp[:, :, 0:8]
                        if n == 0:
                            last = nc.vector.tensor_tensor(out, a, b, ALU.mult).then_inc(gw_tmp, 1)
                        else:
                            nc.vector.tensor_tensor(tmp, a, b, ALU.mult).then_inc(gw_tmp, 1)
                            dve.wait_ge(gw_tmp, steps + 1)
                            last = nc.vector.tensor_tensor(out, out, tmp, ALU.add).then_inc(gw_tmp, 1)
                            steps += 1
                        steps += 1
                        dve.wait_ge(gw_tmp, steps)

            def tile(q, par, tt, split=True):
                if split:
                    dve_lo(dve, q + 1, PIECE, 1 - par, ph["off"])
                dve.wait_ge(xm_ready, tt + 1)
                if not isinstance(tt, int) or tt >= 2:
                    dve.wait_ge(xc_ready, tt - 1)
                for k in range(CONV):
                    src = xm_pad[:, par, k:k + TG]
                    w = conv_w[:, tt, k:k + 1]
                    if k == 0:
                        nc.vector.tensor_scalar(conv[:, par, :], src, w, None, ALU.mult).then_inc(conv_tap, 1)
                    else:
                        last = nc.vector.scalar_tensor_tensor(conv[:, par, :], src, w, conv[:, par, :], ALU.mult, ALU.add)
                        last.then_inc(conv_tap if k < CONV - 1 else conv_ready, 1)
                    if k < CONV - 1:
                        dve.wait_ge(conv_tap, (CONV - 1) * tt + (k + 1))

            tile(q0, 0, 0)
            tile(q0 + 1, 1, 1)
            with dve.Fori(1, NT // 2 - 1) as i:
                tile(2 * i + q0, 0, 2 * i)
                tile(2 * i + (q0 + 1), 1, 2 * i + 1)
            tile(q0 + NT - 2, 0, NT - 2)
            tile(q0 + NT - 1, 1, NT - 1, split=False)

        def dve_gates(dve, ph):
            dve.wait_ge(gate_mm, NT)
            sums = psum[:, 4, 0:80].rearrange("p (j g) -> p j g", j=5)
            nc.vector.tensor_tensor(gt[:].rearrange("p (j d) g -> p j (d g)", d=2), sums,
                                    bgate[:].rearrange("p (a g) -> p a g", a=1).to_broadcast([P, 5, 16]), ALU.add).then_inc(g_dve, 1)
            dve.wait_ge(g_dve, 1)
            f = gt[:, :, 4:8]
            nc.vector.scalar_tensor_tensor(g_abs[:], f, -1.0, f, ALU.mult, ALU.max).then_inc(g_dve, 1)
            dve.wait_ge(g_act, 2)
            nc.vector.scalar_tensor_tensor(logf[:], f, 0.0, g_ln[:], ALU.min, ALU.subtract).then_inc(g_dve, 2)
            dve.wait_ge(g_pe, 1)
            sums = psum[:, 5, 0:40].rearrange("p (j g) -> p j g", g=4)
            nc.vector.tensor_tensor(a_col[:].rearrange("p j d g -> p (j d) g"), gt[:, :, 0:4], sums, ALU.subtract).then_inc(g_dve, 1)
            nc.vector.tensor_copy(b_col[:], sums).then_inc(g_dve, 1)
            dve.wait_ge(g_pe, 2)
            for d in range(2):
                for n, row in enumerate((a_row, b_row)):
                    nc.vector.tensor_copy(row[:, d, NP_:T], psum[0:4, 2 * n + d, :])
                    last = nc.vector.tensor_copy(row[:, d, 0:NP_], psum[0:4, 6, (2 * n + d) * P:(2 * n + d + 1) * P])
            last.then_inc(g_dve, 1)
            dve.wait_ge(g_dve, 7)
            for d in range(2):
                for a, b, start in ((0, NP_, 0.0), (NP_, T, m0row[:, d:d + 1])):
                    v = a_row[:, d, a:b] if d == 0 else a_row[:, d, b - 1:a - 1 if a else None:-1]
                    o = m_row[:, d, a:b] if d == 0 else m_row[:, d, b - 1:a - 1 if a else None:-1]
                    nc.vector.tensor_tensor_scan(o, v, v, start, ALU.max, ALU.max).then_inc(g_dve, 1)
            dve.wait_ge(g_dve, 11)
            nc.vector.tensor_scalar(rows[:, 0:2, :], m_row[:], -1.0, None, ALU.mult).then_inc(g_dve, 1)
            nc.vector.tensor_tensor(s_row[:], m_row[:], b_row[:], ALU.add).then_inc(g_dve, 2)
            dve.wait_ge(g_dve, 14)
            nc.vector.tensor_copy(m_new[:, 0:1], s_row[:, 0, NP_ - 1:NP_])
            nc.vector.tensor_copy(m_new[:, 1:2], s_row[:, 1, 0:1]).then_inc(g_dve, 1)

        def dve_heads(dve, ph):
            q0 = ph["q"]
            dve.wait_ge(rows_out, 16)
            dve.wait_ge(m_out, 16)
            dve.sem_inc(y_ready, HT)
            with dve.Fori(0, NH) as h:
                for s in range(3):
                    a = wq3[:, s, bass.ds(HT * h, HT), :].rearrange("p t (a o) -> p t a o", a=1).to_broadcast([P, HT, 32, 4])
                    b = bdmask.rearrange("p (t n o) -> p t n o", t=1, o=1).to_broadcast([P, HT, 32, 4])
                    nc.vector.tensor_tensor(bd[:, s, :, :].rearrange("p t (n o) -> p t n o", o=4), a, b, ALU.mult)
                nb = n0[:, h, :].rearrange("p (k a) -> p k a", a=1).to_broadcast([P, 8, P])
                nc.vector.tensor_copy(n_bc[:], nb).then_inc(bd_ready, 1)
                dve_lo(dve, 2 * h + q0, PIECE, 0, ph["off"])
                dve_lo(dve, 2 * h + (q0 + 1), PIECE, 1, ph["off"])
                dve.wait_ge(kt_mm, h + 1)
                nc.vector.tensor_copy(k_tok[:], psum[:, 6, :]).then_inc(kt_ev, 1)
                for j in range(5):
                    dve.wait_ge(v_mm, 5 * h + (j + 1))
                    nc.vector.tensor_copy(v_tok[:, j, :], psum[:, 4 + j % 2, :]).then_inc(v_ev, 1)
                    if j == 0:
                        dve.wait_ge(wt_ready, h + 1)
                        dve.wait_ge(v_ev, 5 * h + 1)
                        for d in range(2):
                            last = nc.vector.tensor_scalar(vw[:, d, :], v_tok[:, 0, :], w_tok[:, d:d + 1], None, ALU.mult)
                        last.then_inc(vw_ready, 1)
                dve.wait_ge(in_bc, 16 * h + 16)
                dve.wait_ge(cn_out[0], 80 * h + 80)
                dve.wait_ge(cn_out[1], 80 * h + 80)
                for d, (se, bias) in enumerate(((se_f, bias_f), (se_b, bias_b))):
                    for j in range(4):
                        diag = slice(j * P, (j + 1) * P)
                        nc.vector.scalar_tensor_tensor(se[:, j, diag], bc[:, d, NP_ + j * P:NP_ + (j + 1) * P],
                                                       a_col[:, j + 1, d, bass.ds(h, 1)], bias, ALU.add, ALU.min)
                    last = nc.vector.scalar_tensor_tensor(se_p[:, d, :], bc[:, d, 0:P], a_col[:, 0, d, bass.ds(h, 1)],
                                                          bias, ALU.add, ALU.min)
                last.then_inc(arg_ready, 1)
                dve.wait_ge(s_mm, h + 1)
                dve.wait_ge(e_ready, h + 1)
                for j in range(4):
                    for se, a, b in ((se_f, j * P, NL), (se_b, 0, (j + 1) * P)):
                        nc.vector.scalar_tensor_tensor(se[:, j, a:b], psum[:, j, a:b], S_ML, se[:, j, a:b], ALU.mult, ALU.mult)
                for d in range(2):
                    last = nc.vector.scalar_tensor_tensor(se_p[:, d, :], psum[:, 6, 0:P], S_ML, se_p[:, d, :], ALU.mult, ALU.mult)
                last.then_inc(se_ready, 1)
                dve.wait_ge(nq_mm, h + 1)
                dve.wait_ge(dec_ready, h + 1)
                for d in range(2):
                    last = nc.vector.scalar_tensor_tensor(nq_d[:, d, :], psum[:, 4 + d, :], S_ML, alpha[:, d, :], ALU.mult, ALU.mult)
                last.then_inc(nq_ev, 1)
                dve.wait_ge(den_mm, h + 1)
                dve.wait_ge(nq_ev, h + 1)
                step = 5 * h
                for d in range(2):
                    nc.vector.tensor_tensor(rden[:, d, NP_:T], psum[:, 4 + d, :], nq_d[:, d, :], ALU.add)
                last = nc.vector.tensor_copy(rden[:, :, 0:NP_], psum[:, 6, 0:2 * P].rearrange("p (d n) -> p d n", d=2))
                last.then_inc(den_step, 1)
                dve.wait_ge(den_step, step + 1)
                nc.vector.scalar_tensor_tensor(rden[:], rden[:], -1.0, rden[:], ALU.mult, ALU.max).then_inc(den_step, 1)
                dve.wait_ge(den_step, step + 2)
                nc.vector.tensor_tensor(rden[:], rden[:], bc[:, 2:4, :], ALU.max).then_inc(den_step, 1)
                dve.wait_ge(den_step, step + 3)
                nc.vector.reciprocal(rden[:], rden[:]).then_inc(den_step, 1)
                dve.wait_ge(den_step, step + 4)
                nc.vector.scalar_tensor_tensor(alpha[:], alpha[:], S_ML, rden[:, :, NP_:T], ALU.mult, ALU.mult)
                for j in range(4):
                    nc.vector.tensor_tensor(se_f[:, j, j * P:NL], se_f[:, j, j * P:NL], rden[:, 0, NP_ + j * P:T], ALU.mult)
                    if j:
                        nc.vector.tensor_tensor(se_f[:, j, 0:j * P], se_b[:, j, 0:j * P], rden[:, 1, NP_:NP_ + j * P], ALU.mult)
                    diag = slice(j * P, (j + 1) * P)
                    nc.vector.tensor_tensor(se_b[:, j, diag], se_b[:, j, diag], rden[:, 1, NP_ + j * P:NP_ + (j + 1) * P], ALU.mult)
                nc.vector.tensor_tensor(se_p[:], se_p[:], rden[:, :, 0:NP_], ALU.mult).then_inc(den_step, 1)
                dve.wait_ge(den_step, step + 5)
                for j in range(4):
                    diag = slice(j * P, (j + 1) * P)
                    nc.vector.tensor_tensor(se_f[:, j, diag], se_f[:, j, diag], se_b[:, j, diag], ALU.add)
                nc.vector.tensor_tensor(se_p[:, 0, :], se_p[:, 0, :], se_p[:, 1, :], ALU.add).then_inc(w_ready, 1)
                for n in range(8):
                    v, d = n // 2, n % 2
                    dve.wait_ge(g_mm, 8 * h + (n + 1))
                    if v:
                        dve.wait_ge(h_step, HT * h + v)
                    if d == 0:
                        nc.vector.tensor_tensor(h_t[:, v, NP_:T], psum[:, n % 4, :], alpha[:, 0, :], ALU.mult).then_inc(g_ev, 1)
                    else:
                        nc.vector.tensor_tensor(h_tmp[:], psum[:, n % 4, :], alpha[:, 1, :], ALU.mult).then_inc(g_ev, 1)
                        dve.wait_ge(g_ev, 8 * h + (n + 1))
                        nc.vector.tensor_tensor(h_t[:, v, NP_:T], h_t[:, v, NP_:T], h_tmp[:], ALU.add).then_inc(h_step, 1)
                for v in range(HT):
                    dve.wait_ge(h_mm, HT * h + (v + 1))
                    dve.wait_ge(h_step, HT * h + (v + 1))
                    nc.vector.tensor_copy(h_t[:, v, 0:NP_], psum[:, v, 0:P])
                    nc.vector.tensor_tensor(h_t[:, v, NP_:T], h_t[:, v, NP_:T], psum[:, 4 + v, :], ALU.add).then_inc(h_ready, 1)
                dve.wait_ge(hroot_ready, h + 1)
                nc.vector.reciprocal(h_rstd[:], h_root[:]).then_inc(hrstd_ready, 1)
                dve.wait_ge(hrstd_ready, h + 1)
                dve.wait_ge(in_z, 16 * h + 16)
                dve.wait_ge(in_xc, 16 * h + 16)
                for k in range(HT):
                    nc.vector.scalar_tensor_tensor(h_t[:, k, :], h_t[:, k, :], head_g[:, bass.ds(HT * h + k, 1)], h_rstd[:],
                                                   ALU.mult, ALU.mult).then_inc(y_step, 1)
                for k in range(HT):
                    dve.wait_ge(y_step, 4 * HT * h + (k + 1))
                    nc.vector.scalar_tensor_tensor(h_t[:, k, :], xc_h[:, k, :], skip[:, bass.ds(HT * h + k, 1)], h_t[:, k, :],
                                                   ALU.mult, ALU.add).then_inc(y_step, 1)
                for k in range(HT):
                    dve.wait_ge(y_step, 4 * HT * h + (HT + k + 1))
                    nc.vector.tensor_tensor(h_t[:, k, :], h_t[:, k, :], zs_h[:, k, :], ALU.mult).then_inc(y_step, 1)
                for k in range(HT):
                    dve.wait_ge(y_step, 4 * HT * h + (2 * HT + k + 1))
                    nc.vector.tensor_copy(y_hi[:, k, :], h_t[:, k, :]).then_inc(y_step, 1)
                for k in range(HT):
                    dve.wait_ge(y_step, 4 * HT * h + (3 * HT + k + 1))
                    nc.vector.tensor_tensor(y_lo[:, k, :], h_t[:, k, :], y_hi[:, k, :].bitcast(F32), ALU.subtract).then_inc(y_ready, 1)
                for n in range(8):
                    if n % 4 == 3:
                        dve.wait_ge(used, 2 * h + (q0 + n // 4 + 1))
                    else:
                        dve.wait_ge(wd_mm, 6 * h + (n - n // 4 + 1))
                    add_gated(dve, n, 2 * (n % 2)).then_inc(freed if n % 4 == 3 else wd_ev, 1)

        def pool_up(pool, ph):
            q0 = ph["q"]
            pool.wait_ge(freed, q0)
            pool.dma_start(wgr[:].rearrange("p a b c d -> p (a b c d)"), t["wgr"].rearrange("p a b c d -> p (a b c d)")).then_inc(in_wgr, 16)

        def pool_gates(pool, ph):
            pool.wait_ge(g_act, 3)
            pool.wait_ge(g_dve, 15)
            pool.dma_start(rows_d, rows[:]).then_inc(rows_out, 16)
            pool.dma_start(t["new_m"], m_new[:]).then_inc(m_out, 16)
            pool.wait_ge(rows_out, 16)
            pool.wait_ge(m_out, 16)

        def sp_heads(sp, ph, chunk_in_row):
            heads = lambda d: d.rearrange("(h k) p n -> h p k n", h=NH)
            sp.wait_ge(rows_out, 16)
            sp.wait_ge(g_pe, 2)
            for par in range(2):
                sp.wait_ge(xm_out[par], 16 * NT)
                sp.wait_ge(z_out[par], 8 * NT)
                sp.wait_ge(xc_out[par], 8 * NT)
            with sp.Fori(0, NH) as h:
                chunk_in_row(h + ph["q"] // 2, h + (ph["q"] // 2 + ph["off"]), t["w_heads"][h], PIECE)
                sp.wait_ge(y_ready, HT * h + HT)
                sp.dma_start(bc[:], rows_d[h].rearrange("(a k) n -> a k n", a=1).to_broadcast([P, 4, T])).then_inc(in_bc, 16)
                sp.dma_start(xc_h[:], heads(xc_d)[h]).then_inc(in_xc, 16)
                sp.dma_start(xm_h[:], heads(xm_d)[h]).then_inc(in_xm, 16)
                sp.dma_start(c_t[:], t["c0"][h]).then_inc(in_ct, 16)
                sp.wait_ge(w_ready, h + 1)
                sp.dma_start(zs_h[:], heads(z_d)[h]).then_inc(in_z, 16)
            for par in range(2):
                sp.wait_ge(cn_out[par], 80 * NH)

        pe_mixers = {"up": pe_up, "gates": pe_gates, "heads": pe_heads}
        act_mixers = {"up": act_up, "gates": act_gates, "heads": act_heads}
        dve_mixers = {"up": dve_up, "gates": dve_gates, "heads": dve_heads}
        pool_phases = {"up": pool_up, "gates": pool_gates}

        def pool_mixers(pool):
            for ph in seq:
                if ph["kind"] in pool_phases:
                    pool_phases[ph["kind"]](pool, ph)

        (cq_copied, cache_in, in_ropes, kv_out, in_step_a, in_step_p, in_step_d, q_mm, q_ev, kn_mm, kn_ev) = (
            sem(n) for n in ("cq_copied", "cache_in", "in_ropes", "kv_out", "in_step_a", "in_step_p", "in_step_d",
                             "q_mm", "q_ev", "kn_mm", "kn_ev"))
        (qsq, qss, qroot, rq_ready, ksq, kss, kvar, kroot, rk_ready, scaled, rot_mm, rope_step, roped) = (
            sem("a_" + n) for n in ("qsq", "qss", "qroot", "rq_ready", "ksq", "kss", "kvar", "kroot", "rk_ready",
                                    "scaled", "rot_mm", "rope_step", "roped"))
        (vh_mm, vh_ev, sc_mm, mx_ready, nb_ready, ex_ready, rs_ready, pn_ready, tr_mm, tr_ev, pv_mm, of_ready, oh_ready,
         o_ready) = (
            sem("a_" + n) for n in ("vh_mm", "vh_ev", "sc_mm", "mx_ready", "nb_ready", "ex_ready", "rs_ready", "pn_ready",
                                    "tr_mm", "tr_ev", "pv_mm", "of_ready", "oh_ready", "o_ready"))
        KH = TK // 2
        S_AT = float(QK) ** -0.5
        mx, nb, sums, rsum = (soft[:, i:i + 2] for i in range(0, 8, 2))

        def wide(b):
            return psum[:, b:b + 2, 0:KH]

        def pe_attn_in(pe, ph):
            q = ph["q"]
            pe_in_piece(pe, q, 0, 4, 2 * ph["mod"], ph["mod"])
            pe_in_piece(pe, q + 1, 1, 4, 2 * ph["mod"], ph["mod"])
            for k in range(3):
                pe.wait_ge(in_step_a, 1 + k if k < 2 else 4)
                if k == 0:
                    pe.wait_ge(freed, q + 2)
                for b in range(2):
                    last = pe.matmul(psum[:, 2 * (k // 2) + b, 0:TH], ones[:], half(c_sq[:, k % 2, :], b),
                                     start=(k != 1), stop=(k != 0))
                last.then_inc(in_step_p, 1)

        Q_Q = next(ph["q"] for ph in plan() if ph["kind"] == "attn_q")

        def q_count(each, piece, n):
            return (each, n // 6 * 5 + n % 6 + 1) if n % 6 < 5 else (piece, Q_Q + n // 6 + 1)

        def pe_attn_q(pe, ph):
            pe.wait_ge(in_step_d, 7)
            for n in range(12):
                q, par, tile = ph["q"] + n // 6, n // 6, n % 6
                pe.wait_ge(lo_done, q + 1)
                if n >= 4:
                    pe.wait_ge(*q_count(q_ev, freed, n - 4))
                for k in range(2):
                    s = slice((tile * 2 + k) * P, (tile * 2 + k + 1) * P)
                    for b in range(2):
                        last = mm3(pe, psum[:, 2 * (n % 4) + b, 0:TH], w_hi[:, par, s], w_lo[:, par, s],
                                   half(cq_hi[:, k, :], b), half(cq_lo[:, k, :], b), k == 0, k == 1)
                last.then_inc(q_mm if tile < 5 else used, 1)

        def pe_attn_kv(pe, ph):
            q = ph["q"]
            pe.wait_ge(freed, q)
            for n in range(AH):
                pe.wait_ge(lo_done, q + 1)
                if n >= 4:
                    pe.wait_ge(kn_ev, n - 3)
                s = slice(n * P, (n + 1) * P)
                for b in range(2):
                    e = slice(b * KH, (b + 1) * KH)
                    last = mm3(pe, psum[:, 2 * (n % 4) + b, 0:KH], w_hi[:, 0, s], w_lo[:, 0, s], ent_hi[:, e], ent_lo[:, e],
                               True, True)
                last.then_inc(kn_mm if n < AH - 1 else used, 1)

        def pe_attn(pe, ph):
            q = ph["q"]
            pe.wait_ge(in_step_a, 6)
            pe.wait_ge(freed, q - 1)
            for b in range(2):
                pe.matmul(psum[:, b, 0:KH], sel_a, a_sq[:, b * KH:(b + 1) * KH], start=True, stop=True)
            pe.wait_ge(in_step_d, 8)
            pe.matmul(psum[:, 2, :], rot, k_rot[:, NP_:T], start=True, stop=True).then_inc(in_step_p, 1)
            pe.wait_ge(lo_done, q)
            with pe.Fori(0, AH // 2) as hp:
                for s in range(2):
                    h = 2 * hp + s
                    r = slice(64 * s, 64 * s + 64)
                    pe.wait_ge(qsq, h + 1)
                    pe.wait_ge(o_ready, h + 1)
                    for b in range(2):
                        pe.matmul(psum[:, b, 0:TH], ones[:], half(a_sq[:, 0:T], b), start=True, stop=False)
                        last = pe.matmul(psum[:, b, 0:TH], sel_b if s else sel_a, half(a_root[:, 0:T], b), start=False, stop=True)
                    last.then_inc(qss, 1)
                    for j in range(6):
                        e = slice(j * P, (j + 1) * P)
                        out = psum[:, 5 + j // 4, (j % 4) * P:(j % 4 + 1) * P]
                        col = bass.ds(h * P, P)
                        pe.matmul(out, ent_hi[:, e], w_hi[:, 1, col], start=True, stop=False)
                        pe.matmul(out, ent_lo[:, e], w_hi[:, 1, col], start=False, stop=False)
                        last = pe.matmul(out, ent_hi[:, e], w_lo[:, 1, col], start=False, stop=True)
                    last.then_inc(vh_mm, 1)
                    pe.wait_ge(ksq, h + 1)
                    for b in range(2):
                        last = pe.matmul(psum[:, 2 + b, 0:KH], ones[:], a_sq[:, b * KH:(b + 1) * KH], start=True, stop=True)
                    last.then_inc(kss, 1)
                    pe.wait_ge(scaled, h + 1)
                    pe.matmul(psum[:, 4, :], rot[r, :], qrs[r, NP_:T], start=True, stop=True).then_inc(rot_mm, 1)
                    pe.wait_ge(roped, h + 1)
                    pe.wait_ge(vh_ev, h + 1)

                    def scores(j):
                        if j == 0:
                            outs = [(psum[:, 7, 0:P], slice(0, P))]
                        else:
                            outs = [(psum[:, 2 * ((j - 1) % 2) + b, 0:TH], slice(P + b * TH, P + (b + 1) * TH)) for b in range(2)]
                            if j >= 3:
                                pe.wait_ge(ex_ready, 5 * h + j - 1)
                        for out, e in outs:
                            pe.matmul(out, qs[:, j * P:(j + 1) * P], ks[:, e], start=True, stop=False)
                            last = pe.matmul(out, qrs[r, j * P:(j + 1) * P], krs[r, e], start=False, stop=True)
                        last.then_inc(sc_mm, 1)

                    def turns(j):
                        pe.wait_ge(pn_ready, 5 * h + j + 1)
                        if j:
                            pe.wait_ge(tr_ev, 5 * h + j)
                        for b in range(1 if j == 0 else 5):
                            last = pe.transpose(psum[:, 4 + b // 4, (b % 4) * P:(b % 4 + 1) * P],
                                                prob[:, j % 2, b * P:(b + 1) * P], ident)
                        last.then_inc(tr_mm, 1)

                    scores(0)
                    scores(1)
                    scores(2)
                    turns(0)
                    turns(1)
                    scores(3)
                    turns(2)
                    scores(4)
                    turns(3)
                    turns(4)
                    pe.wait_ge(tr_ev, 5 * h + 5)
                    pe.matmul(psum[:, 1, 0:P], v_h[:, 0, :], a_sq[:, 0:P], start=True, stop=True)
                    for b in range(5):
                        last = pe.matmul(psum[:, 0, :], v_h[:, b + 1, :], pt[:, b, :], start=(b == 0), stop=(b == 4))
                    last.then_inc(pv_mm, 1)
            pe.wait_ge(o_ready, AH + 1)
            pe.sem_inc(used, 1)

        def act_attn_in(act, ph):
            q = ph["q"]
            act_hi(act, q + 1, PIECE, 1, ph["off"])
            act.wait_ge(used, q + 1)
            nc.scalar.activation(two(cq[:, 0, :]), bank2(0), ACT.Copy)
            nc.scalar.activation(two(cq[:, 1, :]), bank2(2), ACT.Copy).then_inc(freed, 1)
            act_hi(act, q + 2, ph["next"], 0, ph["off"])
            act.wait_ge(freed, q + 1)
            nc.scalar.activation(c_sq[:, 0, :], cq[:, 0, :], ACT.Square).then_inc(in_step_a, 1)
            nc.scalar.activation(c_sq[:, 1, :], cq[:, 1, :], ACT.Square).then_inc(in_step_a, 1)
            act.wait_ge(used, q + 2)
            nc.scalar.activation(two(ent[:, 0:T]), bank2(4), ACT.Copy)
            nc.scalar.activation(two(kr[:, 0:T]), bank2(6), ACT.Copy).then_inc(freed, 1)
            act.wait_ge(in_step_p, 2)
            nc.scalar.activation(two(root[:]), bank2(0), ACT.Sqrt, bias=eps_v[:], scale=1.0 / QL).then_inc(in_step_a, 1)
            act.wait_ge(freed, q + 2)
            nc.scalar.activation(c_sq[:, 0, :], ent[:, 0:T], ACT.Square).then_inc(in_step_a, 1)
            act.wait_ge(in_step_p, 3)
            act.wait_ge(in_step_d, 1)
            nc.scalar.activation(two(root[:]), bank2(2), ACT.Sqrt, bias=eps_v[:], scale=1.0 / KV).then_inc(in_step_a, 1)

        def act_attn_q(act, ph):
            q = ph["q"]
            act_hi(act, q + 1, 12 * P, 1, ph["off"])
            for n in range(12):
                act.wait_ge(*q_count(q_mm, used, n))
                p, tile = n // 6, n % 6
                dst = qn_raw[:, 4 * p + tile, :] if tile < 4 else qr_raw[:, 2 * p + tile - 4, :]
                if n == 0:
                    act.wait_ge(in_step_d, 7)
                nc.scalar.activation(two(dst), bank2(2 * (n % 4)), ACT.Copy).then_inc(q_ev if tile < 5 else freed, 1)
                if n == 5:
                    act_hi(act, q + 2, 8 * P, 0, ph["off"])

        def act_attn_kv(act, ph):
            q = ph["q"]
            act_hi(act, q + 1, 8 * P, 1, ph["off"])
            act_hi(act, q + 2, PIECE, 0, ph["off"])

        def act_attn(act, ph):
            act.wait_ge(in_step_d, 7)
            act.wait_ge(cache_in, 32)
            nc.scalar.activation(a_sq[:], kr[:], ACT.Square).then_inc(in_step_a, 1)
            with act.Fori(0, AH // 2) as hp:
                for s in range(2):
                    h = 2 * hp + s
                    act.wait_ge(o_ready, h + 1)
                    nc.scalar.activation(a_sq[:, 0:T], qn_raw[:, h, :], ACT.Square)
                    nc.scalar.activation(a_root[:, 0:T], qr_raw[:, hp, :], ACT.Square).then_inc(qsq, 1)
                    act.wait_ge(qss, h + 1)
                    nc.scalar.activation(two(a_root[:, 0:T]), bank2(0), ACT.Sqrt, bias=eps_v[:], scale=1.0 / QK).then_inc(qroot, 1)
                    nc.scalar.activation(a_sq[:], kn_raw[:, h, :], ACT.Square).then_inc(ksq, 1)
                    act.wait_ge(rq_ready, h + 1)
                    act.wait_ge(kvar, h + 1)
                    nc.scalar.activation(a_root[:], r_k[:], ACT.Sqrt).then_inc(kroot, 1)
                    act.wait_ge(vh_mm, h + 1)
                    nc.scalar.activation(v_h[:, 0:4, :], psum[:, 5, :].rearrange("p (j n) -> p j n", j=4), ACT.Copy)
                    nc.scalar.activation(v_h[:, 4:6, :], psum[:, 6, 0:2 * P].rearrange("p (j n) -> p j n", j=2), ACT.Copy).then_inc(vh_ev, 1)
                    for j in range(5):
                        act.wait_ge(nb_ready, 5 * h + j + 1)
                        if j >= 2:
                            act.wait_ge(tr_mm, 5 * h + j - 1)
                        if j == 0:
                            nc.scalar.activation(prob[:, 0, 0:P], psum[:, 7, 0:P], ACT.Exp, bias=nb[:, 0:1], scale=S_AT,
                                                 accum_out=sums[:, 0:1]).then_inc(ex_ready, 1)
                        else:
                            nc.scalar.activation(two(prob[:, j % 2, :]), bank2(2 * ((j - 1) % 2)), ACT.Exp,
                                                 bias=nb[:, j % 2:j % 2 + 1], scale=S_AT,
                                                 accum_out=sums[:, j % 2:j % 2 + 1]).then_inc(ex_ready, 1)

        def dve_attn_in(dve, ph):
            q = ph["q"]
            dve_lo(dve, q + 1, PIECE, 1, ph["off"])
            dve_lo(dve, q + 2, ph["next"], 0, ph["off"])
            dve.wait_ge(in_step_a, 3)
            nc.vector.reciprocal(rstd[:], root[:]).then_inc(in_step_d, 1)
            dve.wait_ge(in_step_d, 1)
            for k in range(2):
                last = nc.vector.scalar_tensor_tensor(cq[:, k, :], cq[:, k, :], attn_g[:, 4 + k:5 + k], rstd[:], ALU.mult, ALU.mult)
            last.then_inc(in_step_d, 1)
            dve.wait_ge(in_step_d, 2)
            nc.vector.tensor_copy(cq_hi[:], cq[:]).then_inc(in_step_d, 1)
            dve.wait_ge(in_step_d, 3)
            nc.vector.tensor_tensor(cq_lo[:], cq[:], cq_hi[:].bitcast(F32), ALU.subtract)
            dve.wait_ge(in_step_a, 5)
            nc.vector.reciprocal(rstd[:], root[:]).then_inc(in_step_d, 1)
            dve.wait_ge(in_step_d, 4)
            dve.wait_ge(cache_in, 32)
            nc.vector.scalar_tensor_tensor(ent[:, 0:T], ent[:, 0:T], attn_g[:, 6:7], rstd[:], ALU.mult, ALU.mult).then_inc(in_step_d, 1)
            dve.wait_ge(in_step_d, 5)
            nc.vector.tensor_copy(ent_hi[:], ent[:]).then_inc(in_step_d, 1)
            dve.wait_ge(in_step_d, 6)
            nc.vector.tensor_tensor(ent_lo[:], ent[:], ent_hi[:].bitcast(F32), ALU.subtract).then_inc(in_step_d, 1)

        def dve_attn_q(dve, ph):
            q = ph["q"]
            dve_lo(dve, q + 1, 12 * P, 1, ph["off"])
            dve_lo(dve, q + 2, 8 * P, 0, ph["off"])

        def dve_attn_kv(dve, ph):
            q = ph["q"]
            dve_lo(dve, q + 1, 8 * P, 1, ph["off"])
            for n in range(AH):
                dve.wait_ge(kn_mm if n < AH - 1 else used, n + 1 if n < AH - 1 else q + 1)
                nc.vector.tensor_copy(kn_raw[:, n, :].rearrange("p (b n) -> p b n", b=2), wide(2 * (n % 4))).then_inc(
                    kn_ev if n < AH - 1 else freed, 1)
            dve_lo(dve, q + 2, PIECE, 0, ph["off"])

        def dve_attn(dve, ph):
            dve.wait_ge(cache_in, 32)
            nc.vector.tensor_scalar(k_rot[:], kr[:], attn_g[:, 3:4], None, ALU.mult).then_inc(in_step_d, 1)
            dve.wait_ge(in_step_p, 4)
            dve.wait_ge(in_ropes, 16)
            nc.vector.tensor_scalar(kr_ss[:].rearrange("p (b n) -> p b n", b=2), wide(0), 1.0 / QK, EPS, ALU.mult,
                                    ALU.add).then_inc(in_step_d, 1)
            nc.vector.tensor_tensor(a_root[:, 0:NL], psum[:, 2, :], ropes[:, 1, :], ALU.mult).then_inc(in_step_d, 1)
            nc.vector.tensor_tensor(k_rot[:, NP_:T], k_rot[:, NP_:T], ropes[:, 0, :], ALU.mult).then_inc(in_step_d, 1)
            dve.wait_ge(in_step_d, 11)
            nc.vector.tensor_tensor(k_rot[:, NP_:T], k_rot[:, NP_:T], a_root[:, 0:NL], ALU.add).then_inc(o_ready, 1)
            dve.wait_ge(o_ready, 1)
            with dve.Fori(0, AH // 2) as hp:
                for s in range(2):
                    h = 2 * hp + s
                    r = slice(64 * s, 64 * s + 64)
                    dve.wait_ge(qroot, h + 1)
                    nc.vector.reciprocal(r_q[:], a_root[:, 0:T]).then_inc(rq_ready, 1)
                    dve.wait_ge(kss, h + 1)
                    nc.vector.scalar_tensor_tensor(r_k[:].rearrange("p (b n) -> p b n", b=2), wide(2), 1.0 / QK,
                                                   kr_ss[:].rearrange("p (b n) -> p b n", b=2), ALU.mult, ALU.add).then_inc(kvar, 1)
                    dve.wait_ge(rq_ready, h + 1)
                    nc.vector.scalar_tensor_tensor(qs[:], qn_raw[:, h, :], attn_g[:, 0:1], r_q[:], ALU.mult, ALU.mult)
                    nc.vector.scalar_tensor_tensor(qrs[r, :], qr_raw[r, hp, :], attn_g[r, 1:2], r_q[r, :], ALU.mult,
                                                   ALU.mult).then_inc(scaled, 1)
                    dve.wait_ge(kroot, h + 1)
                    nc.vector.reciprocal(r_k[:], a_root[:]).then_inc(rk_ready, 1)
                    dve.wait_ge(rk_ready, h + 1)
                    nc.vector.scalar_tensor_tensor(ks[:], kn_raw[:, h, :], attn_g[:, 2:3], r_k[:], ALU.mult, ALU.mult)
                    nc.vector.tensor_tensor(krs[r, :], k_rot[r, :], r_k[r, :], ALU.mult)
                    dve.wait_ge(rot_mm, h + 1)
                    nc.vector.tensor_tensor(a_root[r, 0:NL], psum[r, 4, :], ropes[r, 1, :], ALU.mult)
                    nc.vector.tensor_tensor(qrs[r, NP_:T], qrs[r, NP_:T], ropes[r, 0, :], ALU.mult).then_inc(rope_step, 1)
                    dve.wait_ge(rope_step, h + 1)
                    nc.vector.tensor_tensor(qrs[r, NP_:T], qrs[r, NP_:T], a_root[r, 0:NL], ALU.add).then_inc(roped, 1)

                    def top(j):
                        k = 5 * h + j + 1
                        dve.wait_ge(sc_mm, k)
                        if j >= 2:
                            dve.wait_ge(ex_ready, k - 2)
                        src = psum[:, 7, 0:P] if j == 0 else bank2(2 * ((j - 1) % 2))
                        m = mx[:, j % 2:j % 2 + 1]
                        nc.vector.tensor_reduce(m, src, AX_X if j == 0 else mybir.AxisListType.XY, ALU.max).then_inc(mx_ready, 1)
                        dve.wait_ge(mx_ready, k)
                        nc.vector.tensor_scalar(nb[:, j % 2:j % 2 + 1], m, -S_AT, None, ALU.mult).then_inc(nb_ready, 1)

                    def normal(j):
                        k = 5 * h + j + 1
                        dve.wait_ge(ex_ready, k)
                        nc.vector.reciprocal(rsum[:, j % 2:j % 2 + 1], sums[:, j % 2:j % 2 + 1]).then_inc(rs_ready, 1)
                        dve.wait_ge(rs_ready, k)
                        p = prob[:, j % 2, 0:P if j == 0 else T]
                        nc.vector.tensor_scalar(p, p, rsum[:, j % 2:j % 2 + 1], None, ALU.mult).then_inc(pn_ready, 1)

                    def turned(j):
                        k = 5 * h + j + 1
                        dve.wait_ge(tr_mm, k)
                        if j == 0:
                            nc.vector.tensor_copy(a_sq[:, 0:P], psum[:, 4, 0:P]).then_inc(tr_ev, 1)
                        else:
                            c = slice((j - 1) * P, j * P)
                            nc.vector.tensor_copy(pt[:, 0:4, c], psum[:, 4, :].rearrange("p (b n) -> p b n", b=4))
                            nc.vector.tensor_copy(pt[:, 4, c], psum[:, 5, 0:P]).then_inc(tr_ev, 1)

                    top(0)
                    top(1)
                    normal(0)
                    top(2)
                    normal(1)
                    turned(0)
                    turned(1)
                    top(3)
                    normal(2)
                    turned(2)
                    top(4)
                    normal(3)
                    turned(3)
                    normal(4)
                    turned(4)
                    dve.wait_ge(pv_mm, h + 1)
                    nc.vector.tensor_copy(qs[:, 0:NP_], psum[:, 1, 0:P])
                    nc.vector.tensor_copy(qs[:, NP_:T], psum[:, 0, :]).then_inc(of_ready, 1)
                    dve.wait_ge(of_ready, h + 1)
                    nc.vector.tensor_scalar(o_hi[:, h, :], qs[:], 1.0, None, ALU.mult).then_inc(oh_ready, 1)
                    dve.wait_ge(oh_ready, h + 1)
                    nc.vector.tensor_tensor(o_lo[:, h, :], qs[:], o_hi[:, h, :].bitcast(F32), ALU.subtract).then_inc(o_ready, 1)
            dve.wait_ge(o_ready, AH + 1)
            dve.sem_inc(freed, 1)

        def pe_attn_out(pe, ph):
            for p in range(4):
                pe_out_piece(pe, ph["q"] + p, p % 2, AH, 2, o_hi, o_lo, (o_ready, 1))

        def act_attn_out(act, ph):
            for p in range(4):
                if p < 3:
                    act_hi(act, ph["q"] + p + 1, PIECE, (p + 1) % 2, ph["off"])
                act.wait_ge(freed, ph["q"] + p + 1)
                act_square(act, ph["stats"], 2 * p)
                act_square(act, ph["stats"], 2 * p + 1)

        def dve_attn_out(dve, ph):
            clear_acc(dve, ph["stats"])
            for p in range(4):
                if p < 3:
                    dve_lo(dve, ph["q"] + p + 1, PIECE, (p + 1) % 2, ph["off"])
                dve.wait_ge(used, ph["q"] + p + 1)
                add_gated(dve, 2 * p, 4 * (p % 2))
                add_gated(dve, 2 * p + 1, 4 * (p % 2) + 2).then_inc(freed, 1)
                add_square(dve, ph["stats"], 2 * p)
                add_square(dve, ph["stats"], 2 * p + 1)

        def pool_attn_in(pool, ph):
            pool.wait_ge(freed, ph["q"])
            pool.dma_start(ent[:, T:TK], t["cache_c"]).then_inc(cache_in, 16)
            pool.dma_start(kr[:, T:TK], t["cache_r"]).then_inc(cache_in, 16)
            pool.wait_ge(in_step_d, 5)
            pool.dma_start(t["new_kv"][0:KV], ent[:, 0:NP_]).then_inc(kv_out, 16)
            pool.dma_start(t["new_kv"][KV:KV + 64], kr[0:64, 0:NP_]).then_inc(kv_out, 16)
            pool.wait_ge(kv_out, 32)
            pool.wait_ge(freed, ph['q'] + 4)
            pool.dma_start(ropes[:], t["ropes"]).then_inc(in_ropes, 16)

        for name, pe_f, act_f, dve_f in (
                ("attn_in", pe_attn_in, act_attn_in, dve_attn_in), ("attn_q", pe_attn_q, act_attn_q, dve_attn_q),
                ("attn_kv", pe_attn_kv, act_attn_kv, dve_attn_kv), ("attn", pe_attn, act_attn, dve_attn),
                ("attn_out", pe_attn_out, act_attn_out, dve_attn_out)):
            pe_mixers[name], act_mixers[name], dve_mixers[name] = pe_f, act_f, dve_f
        pool_phases["attn_in"] = pool_attn_in

        block = ctx.enter_context(nc.Block())

        @block.sync
        def _(sp):
            def slot_free(c):
                if c >= 2:
                    kind, value = leaves[c - 2]
                    sp.wait_ge(lo_done if kind == "w" else mod_used, value)

            def chunk_at(q, c, src, columns):
                slot_free(c)
                if q:
                    sp.wait_ge(raw_in, 8 * q)
                sp.dma_start(raw[:, c % 2, :, 0:columns], src).then_inc(raw_in, 16)

            def chunk_in_row(n, c, src, columns):
                sp.wait_ge(raw_in, 16 * n)
                sp.wait_ge(lo_done, 2 * n - 2)
                sp.dma_start(raw[:, c % 2, :, 0:columns], src).then_inc(raw_in, 16)

            def mod_chunk_at(m, c):
                slot_free(c)
                if m:
                    sp.wait_ge(mod_in, 16 * m)
                sp.dma_start(raw[:, c % 2], t["w_mod"][m]).then_inc(mod_in, 16)

            for ph in seq:
                kind, q, c, n = ph["kind"], ph["q"], ph["c"], ph["n"] // 2
                if kind == "heads":
                    sp_heads(sp, ph, chunk_in_row)
                elif ph["mods"] and n:
                    w, m = t["w_in"][ph["f"]], ph["mod"]
                    chunk_at(q, c, w[ph["pair"]], PIECE)
                    mod_chunk_at(m, c + 1)
                    with sp.Fori(1, n) as i:
                        sp.wait_ge(lo_done, 2 * i + q)
                        sp.dma_start(raw[:, c % 2], w[i + ph["pair"]]).then_inc(raw_in, 16)
                        sp.wait_ge(mod_used, 2 * i + 2 * m)
                        sp.dma_start(raw[:, (c + 1) % 2], t["w_mod"][i + m]).then_inc(mod_in, 16)
                elif ph["mods"]:
                    for i in range(ph["mods"]):
                        mod_chunk_at(i, i)
                elif n:
                    if kind == "in":
                        w, first, columns = t["w_in"][ph["f"]], ph["pair"], PIECE
                    elif kind == "out":
                        w, first, columns = t[f"w_out{ph['half']}"][ph["f"]], 0, ph["tiles"] * P
                    else:
                        w, first, columns = t["w_" + kind], 0, size_of(ph)
                    for i in range(min(n, 2)):
                        chunk_at(q + 2 * i, c + i, w[first + i], columns)
                    if n > 2:
                        with sp.Fori(2, n) as i:
                            chunk_in_row(i + q // 2, i + c, w[i + first], columns)

        @block.gpsimd
        def _(pool):
            for dst, src in ((cst, "cst"), (bmod, "bmod"), (norm_g, "norm_g")):
                pool.dma_start(dst[:], t[src]).then_inc(in_bmod, 16)
            for k in range(KD):
                pool.dma_start(x[:, k, :], t["x"][k]).then_inc(in_x, 16)
            for dst, src in ((mlp, "mlp"), (wq3, "wq3"), (bgate, "bgate"), (m0, "m0"),
                             (n0, "n0"), (m0row, "m0row"), (attn_g, "attn_g")):
                pool.dma_start(dst[:], t[src]).then_inc(in_cst, 16)
            pool_mixers(pool)
            for k in range(KD):
                pool.wait_ge(freed, seq[-1]["q"] + seq[-1]["n"] - KD + k + 1)
                pool.dma_start(t["y"][k], x[:, k, :]).then_inc(y_out, 16)
            pool.wait_ge(y_out, 16 * KD)

        def piece_ready(pe, q):
            pe.wait_ge(lo_done, q + 1)
            if not isinstance(q, int) or q >= 2:
                pe.wait_ge(freed, q - 1)

        def pe_mod(pe, m, slot, hi, bank):
            pe.wait_ge(mod_lo_done, m + 1)
            low = raw_lo[:, slot[0], slot[1], :]
            for k in range(KD):
                s = slice(k * 2 * P, (k + 1) * 2 * P)
                pe.matmul(psum[0:4, bank, 0:2 * P], c4[:, k, :], hi[:, s], start=(k == 0), stop=False)
                last = pe.matmul(psum[0:4, bank, 0:2 * P], c4[:, k, :], low[:, s], start=False, stop=(k == KD - 1))
            last.then_inc(mod_used, 1)

        def pe_mod_turn(pe, c):
            pe.wait_ge(mod_copied, 2 * c + 2)
            for n in range(2):
                last = pe.matmul(psum[:, 2, 4 * n:4 * n + 4], mod_rows[:, n * P:(n + 1) * P], sum_parts,
                                 start=True, stop=True)
            last.then_inc(mod_turned, 1)

        def pe_in_piece(pe, q, par, norm_at, copied, turned):
            piece_ready(pe, q)
            for step in range(KD + 4):
                for ab, k in ((0, step), (1, step - 4)):
                    if not 0 <= k < KD:
                        continue
                    if ab == 0:
                        pe.wait_ge(xn_ready, KD * norm_at + k + 1)
                    elif k == 0:
                        pe.wait_ge(mod_copied, copied)
                        if par == 0:
                            pe.wait_ge(mod_freed, turned)
                    s = slice((k * 2 + ab) * P, (k * 2 + ab + 1) * P)
                    for n in range(2):
                        last = mm3(pe, psum[:, 4 * par + 2 * ab + n, 0:TH], w_hi[:, par, s], w_lo[:, par, s],
                                   half(xn_hi[:, k, :], n), half(xn_lo[:, k, :], n), k == 0, k == KD - 1)
            last.then_inc(used, 1)

        def pe_out_piece(pe, q, par, kt, outs, r_hi, r_lo, ready=None):
            piece_ready(pe, q)
            for m in range(outs):
                for k in range(kt):
                    if ready is not None and m == 0:
                        pe.wait_ge(ready[0], ready[1] + k + 1)
                    s = slice((m * kt + k) * P, (m * kt + k + 1) * P)
                    for n in range(2):
                        last = mm3(pe, psum[:, 4 * par + 2 * m + n, 0:TH], w_hi[:, par, s], w_lo[:, par, s],
                                   half(r_hi[:, k, :], n), half(r_lo[:, k, :], n), k == 0, k == kt - 1)
            last.then_inc(used, 1)

        @block.tensor
        def _(pe):
            for ph in seq:
                kind, q, c = ph["kind"], ph["q"], ph["c"]
                if kind == "mod":
                    pe.wait_ge(c_ready, 1)
                    pe.wait_ge(in_bmod, 48)
                    pe.wait_ge(rows_set, 1)
                    for m in range(2 * ph["mods"]):
                        if m >= 2:
                            pe.wait_ge(mod_copied, m - 1)
                        pe_mod(pe, m, (m // 2 % 2, m % 2), w_hi[:, m % 2, :], 3 + 4 * (m % 2))
                        if m % 2:
                            if m >= 2:
                                pe.wait_ge(mod_freed, m // 2)
                            pe_mod_turn(pe, m // 2)
                elif kind == "norm":
                    pe.wait_ge(ones_set, 1)
                    pe.wait_ge(freed, q) if q else None
                    pe.wait_ge(acc_ready, KD * ph["at"] + KD)
                    for n in range(2):
                        last = pe.matmul(psum[:, n, 0:TH], ones[:], half(acc, n), start=True, stop=True)
                    last.then_inc(ss_ready, 1)
                elif kind == "in":
                    mods = ph["mods"]

                    def body(i):
                        at_ = i + ph["mod"]
                        for par in range(2):
                            if mods:
                                if not isinstance(i, int) or q + par >= 2:
                                    pe.wait_ge(freed, 2 * i + (q + par - 1))
                                pe_mod(pe, 2 * i + (2 * ph["mod"] + par), ((c + 1) % 2, par), mod_hi, 3 + 4 * par)
                            pe_in_piece(pe, 2 * i + (q + par), par, ph["norm"],
                                        2 * i + (2 * ph["mod"] + par + 1) if mods else 2 * ph["mod"],
                                        at_ if mods else ph["mod"])
                        if mods:
                            pe.wait_ge(freed, 2 * i + (q + 1))
                            pe_mod_turn(pe, at_)
                    lead = 0 if q else 1
                    if lead:
                        body(0)
                    with pe.Fori(lead, ph["n"] // 2) as i:
                        body(i)
                elif kind == "out":
                    with pe.Fori(0, KD // 2) as i:
                        for par in range(2):
                            pe_out_piece(pe, 2 * i + (q + par), par, ph["tiles"], 1, hid_hi, hid_lo,
                                         (hid_ready, ph["hid"] - ph["tiles"]))
                else:
                    pe_mixers[kind](pe, ph)

        def act_hi(act, q, size, par, off=None, chunk=None):
            if chunk is None:
                chunk = (q - par) // 2 + off
            act.wait_ge(raw_in, 8 * (q - par) + 16)
            if not isinstance(q, int) or q >= 2:
                act.wait_ge(used, q - 1)
            nc.scalar.activation(w_hi[:, par, 0:size], raw[:, chunk % 2, par, 0:size], ACT.Copy).then_inc(hi_done, 1)

        def act_mod(act, m, slot, hi):
            act.wait_ge(mod_in, 8 * (m - slot[1]) + 16)
            nc.scalar.activation(hi, raw[:, slot[0], slot[1], :], ACT.Copy).then_inc(mod_hi_done, 1)

        def chunk_of(ph, i):
            return 2 * i + ph["c"] if ph["mods"] else i + ph["c"]

        def act_square(act, at_, k):
            n = k + KD * at_
            if not isinstance(n, int) or n >= 2:
                act.wait_ge(acc_ready, k + (KD * at_ - 1))
            nc.scalar.activation(sq[:, k % 2, :], x[:, k, :], ACT.Square).then_inc(sq_ready, 1)

        @block.scalar
        def _(act):
            act.dma_start(cvec[:], t["cvec"]).then_inc(in_c, 16)
            act.wait_ge(in_c, 16)
            nc.scalar.activation(csilu[:], cvec[:], ACT.Silu).then_inc(c_act, 1)
            act.wait_ge(c_act, 1)
            nc.scalar.activation(c4[:, :, 0:2], csilu[:], ACT.Copy).then_inc(c_act, 1)

            def silu_evac(q, par):
                act.wait_ge(used, q + 1)
                nc.scalar.activation(two(silu_s[:, par, :]), bank2(4 * par), ACT.Silu).then_inc(silu_ready, 1)

            for ph in seq:
                kind, q, nxt = ph["kind"], ph["q"], ph["next"]
                if kind == "mod":
                    for m in range(2 * ph["mods"]):
                        if m >= 2:
                            act.wait_ge(mod_used, m - 1)
                        act_mod(act, m, (m // 2 % 2, m % 2), w_hi[:, m % 2, :])
                        if m == 2:
                            act.wait_ge(in_x, 16 * KD)
                        if m >= 2:
                            act_square(act, 0, m - 2)
                elif kind == "norm":
                    n0_ = KD * ph["at"]
                    if not ph["early"]:
                        act.wait_ge(freed, q)
                        for k in range(KD):
                            act_square(act, ph["at"], k)
                    if nxt:
                        if q == 0:
                            act.wait_ge(mod_used, 2 * N_FIRST)
                        act_hi(act, q, nxt, 0, chunk=ph["next_c"])
                        if ph["next_mod"] is not None:
                            act.wait_ge(mod_used, 2 * ph["next_mod"])
                            act_mod(act, 2 * ph["next_mod"], ((ph["next_c"] + 1) % 2, 0), mod_hi[:])
                    act.wait_ge(eps_set, 1)
                    act.wait_ge(ss_ready, ph["at"] + 1)
                    nc.scalar.activation(two(root[:]), bank2(0), ACT.Sqrt, bias=eps_v[:],
                                         scale=1.0 / D).then_inc(root_ready, 1)
                    shift = ph["sub"] * 24
                    for k in range(KD):
                        act.wait_ge(nrm_ready, n0_ + k + 1)
                        for a, b, g in SEG:
                            last = nc.scalar.activation(xn_hi[:, k, a:b], nrm[:, k % 2, a:b], ACT.Identity,
                                                        bias=mod[:, shift + k, g:g + 1])
                        last.then_inc(xhi_ready, 1)
                elif kind == "in":
                    pairs, c, mods = ph["n"] // 2, ph["c"], ph["mods"]
                    slot = (c + 1) % 2

                    def mod_piece(i, par):
                        m = 2 * i + (2 * ph["mod"] + par)
                        act.wait_ge(mod_used, m)
                        act_mod(act, m, (slot, par), mod_hi[:])

                    def body(i, final):
                        act_hi(act, 2 * i + (q + 1), PIECE, 1, chunk=chunk_of(ph, i))
                        if mods:
                            mod_piece(i, 1)
                        silu_evac(2 * i + q, 0)
                        size = nxt if final else PIECE
                        if size:
                            act_hi(act, 2 * i + (q + 2), size, 0, chunk=ph["next_c"] if final else chunk_of(ph, i + 1))
                        if mods and not final:
                            mod_piece(i + 1, 0)
                        silu_evac(2 * i + (q + 1), 1)
                    if mods and not ph["after_norm"]:
                        mod_piece(0, 0)
                    with act.Fori(0, pairs - 1) as i:
                        body(i, False)
                    body(pairs - 1, True)
                elif kind == "out":
                    size, stats = size_of(ph), ph["stats"]

                    def square(i, par):
                        if stats is not None:
                            act.wait_ge(freed, 2 * i + (q + par + 1))
                            act_square(act, stats, 2 * i + par)

                    def body(i, final):
                        act_hi(act, 2 * i + (q + 1), size, 1, chunk=i + ph["c"])
                        square(i, 0)
                        if not final or nxt:
                            act_hi(act, 2 * i + (q + 2), nxt if final else size, 0,
                                   chunk=ph["next_c"] if final else i + (ph["c"] + 1))
                        square(i, 1)
                    with act.Fori(0, KD // 2 - 1) as i:
                        body(i, False)
                    body(KD // 2 - 1, True)
                elif kind != "mod":
                    act_mixers[kind](act, ph)

        def dve_lo(dve, q, size, par, off=None, chunk=None):
            if chunk is None:
                chunk = (q - par) // 2 + off
            dve.wait_ge(hi_done, q + 1)
            nc.vector.tensor_tensor(w_lo[:, par, 0:size], raw[:, chunk % 2, par, 0:size],
                                    w_hi[:, par, 0:size].bitcast(F32), ALU.subtract).then_inc(lo_done, 1)

        def add_gated(dve, m, bank):
            for b, a0, a1, g in PARTS:
                tok = slice(b * TH + a0, b * TH + a1)
                last = nc.vector.scalar_tensor_tensor(x[:, m, tok], psum[:, bank + b, a0:a1],
                                                      gate_v[:, m, g:g + 1], x[:, m, tok], ALU.mult, ALU.add)
            return last

        def clear_acc(dve, at_):
            nc.vector.memset(acc[:], 0.0).then_inc(acc_set, 1)
            dve.wait_ge(acc_set, at_ + 1)

        def add_square(dve, at_, k):
            dve.wait_ge(sq_ready, k + (KD * at_ + 1))
            n = k + KD * at_
            if not isinstance(n, int) or n:
                dve.wait_ge(acc_ready, n)
            nc.vector.tensor_tensor(acc[:], acc[:], sq[:, k % 2, :], ALU.add).then_inc(acc_ready, 1)

        def gate_of(dve, sub):
            dve.wait_ge(mod_freed, 6 * sub + 6)
            nc.vector.tensor_scalar(gate_v[:], mod[:, 24 * sub + 16:24 * sub + 24, :], 1.0 if sub in (1, 4) else 0.5,
                                    None, ALU.mult).then_inc(gate_ready, 1)
            dve.wait_ge(gate_ready, sub + 1)

        @block.vector
        def _(dve):
            nc.vector.memset(eps_v[:], EPS).then_inc(eps_set, 1)
            nc.vector.memset(ones[:], 1.0).then_inc(ones_set, 1)
            nc.vector.memset(mod_rows[:], 0.0).then_inc(rows_set, 1)
            dve.wait_ge(c_act, 2)
            nc.vector.tensor_tensor(c4[:, :, 2:4], csilu[:], c4[:, :, 0:2].bitcast(F32), ALU.subtract).then_inc(c_ready, 1)
            dve.wait_ge(in_bmod, 48)

            def dve_mod(m, slot, hi):
                dve.wait_ge(mod_hi_done, m + 1)
                nc.vector.tensor_tensor(raw_lo[:, slot[0], slot[1], :], raw[:, slot[0], slot[1], :], hi.bitcast(F32), ALU.subtract).then_inc(mod_lo_done, 1)

            def mod_copy(m, par):
                dve.wait_ge(mod_used, m + 1)
                nc.vector.tensor_scalar(mod_rows[32 * par:32 * par + 4, :], psum[0:4, 3 + 4 * par, 0:2 * P], 1.0, None,
                                        ALU.mult).then_inc(mod_copied, 1)

            def mod_evac(c):
                dve.wait_ge(mod_turned, c + 1)
                tiles = bass.ds(4 * c, 4)
                four = lambda buf: buf[:, tiles, :].rearrange("p (j n) g -> p j n g", j=2)
                nc.vector.tensor_tensor(four(mod), psum[:, 2, 0:8].rearrange("p (n j g) -> p j n g", n=2, j=2),
                                        four(bmod), ALU.add).then_inc(mod_freed, 1)

            def hid_evac(q, par, n, m):
                dve.wait_ge(silu_ready, n + 1)
                product = hid_f[:, m, :]
                nc.vector.tensor_tensor(two(product), two(silu_s[:, par, :]), bank2(4 * par + 2),
                                        ALU.mult).then_inc(freed, 1)
                dve.wait_ge(freed, q + 1)
                nc.vector.tensor_scalar(hid_hi[:, m, :], product, 1.0, None, ALU.mult).then_inc(mul_ready, 1)
                dve.wait_ge(mul_ready, n + 1)
                nc.vector.tensor_tensor(hid_lo[:, m, :], product, hid_hi[:, m, :].bitcast(F32),
                                        ALU.subtract).then_inc(hid_ready, 1)

            for ph in seq:
                kind, q, nxt = ph["kind"], ph["q"], ph["next"]
                if kind == "mod":
                    last = 2 * ph["mods"] - 1
                    dve_mod(0, (0, 0), w_hi[:, 0, :])
                    for m in range(last + 1):
                        if m < last:
                            dve_mod(m + 1, ((m + 1) // 2 % 2, (m + 1) % 2), w_hi[:, (m + 1) % 2, :])
                        mod_copy(m, m % 2)
                        if m % 2:
                            mod_evac(m // 2)
                        if m == 1:
                            clear_acc(dve, 0)
                        if m >= 2:
                            add_square(dve, 0, m - 2)
                elif kind == "norm":
                    n0_, sub = KD * ph["at"], ph["sub"]
                    tile0 = 24 * sub
                    if not ph["early"]:
                        dve.wait_ge(freed, q)
                        clear_acc(dve, ph["at"])
                        for k in range(KD):
                            add_square(dve, ph["at"], k)
                    if nxt:
                        dve_lo(dve, q, nxt, 0, chunk=ph["next_c"])
                        if ph["next_mod"] is not None:
                            dve_mod(2 * ph["next_mod"], ((ph["next_c"] + 1) % 2, 0), mod_hi[:])
                    dve.wait_ge(mod_freed, 6 * sub + 4)
                    if q:
                        dve.wait_ge(freed, q)
                    nc.vector.scalar_tensor_tensor(scale_v[:], mod[:, tile0 + 8:tile0 + 16, :], 1.0,
                                                   norm_g[:, 8 * sub:8 * sub + 8, :], ALU.add, ALU.mult).then_inc(vec_ready, 1)
                    if sub in (1, 4):
                        gate_of(dve, sub)
                    dve.wait_ge(vec_ready, ph["at"] + 1)
                    dve.wait_ge(root_ready, ph["at"] + 1)
                    nc.vector.reciprocal(rstd[:], root[:]).then_inc(rstd_ready, 1)
                    dve.wait_ge(rstd_ready, ph["at"] + 1)

                    def low(k):
                        dve.wait_ge(xhi_ready, n0_ + k + 1)
                        for a, b, g in SEG:
                            last = nc.vector.scalar_tensor_tensor(xn_lo[:, k, a:b], nrm[:, k % 2, a:b],
                                                                  mod[:, tile0 + k, g:g + 1],
                                                                  xn_hi[:, k, a:b].bitcast(F32), ALU.add, ALU.subtract)
                        last.then_inc(xn_ready, 1)
                    for k in range(KD):
                        if n0_ + k >= 2:
                            dve.wait_ge(xn_ready, n0_ + k - 1)
                        for a, b, g in SEG:
                            last = nc.vector.scalar_tensor_tensor(nrm[:, k % 2, a:b], x[:, k, a:b], scale_v[:, k, g:g + 1],
                                                                  rstd[:, a:b], ALU.mult, ALU.mult)
                        last.then_inc(nrm_ready, 1)
                        if k >= 1:
                            low(k - 1)
                    low(KD - 1)
                    if ph["at"] == 0:
                        dve.wait_ge(in_cst, 112)
                elif kind == "in":
                    pairs, mods = ph["n"] // 2, ph["mods"]
                    slot = (ph["c"] + 1) % 2

                    def body(i, final):
                        m = 2 * i + 2 * ph["mod"]
                        if mods:
                            mod_copy(m, 0)
                        dve_lo(dve, 2 * i + (q + 1), PIECE, 1, chunk=chunk_of(ph, i))
                        if mods:
                            dve_mod(m + 1, (slot, 1), mod_hi[:])
                        hid_evac(2 * i + q, 0, 2 * i + ph["hid"], 2 * i + ph["k0"])
                        if mods:
                            mod_copy(m + 1, 1)
                        size = nxt if final else PIECE
                        if size:
                            dve_lo(dve, 2 * i + (q + 2), size, 0, chunk=ph["next_c"] if final else chunk_of(ph, i + 1))
                        if mods and not final:
                            dve_mod(m + 2, (slot, 0), mod_hi[:])
                        hid_evac(2 * i + (q + 1), 1, 2 * i + (ph["hid"] + 1), 2 * i + (ph["k0"] + 1))
                        if mods:
                            mod_evac(i + ph["mod"])
                    if mods and not ph["after_norm"]:
                        dve_mod(2 * ph["mod"], (slot, 0), mod_hi[:])
                    with dve.Fori(0, pairs - 1) as i:
                        body(i, False)
                    body(pairs - 1, True)
                elif kind == "out":
                    size, stats = size_of(ph), ph["stats"]
                    if ph["half"] == 0:
                        gate_of(dve, ph["sub"])
                    if stats is not None:
                        clear_acc(dve, stats)

                    def body(i, final):
                        for par in range(2):
                            nsize = size if par == 0 or not final else nxt
                            if nsize:
                                chunk = i + ph["c"] + par if not final or par == 0 else ph["next_c"]
                                dve_lo(dve, 2 * i + (q + par + 1), nsize, 1 - par, chunk=chunk)
                            dve.wait_ge(used, 2 * i + (q + par + 1))
                            add_gated(dve, 2 * i + par, 4 * par).then_inc(freed, 1)
                            if stats is not None:
                                add_square(dve, stats, 2 * i + par)
                    with dve.Fori(0, KD // 2 - 1) as i:
                        body(i, False)
                    body(KD // 2 - 1, True)
                else:
                    dve_mixers[kind](dve, ph)


def layout(a):
    f = lambda v: np.ascontiguousarray(v, dtype=np.float32)
    a = {k: np.asarray(v) for k, v in a.items()}

    def cols(v):
        return np.moveaxis(v.reshape(v.shape[:-1] + (-1, P)), -1, 0)

    o = {}
    tokens = np.concatenate([a["x_prompt"][0], a["x_sample"][0]], 0)
    o["x"] = tokens.T.reshape(KD, P, T)
    o["cvec"] = np.stack([cols(a["c_ctx"]), cols(a["c"][0])], -1)
    twice = lambda v: np.repeat(v[..., None], 2, -1)
    o["bmod"] = twice(cols(a["b_mod"]).reshape(P, 144))
    o["norm_g"] = twice(cols(a["norm_g"]).reshape(P, 48))
    o["w_mod"] = a["w_mod"].reshape(2, KD, P, 18, 2, 2 * P).transpose(0, 3, 2, 4, 1, 5).reshape(36, P, 2, PIECE)
    w = a["ffn_w_in"].reshape(4, KD, P, 2, MF // 2, 2, P)
    o["w_in"] = w.transpose(0, 4, 2, 5, 1, 3, 6).reshape(4, MF // 2, P, 2, PIECE)
    w = a["ffn_w_out"].reshape(4, MF, P, KD // 2, 2, P)
    for n, (k0, kt) in enumerate(((0, HALVES[0]), HALVES)):
        o[f"w_out{n}"] = w[:, k0:k0 + kt].transpose(0, 3, 2, 4, 1, 5).reshape(4, KD // 2, P, 2, kt * P)
    w = a["ml_w_up"][0].reshape(KD, P, 2, NT // 2, 2, P)
    o["w_up"] = w.transpose(3, 1, 4, 0, 2, 5).reshape(NT // 2, P, 2, PIECE)
    w = a["ml_w_down"][0].reshape(NH, HT, P, 2, 4, P)
    o["w_heads"] = w.transpose(0, 2, 3, 4, 1, 5).reshape(NH, P, 2, PIECE)
    params = np.concatenate([a["ml_conv_w"][0].T.reshape(NT, P, CONV).transpose(1, 0, 2).reshape(P, -1),
                             cols(a["ml_conv_b"][0]), cols(a["ml_head_g"][0]), cols(a["ml_skip"][0])], 1)
    o["mlp"] = params
    o["wq3"] = a["ml_w_qkv"][0].reshape(3, NT, P // 4, 4, 4).transpose(2, 3, 0, 1, 4).reshape(P, 3, NT, 4)
    w = a["ml_w_gate"][0].reshape(2, 3, NT, P // 4, 4 * 8).transpose(3, 1, 0, 2, 4)
    o["wgr"] = np.repeat(w, 4, 0)
    o["bgate"] = np.broadcast_to(a["ml_b_gate"][0].reshape(1, 16), (P, 16))
    o["m0"] = np.broadcast_to(a["state_mlstm_m"][0, 0].reshape(1, 8), (P, 8))
    o["m0row"] = a["state_mlstm_m"][0, 0].T
    o["n0"] = cols(a["state_mlstm_n"][0, 0]).transpose(0, 2, 1, 3).reshape(P, NH, 8)
    o["c0"] = a["state_mlstm_C"][0, 0].reshape(2, NH, DH, HT, P).transpose(1, 4, 0, 3, 2)
    w = a["mla_w_in"][0]
    kr = w[:, QL + KV:]
    w = np.concatenate([w, kr], 1).reshape(KD, P, 2, 2, P)
    o["w_attn_in"] = w.transpose(1, 2, 0, 3, 4).reshape(1, P, 2, PIECE)
    w = a["mla_w_uq"][0].reshape(2, P, 2, 4, QK)
    nope = w[..., :128].reshape(2, P, 2, 4, P)
    rope = w[..., 128:].reshape(2, P, 2, 2, P)
    w = np.concatenate([nope, rope], 3)
    o["w_attn_q"] = w.transpose(1, 2, 3, 0, 4).reshape(1, P, 2, 12 * P)
    w = a["mla_w_ukv"][0].reshape(P, AH, 2, P).transpose(0, 2, 1, 3)
    o["w_attn_kv"] = w.reshape(1, P, 2, AH * P)
    w = a["mla_w_o"][0].reshape(AH, P, 2, 2, 2, P)
    o["w_attn_out"] = w.transpose(2, 1, 3, 4, 0, 5).reshape(2, P, 2, PIECE)
    g = a["mla_qk_g"][0]
    dup = lambda v: np.concatenate([v, v])
    o["attn_g"] = np.stack([g[0, :128], dup(g[0, 128:]), g[1, :128], dup(g[1, 128:]),
                            *cols(a["mla_q_norm_g"][0]).T, a["mla_kv_norm_g"][0], a["mla_kv_norm_g"][0]], 1)
    cache = a["cache_mla"][0, 0].T
    o["cache_c"] = cache[:KV]
    o["cache_r"] = np.concatenate([cache[KV:], cache[KV:]], 0)
    i = np.arange(P)
    low, high = (i[:, None] <= i[None, :]), (i[:, None] >= i[None, :])
    rot = np.zeros((P, P))
    for b in (0, 64):
        for n in range(32):
            rot[b + 32 + n, b + n] = -1.0
            rot[b + n, b + 32 + n] = 1.0
    o["cst"] = np.concatenate([np.eye(P), low, high, np.where(low, 0.0, -1e30), np.where(high, 0.0, -1e30),
                               np.repeat(i[:, None] < 64, P, 1), np.repeat(i[:, None] >= 64, P, 1), rot,
                               i[:, None] // 4 == np.arange(32)[None, :],
                               [[r % 32 < 4 and (r // 32, r % 2) == divmod(n, 2) for n in range(4)] for r in i]], 1)
    pos = np.arange(NL)
    freqs = 10000.0 ** -(np.arange(16) / 16.0)
    ang = np.concatenate([(pos // 64)[:, None] * freqs, (pos % 64)[:, None] * freqs], 1).T
    four = np.concatenate([ang] * 4, 0)
    o["ropes"] = np.stack([np.cos(four), np.sin(four)], 1)
    return {k: f(v) for k, v in o.items()}


OUTS = {"y": (KD, P, T), "new_c": (NH, 2, DH, DH), "new_n": (NH, 2, 1, DH), "new_m": (4, 2), "new_kv": (KV + 64, NP_)}


def kernel(**inputs):
    import concourse.bacc as bacc
    from concourse.bass_utils import run_bass_kernel_spmd

    nc = bacc.Bacc("TRN2", target_bir_lowering=False, num_devices=1)
    arrays = {"in_" + n: v for n, v in layout(inputs).items()}
    t = {n[3:]: nc.dram_tensor(n, v.shape, F32, kind="ExternalInput").ap() for n, v in arrays.items()}
    t.update({n: nc.dram_tensor("out_" + n, s, F32, kind="ExternalOutput").ap() for n, s in OUTS.items()})
    build(nc, t)
    r = run_bass_kernel_spmd(nc, [arrays], core_ids=[0]).results[0]
    y = r["out_y"].reshape(D, T).T
    return (np.ascontiguousarray(y[:NP_])[None], np.ascontiguousarray(y[NP_:])[None],
            np.ascontiguousarray(r["out_new_c"].transpose(1, 0, 2, 3))[None, None],
            np.ascontiguousarray(r["out_new_n"].reshape(NH, 2, DH).transpose(1, 0, 2))[None, None],
            np.ascontiguousarray(r["out_new_m"].T)[None, None],
            np.ascontiguousarray(r["out_new_kv"].T)[None, None])
```

```python
from contextlib import ExitStack

import concourse.bass as bass
from concourse import mybir
import numpy as np

F32 = mybir.dt.float32
F32R = mybir.dt.float32r
ALU = mybir.AluOpType
ACT = mybir.ActivationFunctionType
AX_X = mybir.AxisListType.X

P = 128
D = 1024
KD = D // P
NP_ = 128
NL = 512
T = NP_ + NL
TH = T // 2
FF = 2816
MF = FF // P
HALVES = (12, MF - 12)
PIECE = 16 * P
DI = 2048
NT = DI // P
NH = 4
DH = DI // NH
HT = DH // P
CONV = 5
GAP = CONV // 2
TG = T + GAP
AH = 8
QK = 192
QL = 256
KV = 128
PAST = 128
TK = T + PAST
EPS = 1e-6
N_MOD = 36
N_FIRST = 5
SEG = ((0, NP_, 0), (NP_, T, 1))


def mm3(pe, out, w_hi, w_lo, x_hi, x_lo, first, last):
    pe.matmul(out, w_hi, x_hi, start=first, stop=False)
    pe.matmul(out, w_hi, x_lo, start=False, stop=False)
    return pe.matmul(out, w_lo, x_hi, start=False, stop=last)


def plan():
    seq = []
    q = c = n_norm = n_hid = n_mod = 0

    def add(kind, pieces, mods=0, **kw):
        nonlocal q, c, n_mod
        seq.append(dict(kind=kind, q=q, n=pieces, c=c, mods=mods, mod=n_mod, off=c - q // 2, **kw))
        q += pieces
        c += pieces // 2 + mods
        n_mod += mods

    def norm(sub, early=True):
        nonlocal n_norm
        add("norm", 0, 0, sub=sub, at=n_norm, early=early)
        n_norm += 1

    def ffn(f, sub, with_mod):
        nonlocal n_hid
        for half, tiles in enumerate(HALVES):
            k = 0
            for n, mods in ((2 * with_mod[half], with_mod[half]), (tiles - 2 * with_mod[half], 0)):
                if n:
                    add("in", n, mods, f=f, pair=(half * HALVES[0] + k) // 2, k0=k, hid=n_hid, norm=n_norm - 1)
                    n_hid += n
                    k += n
            add("out", KD, f=f, half=half, tiles=tiles, sub=sub, hid=n_hid, stats=n_norm if half else None)

    add("mod", 0, N_FIRST)
    norm(0)
    ffn(0, 0, (6, 5))
    norm(1)
    add("up", NT)
    add("gates", 0)
    add("heads", 2 * NH, sub=1)
    norm(2, early=False)
    ffn(1, 2, (6, 5))
    norm(3)
    ffn(2, 3, (6, 3))
    norm(4)
    add("attn_in", 2)
    add("attn_q", 2)
    add("attn_kv", 2)
    add("attn", 0)
    add("attn_out", 4, sub=4, stats=n_norm)
    norm(5)
    ffn(3, 5, (0, 0))
    seq[-1]["stats"] = None
    assert n_mod == N_MOD
    return seq


SIZE = {"in": PIECE, "up": PIECE, "heads": PIECE, "attn_in": PIECE, "attn_q": 12 * P,
        "attn_kv": 8 * P, "attn_out": PIECE}


def size_of(phase):
    return phase["tiles"] * P if phase["kind"] == "out" else SIZE[phase["kind"]]


def build(nc, t):
    with ExitStack() as ctx:
        def sb(name, shape, dt=F32):
            return ctx.enter_context(nc.sbuf_tensor(name, shape, dt))

        def sem(name):
            return ctx.enter_context(nc.semaphore(name))

        seq = plan()
        for n, ph in enumerate(seq):
            after = seq[n + 1] if n + 1 < len(seq) else None
            ph["next"] = size_of(after) if after and after["n"] else None
            ph["next_c"] = after["c"] if after else None
            ph["next_mod"] = after["mod"] if after and after["mods"] else None
            ph["after_norm"] = n > 0 and seq[n - 1]["kind"] == "norm"
            if ph["kind"] in ("up", "heads", "gates"):
                ph["next"] = None

        x = sb("x", [P, KD, T])
        w_hi = sb("w_hi", [P, 2, PIECE], F32R)
        w_lo = sb("w_lo", [P, 2, PIECE], F32R)
        mod = sb("mod", [P, 2 * 72, 2])
        bmod = sb("bmod", [P, 2 * 72, 2])
        norm_g = sb("norm_g", [P, 48, 2])
        cvec = sb("cvec", [P, KD, 2])
        csilu = sb("csilu", [P, KD, 2])
        c4 = sb("c4", [P, KD, 4], F32R)
        mod_rows = sb("mod_rows", [36, 2 * P])
        scale_v = sb("scale_v", [P, KD, 2])
        gate_v = sb("gate_v", [P, KD, 2])
        eps_v = sb("eps_v", [P, 1])
        ones = sb("ones", [P, P])
        cst = sb("cst", [P, 8 * P + 36])
        ident, upto, downto, bias_f, bias_b, sel_a, sel_b, rot = (cst[:, i * P:(i + 1) * P] for i in range(8))
        bdmask = cst[:, 8 * P:8 * P + 32]
        sum_parts = cst[0:36, 8 * P + 32:]
        mlp = sb("mlp", [P, NT * (CONV + 3)])
        conv_w = mlp[:, 0:NT * CONV].rearrange("p (t k) -> p t k", k=CONV)
        conv_b, head_g, skip = (mlp[:, NT * (CONV + i):NT * (CONV + i + 1)] for i in range(3))
        wq3 = sb("wq3", [P, 3, NT, 4])
        bgate = sb("bgate", [P, 16])
        m0 = sb("m0", [P, 8])
        n0 = sb("n0", [P, NH, 8])
        m0row = sb("m0row", [4, 2])
        a_col = sb("a_col", [P, 5, 2, 4])
        attn_g = sb("attn_g", [P, 8])
        soft = sb("soft", [P, 8])
        psum = ctx.enter_context(nc.psum_tensor("psum", [P, 8, 512], F32))

        base = (nc.sbuf_base + 31) // 32 * 32
        raw = nc.alloc_sbuf_tensor_at("raw", [P, 2, 2, PIECE], F32, offset=base)
        raw_lo = nc.alloc_sbuf_tensor_at("raw_lo", [P, 2, 2, PIECE], F32R, offset=base)
        base += 16 * PIECE
        arena_kb = (nc.sbuf_usable_end - base) // 1024

        def at(name, kb, shape, dt=F32):
            size = 4
            for n in shape[1:]:
                size *= n
            assert kb * 1024 + size <= arena_kb * 1024, (name, arena_kb)
            return nc.alloc_sbuf_tensor_at(name, shape, dt, offset=base + int(kb * 1024))

        xn_hi = at("xn_hi", 0, [P, KD, T], F32R)
        xn_lo = at("xn_lo", 20, [P, KD, T], F32R)
        hid_hi = at("hid_hi", 40, [P, HALVES[0], T], F32R)
        hid_lo = at("hid_lo", 70, [P, HALVES[0], T], F32R)
        hid_f = at("hid_f", 70, [P, HALVES[0], T])
        silu_s = at("silu_s", 100, [P, 2, T])
        mod_hi = at("mod_hi", 105, [P, PIECE], F32R)
        sq = at("sq", 100, [P, 2, T])
        acc = at("acc", 0, [P, T])
        root = at("root", 45, [P, T])
        rstd = at("rstd", 47.5, [P, T])
        nrm = at("nrm", 50, [P, 2, T])
        wgr = at("wgr", 64, [P, 3, 2, NT, 32])
        gate_w = at("gate_w", 80, [P, 2, NT, 16])
        gtmp = at("gtmp", 76, [P, NT, 16])
        xm_pad = at("xm_pad", 40, [P, 2, TG + 2 * GAP])
        conv = at("conv", 46, [P, 2, TG])
        xc_s = at("xc_s", 52, [P, 2, T])
        z_s = at("z_s", 57, [P, 2, T])
        gt = at("gt", 64, [P, 10, 8])
        g_abs = at("g_abs", 65, [P, 10, 4])
        g_exp = at("g_exp", 66, [P, 10, 4])
        g_ln = at("g_ln", 67, [P, 10, 4])
        logf = at("logf", 68, [P, 10, 4])
        b_col = at("b_col", 69, [P, 10, 4])
        a_row = at("a_row", 70, [4, 2, T])
        b_row = at("b_row", 75, [4, 2, T])
        m_row = at("m_row", 80, [4, 2, T])
        s_row = at("s_row", 85, [4, 2, T])
        rows = at("rows", 90, [4, 4, T])
        m_new = at("m_new", 100, [4, 2])
        xm_h = at("xm_h", 0, [P, HT, T])
        alpha = at("alpha", 0, [P, 2, NL])
        rden = at("rden", 4, [P, 2, T])
        se_p = at("se_p", 9, [P, 2, P])
        xc_h = at("xc_h", 10, [P, HT, T])
        w_tok = at("w_tok", 20, [P, 2])
        vw = at("vw", 22, [P, 2, DH])
        nq_d = at("nq_d", 22, [P, 2, NL])
        k_tok = at("k_tok", 26, [P, DH])
        h_tmp = at("h_tmp", 26, [P, NL])
        q_t = at("q_t", 28, [P, HT, T])
        k_t = at("k_t", 38, [P, HT, T])
        y_hi = at("y_hi", 28, [P, HT, T], F32R)
        y_lo = at("y_lo", 38, [P, HT, T], F32R)
        v_tok = at("v_tok", 48, [P, 5, DH])
        c_out = at("c_out", 58, [P, 2, DH])
        se_f = at("se_f", 58, [P, 4, NL])
        se_b = at("se_b", 66, [P, 4, NL])
        zs_h = at("zs_h", 66, [P, HT, T])
        c_t = at("c_t", 76, [P, 2, HT, DH])
        h_sq = at("h_sq", 76, [P, 2, T])
        h_root = at("h_root", 81, [P, T])
        h_rstd = at("h_rstd", 83.5, [P, T])
        h_t = at("h_t", 92, [P, HT, T])
        bd = at("bd", 92, [P, 3, HT, P])
        n_bc = at("n_bc", 98, [P, 8, P])
        bc = at("bc", 102, [P, 4, T])
        c_sq = at("c_sq", 40, [P, 2, T])
        c_root = at("c_root", 68, [P, 2, T])
        c_rstd = at("c_rstd", 73, [P, 2, T])
        kn_raw = at("kn_raw", 24, [P, AH, TK])
        qn_raw = at("qn_raw", 48, [P, AH, T])
        qr_raw = at("qr_raw", 68, [P, AH // 2, T])
        cq = at("cq", 78, [P, 2, T])
        ent = at("ent", 83, [P, TK])
        kr = at("kr", 86, [P, TK])
        cq_hi = at("cq_hi", 89, [P, 2, T], F32R)
        cq_lo = at("cq_lo", 94, [P, 2, T], F32R)
        ent_hi = at("ent_hi", 99, [P, TK], F32R)
        ent_lo = at("ent_lo", 102, [P, TK], F32R)
        k_rot = at("k_rot", 105, [P, TK])
        r_in = at("r_in", 108, [P, 88])
        r_out = at("r_out", 108.5, [P, 88])
        r_s = at("r_s", 109, [P, 88])
        r_n = at("r_n", 109.5, [P, 88])
        r_kr = at("r_kr", 110, [P, TK // P])
        g_both = at("g_both", 110.25, [P, 1])
        sq_q = at("sq_q", 84, [P, 2, T])
        sq_r = at("sq_r", 94, [P, 2, T])
        rope_t = at("rope_t", 12, [P, NL])
        sq_k = at("sq_k", 18, [P, 2, TK])
        kr_sq = at("kr_sq", 78, [P, TK])
        ropes = at("ropes", 89.5, [P, 2, NL])
        dg = at("dg", 78, [P, 2, TK // P, P])
        krs = at("krs", 0, [P, AH // 2, TK])
        v_h = at("v_h", 12, [P, TK // P, P])
        qs = at("qs", 15, [P, 2, T])
        qrs = at("qrs", 78, [P, 2, T])
        pt = at("pt", 84, [P, 5, NL])
        prob = at("prob", 94, [P, 2, T])
        pt0 = at("pt0", 110.5, [P, P])
        o_hi = at("o_hi", 48, [P, AH, T], F32R)
        o_lo = at("o_lo", 24, [P, AH, T], F32R)

        xm_d = nc.dram_tensor("xm_d", (NT, P, T), F32, kind="Internal").ap()
        xc_d = nc.dram_tensor("xc_d", (NT, P, T), F32, kind="Internal").ap()
        z_d = nc.dram_tensor("z_d", (NT, P, T), F32, kind="Internal").ap()
        rows_d = nc.dram_tensor("rows_d", (NH, 4, T), F32, kind="Internal").ap()

        raw_in, mod_in, hi_done, lo_done, used, freed = (sem(n) for n in ("raw_in", "mod_in", "hi_done", "lo_done", "used", "freed"))
        mod_hi_done, mod_lo_done, mod_used, mod_copied, mod_turned, mod_freed = (
            sem(n) for n in ("mod_hi_done", "mod_lo_done", "mod_used", "mod_copied", "mod_turned", "mod_freed"))
        rows_set = sem("rows_set")
        in_c, in_bmod, in_cst, in_x = sem("in_c"), sem("in_bmod"), sem("in_cst"), sem("in_x")
        eps_set, ones_set, c_act, c_ready = sem("eps_set"), sem("ones_set"), sem("c_act"), sem("c_ready")
        vec_ready, gate_ready, sq_ready, acc_set, acc_ready = (
            sem(n) for n in ("vec_ready", "gate_ready", "sq_ready", "acc_set", "acc_ready"))
        ss_ready, root_ready, rstd_ready, nrm_ready = sem("ss_ready"), sem("root_ready"), sem("rstd_ready"), sem("nrm_ready")
        xhi_ready, xn_ready = sem("xhi_ready"), sem("xn_ready")
        silu_ready, mul_ready, hid_ready = sem("silu_ready"), sem("mul_ready"), sem("hid_ready")
        y_out = sem("y_out")

        def bank2(b):
            return psum[:, b:b + 2, 0:TH]

        def half(ap, n):
            return ap[..., n * TH:(n + 1) * TH]

        def two(ap):
            return ap.rearrange("p (h n) -> p h n", h=2)

        PARTS = ((0, 0, NP_, 0), (0, NP_, TH, 1), (1, 0, TH, 1))

        leaves = []
        for ph in seq:
            for i in range(max(ph["n"] // 2, ph["mods"])):
                if ph["n"]:
                    leaves.append(("w", ph["q"] + 2 * i + 2))
                if ph["mods"]:
                    leaves.append(("mod", 2 * (ph["mod"] + i) + 2))

        in_wgr, gw_tmp = sem("in_wgr"), sem("gw_tmp")
        xm_acc, xm_ready, conv_ready, xc_ready = sem("xm_acc"), sem("xm_ready"), sem("conv_ready"), sem("xc_ready")
        pad_set, gate_mm = sem("pad_set"), sem("gate_mm")
        xm_out, xc_out, z_out = ([sem(f"{n}_out{par}") for par in range(2)] for n in ("xm", "xc", "z"))
        conv_tap = sem("conv_tap")
        g_dve, g_act, g_pe, rows_out, m_out = sem("g_dve"), sem("g_act"), sem("g_pe"), sem("rows_out"), sem("m_out")
        in_xm, in_xc, in_bc, in_ct, in_z = sem("in_xm"), sem("in_xc"), sem("in_bc"), sem("in_ct"), sem("in_z")
        bd_ready, qk_mm, qk_ev, kt_mm, kt_ev, v_mm, v_ev = (sem(n) for n in ("bd_ready", "qk_mm", "qk_ev", "kt_mm", "kt_ev", "v_mm", "v_ev"))
        wt_ready, vw_ready, cn_mm, cn_ev = (sem(n) for n in ("wt_ready", "vw_ready", "cn_mm", "cn_ev"))
        cn_out = [sem("cn_out0"), sem("cn_out1")]
        s_mm, nq_mm, nq_ev, arg_ready, e_ready, dec_ready, se_ready = (sem(n) for n in ("s_mm", "nq_mm", "nq_ev", "arg_ready", "e_ready", "dec_ready", "se_ready"))
        den_mm, den_step, w_ready, g_mm, g_ev, h_step = (sem(n) for n in ("den_mm", "den_step", "w_ready", "g_mm", "g_ev", "h_step"))
        h_mm, h_ready, hsq_ready, hsq_used, hroot_ready, hrstd_ready = (sem(n) for n in ("h_mm", "h_ready", "hsq_ready", "hsq_used", "hroot_ready", "hrstd_ready"))
        y_norm, y_sum, y_high = sem("y_norm"), sem("y_sum"), sem("y_high")
        y_step, y_ready, wd_mm, wd_ev = sem("y_step"), sem("y_ready"), sem("wd_mm"), sem("wd_ev")

        S_ML = float(DH) ** -0.5

        def lat(j):
            return slice(j * P, (j + 1) * P)

        def pe_up(pe, ph):
            q0, n_at = ph["q"], 1

            def gate_sums(tt, first, last_):
                pe.wait_ge(xc_ready, tt + 1)
                for j in range(5):
                    a, b = j * P, (j + 1) * P
                    g = a + (GAP if j else 0) + GAP
                    for src, (lhs, w) in enumerate(((xc_s[:, first % 2, a:b], 0), (xm_pad[:, first % 2, g:g + P], 1))):
                        last = pe.matmul(psum[:, 4, 16 * j:16 * j + 16], lhs, gate_w[:, w, tt, :],
                                         start=(first == 0 and j == 0 and src == 0), stop=(last_ and src == 1),
                                         skip_group_check=True)
                last.then_inc(gate_mm, 1)

            def tile(q, par, tt):
                pe.wait_ge(lo_done, q + 1)
                for side in range(2):
                    if side == 0:
                        if not isinstance(tt, int) or tt:
                            pe.wait_ge(xm_ready, tt)
                    else:
                        pe.wait_ge(freed, q)
                        if isinstance(tt, int):
                            pe.wait_ge(mod_freed, ph["mod"])
                    for k in range(KD):
                        if side == 0:
                            pe.wait_ge(xn_ready, KD * n_at + k + 1)
                        s = slice((k * 2 + side) * P, (k * 2 + side + 1) * P)
                        for n in range(2):
                            last = mm3(pe, psum[:, 2 * side + n, 0:TH], w_hi[:, par, s], w_lo[:, par, s],
                                       half(xn_hi[:, k, :], n), half(xn_lo[:, k, :], n), k == 0, k == KD - 1)
                    last.then_inc(xm_acc if side == 0 else used, 1)

            tile(q0, 0, 0)
            tile(q0 + 1, 1, 1)
            pe.wait_ge(gw_tmp, 44)
            gate_sums(0, 0, False)
            with pe.Fori(1, NT // 2) as i:
                tile(2 * i + q0, 0, 2 * i)
                gate_sums(2 * i - 1, 3, False)
                tile(2 * i + (q0 + 1), 1, 2 * i + 1)
                gate_sums(2 * i, 2, False)
            gate_sums(NT - 1, NT - 1, True)

        def pe_gates(pe, ph):
            pe.wait_ge(g_dve, 4)
            for j in range(5):
                for d, tri in enumerate((upto, downto)):
                    out = psum[:, 5, 8 * j + 4 * d:8 * j + 4 * d + 4]
                    others = [] if j == 0 else [s for s in range(1, 5) if (s < j if d == 0 else s > j)]
                    last = pe.matmul(out, tri, logf[:, 2 * j + d, :], start=True, stop=not others)
                    for s in others:
                        last = pe.matmul(out, ones[:], logf[:, 2 * s + d, :], start=False, stop=(s == others[-1]))
            last.then_inc(g_pe, 1)
            pe.wait_ge(g_dve, 6)
            for src, col in enumerate((a_col, b_col)):
                for d in range(2):
                    for j in range(5):
                        c_in = a_col[:, j, d, :] if src == 0 else b_col[:, 2 * j + d, :]
                        out = psum[0:4, 2 * src + d, (j - 1) * P:j * P] if j else psum[0:4, 6, (2 * src + d) * P:(2 * src + d + 1) * P]
                        last = pe.transpose(out, c_in, ident)
            last.then_inc(g_pe, 1)

        def pe_heads(pe, ph):
            q0 = ph["q"]
            with pe.Fori(0, NH) as h:
                pe.wait_ge(freed, 2 * h + q0)
                pe.wait_ge(bd_ready, h + 1)
                pe.wait_ge(in_xc, 16 * h + 16)
                for n in range(2 * HT):
                    if n >= 2:
                        pe.wait_ge(qk_ev, 2 * HT * h + (n - 1))
                    for b in range(2):
                        last = pe.matmul(psum[:, 2 * (n % 2) + b, 0:TH], bd[:, n // HT, n % HT, :],
                                         half(xc_h[:, n % HT, :], b), start=True, stop=True)
                    last.then_inc(qk_mm, 1)
                for k in range(HT):
                    last = pe.matmul(psum[:, 6, k * P:(k + 1) * P], xc_h[:, k, 0:P], bd[:, 1, k, :], start=True, stop=True)
                last.then_inc(kt_mm, 1)
                pe.wait_ge(in_xm, 16 * h + 16)
                for j in range(5):
                    if j >= 2:
                        pe.wait_ge(v_ev, 5 * h + (j - 1))
                    for k in range(HT):
                        last = pe.matmul(psum[:, 4 + j % 2, k * P:(k + 1) * P], xm_h[:, k, j * P:(j + 1) * P],
                                         bd[:, 2, k, :], start=True, stop=True)
                    last.then_inc(v_mm, 1)
                pe.wait_ge(vw_ready, h + 1)
                pe.wait_ge(kt_ev, h + 1)
                for n in range(10):
                    if n >= 2:
                        pe.wait_ge(cn_ev, 10 * h + (n - 1))
                    if n < 8:
                        last = pe.matmul(psum[:, 6 + n % 2, :], vw[:, n // HT, (n % HT) * P:(n % HT + 1) * P],
                                         k_tok[:], start=True, stop=True)
                    else:
                        last = pe.matmul(psum[0:1, 6 + n % 2, :], w_tok[:, n - 8:n - 7], k_tok[:], start=True, stop=True)
                    last.then_inc(cn_mm, 1)
                pe.wait_ge(qk_ev, 2 * HT * h + 2 * HT)
                for j in range(4):
                    for k in range(HT):
                        last = pe.matmul(psum[:, j, :], k_t[:, k, lat(j + 1)], q_t[:, k, NP_:T], start=(k == 0), stop=(k == HT - 1))
                pe.wait_ge(cn_ev, 10 * h + 10)
                for k in range(HT):
                    last = pe.matmul(psum[:, 6, 0:P], k_t[:, k, 0:P], q_t[:, k, 0:P], start=(k == 0), stop=(k == HT - 1))
                last.then_inc(s_mm, 1)
                pe.wait_ge(v_ev, 5 * h + 5)
                for d in range(2):
                    for k in range(HT):
                        last = pe.matmul(psum[:, 4 + d, :], n_bc[:, HT * d + k, :], q_t[:, k, NP_:T], start=(k == 0), stop=(k == HT - 1))
                last.then_inc(nq_mm, 1)
                pe.wait_ge(nq_ev, h + 1)
                pe.wait_ge(se_ready, h + 1)
                for k in range(4):
                    pe.matmul(psum[:, 4, k * P:NL], ones[:], se_f[:, k, k * P:NL], start=(k == 0), stop=(k == 3))
                for k in (3, 2, 1, 0):
                    pe.matmul(psum[:, 5, 0:(k + 1) * P], ones[:], se_b[:, k, 0:(k + 1) * P], start=(k == 3), stop=(k == 0))
                for d in range(2):
                    last = pe.matmul(psum[:, 6, d * P:(d + 1) * P], ones[:], se_p[:, d, :], start=True, stop=True)
                last.then_inc(den_mm, 1)
                pe.wait_ge(in_ct, 16 * h + 16)
                for n in range(8):
                    if n == 4:
                        pe.wait_ge(den_step, 5 * h + 1)
                    for k in range(HT):
                        last = pe.matmul(psum[:, n, :], c_t[:, n % 2, k, (n // 2) * P:(n // 2 + 1) * P],
                                         q_t[:, k, NP_:T], start=(k == 0), stop=(k == HT - 1))
                    last.then_inc(g_mm, 1)
                pe.wait_ge(w_ready, h + 1)
                for n in range(HT):
                    pe.wait_ge(g_ev, 8 * h + (n + 1))
                    for k in range(4):
                        last = pe.matmul(psum[:, n, :], v_tok[:, k + 1, n * P:(n + 1) * P], se_f[:, k, :], start=(k == 0), stop=(k == 3))
                    pe.wait_ge(g_ev, 8 * h + (n + 5))
                    last = pe.matmul(psum[:, 4 + n, 0:P], v_tok[:, 0, n * P:(n + 1) * P], se_p[:, 0, :], start=True, stop=True)
                    last.then_inc(h_mm, 1)
                pe.wait_ge(h_ready, HT * h + HT)
                for k in range(HT):
                    pe.wait_ge(hsq_ready, HT * h + (k + 1))
                    for b in range(2):
                        last = pe.matmul(psum[:, b, 0:TH], ones[:], half(h_sq[:, k % 2, :], b), start=(k == 0), stop=(k == HT - 1))
                    last.then_inc(hsq_used, 1)
                pe.wait_ge(hroot_ready, h + 1)
                for p in range(2):
                    pe.wait_ge(lo_done, 2 * h + (q0 + p + 1))
                    for m in range(4):
                        n = 4 * p + m
                        if n - 2 in (3, 7):
                            pe.wait_ge(freed, 2 * h + (q0 + (n - 2) // 4 + 1))
                        elif n >= 2:
                            pe.wait_ge(wd_ev, 6 * h + (n - 2 - (n - 2) // 4 + 1))
                        for k in range(HT):
                            if n == 0:
                                pe.wait_ge(y_ready, HT * h + (HT + k + 1))
                            s = slice((m * HT + k) * P, (m * HT + k + 1) * P)
                            for b in range(2):
                                last = mm3(pe, psum[:, 2 * (n % 2) + b, 0:TH], w_hi[:, p, s], w_lo[:, p, s],
                                           half(y_hi[:, k, :], b), half(y_lo[:, k, :], b), k == 0, k == HT - 1)
                        last.then_inc(used if m == 3 else wd_mm, 1)

        def act_up(act, ph):
            q0 = ph["q"]

            def tile(q, par, tt, use, split=True):
                first = isinstance(use, int) and use == 0
                if split:
                    act_hi(act, q + 1, PIECE, 1 - par, ph["off"])
                act.wait_ge(xm_acc, tt + 1)
                if first:
                    act.wait_ge(pad_set, 1)
                else:
                    act.wait_ge(gate_mm, tt - 1)
                    act.wait_ge(xm_out[par], use * 32)
                nc.scalar.activation(xm_pad[:, par, GAP:GAP + NP_], psum[:, 0, 0:NP_], ACT.Copy)
                nc.scalar.activation(xm_pad[:, par, 2 * GAP + NP_:2 * GAP + TH], psum[:, 0, NP_:TH], ACT.Copy)
                nc.scalar.activation(xm_pad[:, par, 2 * GAP + TH:2 * GAP + T], psum[:, 1, 0:TH], ACT.Copy).then_inc(xm_ready, 1)
                act.wait_ge(xm_ready, tt + 1)
                act.dma_start(xm_d[tt, :, 0:NP_], xm_pad[:, par, GAP:GAP + NP_]).then_inc(xm_out[par], 16)
                act.dma_start(xm_d[tt, :, NP_:T], xm_pad[:, par, 2 * GAP + NP_:2 * GAP + T]).then_inc(xm_out[par], 16)
                act.wait_ge(used, q + 1)
                if not first:
                    act.wait_ge(z_out[par], use * 16)
                nc.scalar.activation(two(z_s[:, par, :]), bank2(2), ACT.Silu).then_inc(freed, 1)
                act.wait_ge(freed, q + 1)
                act.dma_start(z_d[tt], z_s[:, par, :]).then_inc(z_out[par], 16)
                act.wait_ge(conv_ready, tt + 1)
                if not first:
                    act.wait_ge(xc_out[par], use * 16)
                for a, b, off in ((0, NP_, 0), (NP_, T, GAP)):
                    last = nc.scalar.activation(xc_s[:, par, a:b], conv[:, par, a + off:b + off], ACT.Silu,
                                                bias=conv_b[:, bass.ds(tt, 1)])
                last.then_inc(xc_ready, 1)
                act.wait_ge(xc_ready, tt + 1)
                act.dma_start(xc_d[tt], xc_s[:, par, :]).then_inc(xc_out[par], 16)

            tile(q0, 0, 0, 0)
            tile(q0 + 1, 1, 1, 0)
            with act.Fori(1, NT // 2 - 1) as i:
                tile(2 * i + q0, 0, 2 * i, i)
                tile(2 * i + (q0 + 1), 1, 2 * i + 1, i)
            tile(q0 + NT - 2, 0, NT - 2, NT // 2 - 1)
            tile(q0 + NT - 1, 1, NT - 1, NT // 2 - 1, split=False)

        def act_gates(act, ph):
            act.wait_ge(g_dve, 2)
            nc.scalar.activation(g_exp[:], g_abs[:], ACT.Exp, scale=-1.0).then_inc(g_act, 1)
            act.wait_ge(g_act, 1)
            nc.scalar.activation(g_ln[:], g_exp[:], ACT.Ln, bias=ones[:, 0:1]).then_inc(g_act, 1)
            act.wait_ge(g_dve, 14)
            nc.scalar.activation(rows[:, 2:4, :], s_row[:], ACT.Exp, scale=-1.0).then_inc(g_act, 1)

        def act_heads(act, ph):
            q0 = ph["q"]
            with act.Fori(0, NH) as h:
                act_hi(act, 2 * h + q0, PIECE, 0, ph["off"])
                act_hi(act, 2 * h + (q0 + 1), PIECE, 1, ph["off"])
                act.wait_ge(in_bc, 16 * h + 16)
                for d in range(2):
                    edge = NP_ - 1 if d == 0 else 0
                    last = nc.scalar.activation(w_tok[:, d:d + 1], a_col[:, 0, d, bass.ds(h, 1)], ACT.Exp,
                                                bias=bc[:, d, edge:edge + 1])
                last.then_inc(wt_ready, 1)
                for n in range(2 * HT):
                    act.wait_ge(qk_mm, 2 * HT * h + (n + 1))
                    dst = q_t if n < HT else k_t
                    nc.scalar.activation(two(dst[:, n % HT, :]), bank2(2 * (n % 2)), ACT.Copy).then_inc(qk_ev, 1)
                for n in range(10):
                    act.wait_ge(cn_mm, 10 * h + (n + 1))
                    if n >= 2:
                        act.wait_ge(cn_out[n % 2], 80 * h + 16 * (n // 2))
                    used_rows = P if n < 8 else 1
                    nc.scalar.activation(c_out[0:used_rows, n % 2, :], psum[0:used_rows, 6 + n % 2, :], ACT.Copy).then_inc(cn_ev, 1)
                    act.wait_ge(cn_ev, 10 * h + (n + 1))
                    if n < 8:
                        dst = t["new_c"][h, n // HT, (n % HT) * P:(n % HT + 1) * P, :]
                    else:
                        dst = t["new_n"][h, n - 8]
                    act.dma_start(dst, c_out[0:used_rows, n % 2, :]).then_inc(cn_out[n % 2], 16)
                act.wait_ge(arg_ready, h + 1)
                for j in range(4):
                    diag = slice(j * P, (j + 1) * P)
                    nc.scalar.activation(se_f[:, j, diag], se_f[:, j, diag], ACT.Exp)
                    nc.scalar.activation(se_b[:, j, diag], se_b[:, j, diag], ACT.Exp)
                    if j < 3:
                        nc.scalar.activation(se_f[:, j, (j + 1) * P:NL], bc[:, 0, NP_ + (j + 1) * P:T], ACT.Exp,
                                             bias=a_col[:, j + 1, 0, bass.ds(h, 1)])
                    if j > 0:
                        nc.scalar.activation(se_b[:, j, 0:j * P], bc[:, 1, NP_:NP_ + j * P], ACT.Exp,
                                             bias=a_col[:, j + 1, 1, bass.ds(h, 1)])
                nc.scalar.activation(se_p[:], se_p[:], ACT.Exp).then_inc(e_ready, 1)
                for d in range(2):
                    last = nc.scalar.activation(alpha[:, d, :], bc[:, d, NP_:T], ACT.Exp, bias=m0[:, bass.ds(h + 4 * d, 1)])
                last.then_inc(dec_ready, 1)
                for k in range(HT):
                    act.wait_ge(h_ready, HT * h + (k + 1))
                    if k == 0:
                        act.wait_ge(g_mm, 8 * h + 8)
                    if k >= 2:
                        act.wait_ge(hsq_used, HT * h + (k - 1))
                    nc.scalar.activation(h_sq[:, k % 2, :], h_t[:, k, :], ACT.Square).then_inc(hsq_ready, 1)
                act.wait_ge(hsq_used, HT * h + HT)
                nc.scalar.activation(two(h_root[:]), bank2(0), ACT.Sqrt, bias=eps_v[:], scale=1.0 / DH).then_inc(hroot_ready, 1)
                for k in range(HT):
                    act.wait_ge(y_sum, HT * h + (k + 1))
                    nc.scalar.activation(y_hi[:, k, :], h_t[:, k, :], ACT.Copy).then_inc(y_high, 1)

        def dve_up(dve, ph):
            q0 = ph["q"]
            nc.vector.memset(xm_pad[:], 0.0).then_inc(pad_set, 1)
            dve.wait_ge(in_wgr, 16)
            steps = 0
            for dst in range(2):
                parts = (0, 1) if dst == 0 else (2,)
                for d in range(2):
                    out = gate_w[:, dst, :, 8 * d:8 * d + 8]
                    for n, (s, o) in enumerate((s, o) for s in parts for o in range(4)):
                        a = wgr[:, s, d, :, 8 * o:8 * o + 8]
                        b = wq3[:, s, :, o:o + 1].to_broadcast([P, NT, 8])
                        tmp = gtmp[:, :, 0:8]
                        if n == 0:
                            last = nc.vector.tensor_tensor(out, a, b, ALU.mult).then_inc(gw_tmp, 1)
                        else:
                            nc.vector.tensor_tensor(tmp, a, b, ALU.mult).then_inc(gw_tmp, 1)
                            dve.wait_ge(gw_tmp, steps + 1)
                            last = nc.vector.tensor_tensor(out, out, tmp, ALU.add).then_inc(gw_tmp, 1)
                            steps += 1
                        steps += 1
                        dve.wait_ge(gw_tmp, steps)

            def tile(q, par, tt, split=True):
                if split:
                    dve_lo(dve, q + 1, PIECE, 1 - par, ph["off"])
                dve.wait_ge(xm_ready, tt + 1)
                if not isinstance(tt, int) or tt >= 2:
                    dve.wait_ge(xc_ready, tt - 1)
                for k in range(CONV):
                    src = xm_pad[:, par, k:k + TG]
                    w = conv_w[:, tt, k:k + 1]
                    if k == 0:
                        nc.vector.tensor_scalar(conv[:, par, :], src, w, None, ALU.mult).then_inc(conv_tap, 1)
                    else:
                        last = nc.vector.scalar_tensor_tensor(conv[:, par, :], src, w, conv[:, par, :], ALU.mult, ALU.add)
                        last.then_inc(conv_tap if k < CONV - 1 else conv_ready, 1)
                    if k < CONV - 1:
                        dve.wait_ge(conv_tap, (CONV - 1) * tt + (k + 1))

            tile(q0, 0, 0)
            tile(q0 + 1, 1, 1)
            with dve.Fori(1, NT // 2 - 1) as i:
                tile(2 * i + q0, 0, 2 * i)
                tile(2 * i + (q0 + 1), 1, 2 * i + 1)
            tile(q0 + NT - 2, 0, NT - 2)
            tile(q0 + NT - 1, 1, NT - 1, split=False)

        def dve_gates(dve, ph):
            dve.wait_ge(gate_mm, NT)
            dve.sem_inc(y_ready, HT)
            sums = psum[:, 4, 0:80].rearrange("p (j g) -> p j g", j=5)
            nc.vector.tensor_tensor(gt[:].rearrange("p (j d) g -> p j (d g)", d=2), sums,
                                    bgate[:].rearrange("p (a g) -> p a g", a=1).to_broadcast([P, 5, 16]), ALU.add).then_inc(g_dve, 1)
            dve.wait_ge(g_dve, 1)
            f = gt[:, :, 4:8]
            nc.vector.scalar_tensor_tensor(g_abs[:], f, -1.0, f, ALU.mult, ALU.max).then_inc(g_dve, 1)
            dve.wait_ge(g_act, 2)
            nc.vector.scalar_tensor_tensor(logf[:], f, 0.0, g_ln[:], ALU.min, ALU.subtract).then_inc(g_dve, 2)
            dve.wait_ge(g_pe, 1)
            sums = psum[:, 5, 0:40].rearrange("p (j g) -> p j g", g=4)
            nc.vector.tensor_tensor(a_col[:].rearrange("p j d g -> p (j d) g"), gt[:, :, 0:4], sums, ALU.subtract).then_inc(g_dve, 1)
            nc.vector.tensor_copy(b_col[:], sums).then_inc(g_dve, 1)
            dve.wait_ge(g_pe, 2)
            for d in range(2):
                for n, row in enumerate((a_row, b_row)):
                    nc.vector.tensor_copy(row[:, d, NP_:T], psum[0:4, 2 * n + d, :])
                    last = nc.vector.tensor_copy(row[:, d, 0:NP_], psum[0:4, 6, (2 * n + d) * P:(2 * n + d + 1) * P])
            last.then_inc(g_dve, 1)
            dve.wait_ge(g_dve, 7)
            for d in range(2):
                for a, b, start in ((0, NP_, 0.0), (NP_, T, m0row[:, d:d + 1])):
                    v = a_row[:, d, a:b] if d == 0 else a_row[:, d, b - 1:a - 1 if a else None:-1]
                    o = m_row[:, d, a:b] if d == 0 else m_row[:, d, b - 1:a - 1 if a else None:-1]
                    nc.vector.tensor_tensor_scan(o, v, v, start, ALU.max, ALU.max).then_inc(g_dve, 1)
            dve.wait_ge(g_dve, 11)
            nc.vector.tensor_scalar(rows[:, 0:2, :], m_row[:], -1.0, None, ALU.mult).then_inc(g_dve, 1)
            nc.vector.tensor_tensor(s_row[:], m_row[:], b_row[:], ALU.add).then_inc(g_dve, 2)
            dve.wait_ge(g_dve, 14)
            nc.vector.tensor_copy(m_new[:, 0:1], s_row[:, 0, NP_ - 1:NP_])
            nc.vector.tensor_copy(m_new[:, 1:2], s_row[:, 1, 0:1]).then_inc(g_dve, 1)

        def dve_heads(dve, ph):
            q0 = ph["q"]
            dve.wait_ge(rows_out, 16)
            dve.wait_ge(m_out, 16)
            with dve.Fori(0, NH) as h:
                for s in range(3):
                    a = wq3[:, s, bass.ds(HT * h, HT), :].rearrange("p t (a o) -> p t a o", a=1).to_broadcast([P, HT, 32, 4])
                    b = bdmask.rearrange("p (t n o) -> p t n o", t=1, o=1).to_broadcast([P, HT, 32, 4])
                    nc.vector.tensor_tensor(bd[:, s, :, :].rearrange("p t (n o) -> p t n o", o=4), a, b, ALU.mult)
                nb = n0[:, h, :].rearrange("p (k a) -> p k a", a=1).to_broadcast([P, 8, P])
                nc.vector.tensor_copy(n_bc[:], nb).then_inc(bd_ready, 1)
                dve_lo(dve, 2 * h + q0, PIECE, 0, ph["off"])
                dve_lo(dve, 2 * h + (q0 + 1), PIECE, 1, ph["off"])
                dve.wait_ge(kt_mm, h + 1)
                nc.vector.tensor_copy(k_tok[:], psum[:, 6, :]).then_inc(kt_ev, 1)
                for j in range(5):
                    dve.wait_ge(v_mm, 5 * h + (j + 1))
                    nc.vector.tensor_copy(v_tok[:, j, :], psum[:, 4 + j % 2, :]).then_inc(v_ev, 1)
                    if j == 0:
                        dve.wait_ge(wt_ready, h + 1)
                        dve.wait_ge(v_ev, 5 * h + 1)
                        for d in range(2):
                            last = nc.vector.tensor_scalar(vw[:, d, :], v_tok[:, 0, :], w_tok[:, d:d + 1], None, ALU.mult)
                        last.then_inc(vw_ready, 1)
                dve.wait_ge(in_bc, 16 * h + 16)
                dve.wait_ge(cn_out[0], 80 * h + 80)
                dve.wait_ge(cn_out[1], 80 * h + 80)
                for d, (se, bias) in enumerate(((se_f, bias_f), (se_b, bias_b))):
                    for j in range(4):
                        diag = slice(j * P, (j + 1) * P)
                        nc.vector.scalar_tensor_tensor(se[:, j, diag], bc[:, d, NP_ + j * P:NP_ + (j + 1) * P],
                                                       a_col[:, j + 1, d, bass.ds(h, 1)], bias, ALU.add, ALU.min)
                    last = nc.vector.scalar_tensor_tensor(se_p[:, d, :], bc[:, d, 0:P], a_col[:, 0, d, bass.ds(h, 1)],
                                                          bias, ALU.add, ALU.min)
                last.then_inc(arg_ready, 1)
                dve.wait_ge(s_mm, h + 1)
                dve.wait_ge(e_ready, h + 1)
                for j in range(4):
                    for se, a, b in ((se_f, j * P, NL), (se_b, 0, (j + 1) * P)):
                        nc.vector.scalar_tensor_tensor(se[:, j, a:b], psum[:, j, a:b], S_ML, se[:, j, a:b], ALU.mult, ALU.mult)
                for d in range(2):
                    last = nc.vector.scalar_tensor_tensor(se_p[:, d, :], psum[:, 6, 0:P], S_ML, se_p[:, d, :], ALU.mult, ALU.mult)
                last.then_inc(se_ready, 1)
                dve.wait_ge(nq_mm, h + 1)
                dve.wait_ge(dec_ready, h + 1)
                for d in range(2):
                    last = nc.vector.scalar_tensor_tensor(nq_d[:, d, :], psum[:, 4 + d, :], S_ML, alpha[:, d, :], ALU.mult, ALU.mult)
                last.then_inc(nq_ev, 1)
                dve.wait_ge(den_mm, h + 1)
                dve.wait_ge(nq_ev, h + 1)
                step = 5 * h
                for d in range(2):
                    nc.vector.tensor_tensor(rden[:, d, NP_:T], psum[:, 4 + d, :], nq_d[:, d, :], ALU.add)
                last = nc.vector.tensor_copy(rden[:, :, 0:NP_], psum[:, 6, 0:2 * P].rearrange("p (d n) -> p d n", d=2))
                last.then_inc(den_step, 1)
                dve.wait_ge(den_step, step + 1)
                nc.vector.scalar_tensor_tensor(rden[:], rden[:], -1.0, rden[:], ALU.mult, ALU.max).then_inc(den_step, 1)
                dve.wait_ge(den_step, step + 2)
                nc.vector.tensor_tensor(rden[:], rden[:], bc[:, 2:4, :], ALU.max).then_inc(den_step, 1)
                dve.wait_ge(den_step, step + 3)
                nc.vector.reciprocal(rden[:], rden[:]).then_inc(den_step, 1)
                dve.wait_ge(den_step, step + 4)
                nc.vector.scalar_tensor_tensor(alpha[:], alpha[:], S_ML, rden[:, :, NP_:T], ALU.mult, ALU.mult)
                for j in range(4):
                    nc.vector.tensor_tensor(se_f[:, j, j * P:NL], se_f[:, j, j * P:NL], rden[:, 0, NP_ + j * P:T], ALU.mult)
                    if j:
                        nc.vector.tensor_tensor(se_f[:, j, 0:j * P], se_b[:, j, 0:j * P], rden[:, 1, NP_:NP_ + j * P], ALU.mult)
                    diag = slice(j * P, (j + 1) * P)
                    nc.vector.tensor_tensor(se_b[:, j, diag], se_b[:, j, diag], rden[:, 1, NP_ + j * P:NP_ + (j + 1) * P], ALU.mult)
                nc.vector.tensor_tensor(se_p[:], se_p[:], rden[:, :, 0:NP_], ALU.mult).then_inc(den_step, 1)
                dve.wait_ge(den_step, step + 5)
                for j in range(4):
                    diag = slice(j * P, (j + 1) * P)
                    nc.vector.tensor_tensor(se_f[:, j, diag], se_f[:, j, diag], se_b[:, j, diag], ALU.add)
                nc.vector.tensor_tensor(se_p[:, 0, :], se_p[:, 0, :], se_p[:, 1, :], ALU.add).then_inc(w_ready, 1)
                for n in range(8):
                    v, d = n // 2, n % 2
                    dve.wait_ge(g_mm, 8 * h + (n + 1))
                    if v:
                        dve.wait_ge(h_step, HT * h + v)
                    if d == 0:
                        nc.vector.tensor_tensor(h_t[:, v, NP_:T], psum[:, n, :], alpha[:, 0, :], ALU.mult).then_inc(g_ev, 1)
                    else:
                        nc.vector.tensor_tensor(h_tmp[:], psum[:, n, :], alpha[:, 1, :], ALU.mult).then_inc(g_ev, 1)
                        dve.wait_ge(g_ev, 8 * h + (n + 1))
                        nc.vector.tensor_tensor(h_t[:, v, NP_:T], h_t[:, v, NP_:T], h_tmp[:], ALU.add).then_inc(h_step, 1)
                for v in range(HT):
                    dve.wait_ge(h_mm, HT * h + (v + 1))
                    dve.wait_ge(h_step, HT * h + (v + 1))
                    nc.vector.tensor_copy(h_t[:, v, 0:NP_], psum[:, 4 + v, 0:P])
                    nc.vector.tensor_tensor(h_t[:, v, NP_:T], h_t[:, v, NP_:T], psum[:, v, :], ALU.add).then_inc(h_ready, 1)
                dve.wait_ge(in_z, 16 * h + 16)
                dve.wait_ge(in_xc, 16 * h + 16)
                for k in range(HT):
                    nc.vector.scalar_tensor_tensor(xc_h[:, k, :], xc_h[:, k, :], skip[:, bass.ds(HT * h + k, 1)], zs_h[:, k, :],
                                                   ALU.mult, ALU.mult)
                    dve.wait_ge(hsq_ready, HT * h + (k + 1))
                    nc.vector.scalar_tensor_tensor(h_t[:, k, :], h_t[:, k, :], head_g[:, bass.ds(HT * h + k, 1)], zs_h[:, k, :],
                                                   ALU.mult, ALU.mult).then_inc(y_step, 1)
                dve.wait_ge(hroot_ready, h + 1)
                nc.vector.reciprocal(h_rstd[:], h_root[:]).then_inc(hrstd_ready, 1)
                dve.wait_ge(hrstd_ready, h + 1)
                dve.wait_ge(y_step, HT * h + HT)

                def y_low(k):
                    dve.wait_ge(y_high, HT * h + (k + 1))
                    nc.vector.tensor_tensor(y_lo[:, k, :], h_t[:, k, :], y_hi[:, k, :].bitcast(F32), ALU.subtract).then_inc(y_ready, 1)
                for k in range(HT):
                    nc.vector.tensor_tensor(h_t[:, k, :], h_t[:, k, :], h_rstd[:], ALU.mult).then_inc(y_norm, 1)
                    dve.wait_ge(y_norm, HT * h + (k + 1))
                    nc.vector.tensor_tensor(h_t[:, k, :], h_t[:, k, :], xc_h[:, k, :], ALU.add).then_inc(y_sum, 1)
                    if k:
                        y_low(k - 1)
                y_low(HT - 1)
                for n in range(8):
                    if n % 4 == 3:
                        dve.wait_ge(used, 2 * h + (q0 + n // 4 + 1))
                    else:
                        dve.wait_ge(wd_mm, 6 * h + (n - n // 4 + 1))
                    add_gated(dve, n, 2 * (n % 2)).then_inc(freed if n % 4 == 3 else wd_ev, 1)

        def pool_up(pool, ph):
            q0 = ph["q"]
            pool.wait_ge(freed, q0)
            pool.dma_start(wgr[:].rearrange("p a b c d -> p (a b c d)"), t["wgr"].rearrange("p a b c d -> p (a b c d)")).then_inc(in_wgr, 16)

        def pool_gates(pool, ph):
            pool.wait_ge(g_act, 3)
            pool.wait_ge(g_dve, 15)
            pool.dma_start(rows_d, rows[:]).then_inc(rows_out, 16)
            pool.dma_start(t["new_m"], m_new[:]).then_inc(m_out, 16)
            pool.wait_ge(rows_out, 16)
            pool.wait_ge(m_out, 16)

        def sp_heads(sp, ph, chunk_in_row):
            heads = lambda d: d.rearrange("(h k) p n -> h p k n", h=NH)
            for par in range(2):
                sp.wait_ge(xm_out[par], 16 * NT)
                sp.wait_ge(z_out[par], 8 * NT)
                sp.wait_ge(xc_out[par], 8 * NT)
            with sp.Fori(0, NH) as h:
                sp.wait_ge(y_ready, HT * h + HT)
                sp.dma_start(xc_h[:], heads(xc_d)[h]).then_inc(in_xc, 16)
                sp.dma_start(xm_h[:], heads(xm_d)[h]).then_inc(in_xm, 16)
                sp.wait_ge(rows_out, 16)
                sp.dma_start(bc[:], rows_d[h].rearrange("(a k) n -> a k n", a=1).to_broadcast([P, 4, T])).then_inc(in_bc, 16)
                chunk_in_row(h + ph["q"] // 2, h + (ph["q"] // 2 + ph["off"]), t["w_heads"][h], PIECE)
                sp.dma_start(c_t[:], t["c0"][h]).then_inc(in_ct, 16)
                sp.wait_ge(w_ready, h + 1)
                sp.dma_start(zs_h[:], heads(z_d)[h]).then_inc(in_z, 16)
            for par in range(2):
                sp.wait_ge(cn_out[par], 80 * NH)

        pe_mixers = {"up": pe_up, "gates": pe_gates, "heads": pe_heads}
        act_mixers = {"up": act_up, "gates": act_gates, "heads": act_heads}
        dve_mixers = {"up": dve_up, "gates": dve_gates, "heads": dve_heads}
        pool_phases = {"up": pool_up, "gates": pool_gates}

        def pool_mixers(pool):
            for ph in seq:
                if ph["kind"] in pool_phases:
                    pool_phases[ph["kind"]](pool, ph)

        (cq_ready, cache_in, in_ropes, kv_out, in_step_a, in_step_p, in_step_d, q_mm, q_ev, kn_mm, kn_ev) = (
            sem(n) for n in ("cq_ready", "cache_in", "in_ropes", "kv_out", "in_step_a", "in_step_p", "in_step_d",
                             "q_mm", "q_ev", "kn_mm", "kn_ev"))
        sq_in, sq_sum, sums_mm, cols_ev, inv_step, rot_mm, rope_step, roped = (
            sem("a_" + n) for n in ("sq_in", "sq_sum", "sums_mm", "cols_ev", "inv_step", "rot_mm", "rope_step", "roped"))
        dg_ready, rk_mm, keys_ready, q_copied = (sem("a_" + n) for n in ("dg_ready", "rk_mm", "keys_ready", "q_copied"))
        vh_mm, vh_ev, sc_mm, mx_ready, nb_ready, ex_ready, rs_ready, pn_ready, tr_mm, tr_ev, pv_mm, oh_ready, o_ready = (
            sem("a_" + n) for n in ("vh_mm", "vh_ev", "sc_mm", "mx_ready", "nb_ready", "ex_ready", "rs_ready", "pn_ready",
                                    "tr_mm", "tr_ev", "pv_mm", "oh_ready", "o_ready"))
        NC_ = TK // P + T // P
        KH = TK // 2
        S_AT = float(QK) ** -0.5
        mx, nb, sums, rsum = (soft[:, i:i + 2] for i in range(0, 8, 2))

        def wide(b):
            return psum[:, b:b + 2, 0:KH]

        def pe_attn_in(pe, ph):
            q = ph["q"]
            pe_in_piece(pe, q, 0, 4, 2 * ph["mod"], ph["mod"])
            def sums(k):
                pe.wait_ge(in_step_a, 1 + k if k < 2 else 4)
                pe.wait_ge(freed, q + 1 + k // 2)
                for b in range(2):
                    last = pe.matmul(psum[:, 6 * (k // 2) + b, 0:TH], ones[:], half(c_sq[:, k % 2, :], b),
                                     start=(k != 1), stop=(k != 0))
                last.then_inc(in_step_p, 1)

            def queries():
                sums(0)
                sums(1)
            pe_in_piece(pe, q + 1, 1, 4, 2 * ph["mod"], ph["mod"], between=queries)
            sums(2)

        Q_Q = next(ph["q"] for ph in plan() if ph["kind"] == "attn_q")

        def q_count(each, piece, n):
            return (each, n // 6 * 5 + n % 6 + 1) if n % 6 < 5 else (piece, Q_Q + n // 6 + 1)

        def pe_attn_q(pe, ph):
            pe.wait_ge(cq_ready, 1)
            for n in range(12):
                q, par, tile = ph["q"] + n // 6, n // 6, n % 6
                pe.wait_ge(lo_done, q + 1)
                if n == 3:
                    pe.wait_ge(in_step_a, 5)
                if n >= 4:
                    pe.wait_ge(*q_count(q_ev, freed, n - 4))
                for k in range(2):
                    s = slice((tile * 2 + k) * P, (tile * 2 + k + 1) * P)
                    for b in range(2):
                        last = mm3(pe, psum[:, 2 * (n % 4) + b, 0:TH], w_hi[:, par, s], w_lo[:, par, s],
                                   half(cq_hi[:, k, :], b), half(cq_lo[:, k, :], b), k == 0, k == 1)
                last.then_inc(q_mm if tile < 5 else used, 1)

        def pe_attn_kv(pe, ph):
            q = ph["q"]
            pe.wait_ge(freed, q)
            pe.wait_ge(in_step_d, 7)
            for n in range(AH):
                pe.wait_ge(lo_done, q + 1)
                if n >= 4:
                    pe.wait_ge(kn_ev, n - 3)
                s = slice(n * P, (n + 1) * P)
                for b in range(2):
                    e = slice(b * KH, (b + 1) * KH)
                    last = mm3(pe, psum[:, 2 * (n % 4) + b, 0:KH], w_hi[:, 0, s], w_lo[:, 0, s], ent_hi[:, e], ent_lo[:, e],
                               True, True)
                last.then_inc(kn_mm if n < AH - 1 else used, 1)

        def pe_attn(pe, ph):
            q = ph["q"]
            pe.wait_ge(in_step_a, 6)
            pe.wait_ge(freed, q - 1)
            for j in range(TK // P):
                pe.matmul(psum[:, 7, j:j + 1], kr_sq[:, j * P:(j + 1) * P], sel_a[:, 0:1], start=True, stop=True)
            pe.wait_ge(in_step_d, 8)
            pe.matmul(psum[:, 2, :], rot, k_rot[:, NP_:T], start=True, stop=True).then_inc(in_step_p, 1)
            pe.sem_inc(sums_mm, 2)

            def sums(hp):
                pe.wait_ge(cols_ev, hp + 1)
                for s in range(2):
                    pe.wait_ge(sq_in, 2 * hp + (s + 1))
                    for j in range(TK // P):
                        c = NC_ * s + j
                        pe.matmul(psum[:, 6, c:c + 1], sq_k[:, s, j * P:(j + 1) * P], ones[:, 0:1], start=True, stop=True)
                    pe.wait_ge(sq_sum, 2 * hp + (s + 1))
                    for j in range(T // P):
                        c = NC_ * s + TK // P + j
                        last = pe.matmul(psum[:, 6, c:c + 1], sq_q[:, s, j * P:(j + 1) * P], ones[:, 0:1], start=True, stop=True)
                    last.then_inc(sums_mm, 1)
                pe.wait_ge(rope_step, 2 * hp + 2)
                pe.matmul(psum[:, 4, :], rot, qr_raw[:, hp, NP_:T], start=True, stop=True).then_inc(rot_mm, 1)

            def factors(hp):
                for s in range(2):
                    pe.wait_ge(dg_ready, 2 * hp + (s + 1))
                    pe.wait_ge(keys_ready, 2 * hp + (s + 1))
                    for j in range(TK // P):
                        last = pe.matmul(psum[:, 2 * s + j // 3, (j % 3) * P:(j % 3 + 1) * P], ones[:], dg[:, s, j, :],
                                         start=True, stop=True)
                    last.then_inc(rk_mm, 1)
            sums(0)
            with pe.Fori(1, AH // 2) as hp:
                sums(hp)
                factors(hp - 1)
            factors(AH // 2 - 1)
            pe.wait_ge(lo_done, q)
            pe.wait_ge(keys_ready, AH + 3)
            with pe.Fori(0, AH // 2) as hp:
                for s in range(2):
                    h = 2 * hp + s

                    def scores(j):
                        if j == 0:
                            outs = [(psum[:, 2, 0:P], slice(0, P))]
                        else:
                            outs = [(psum[:, 2 * ((j + 1) % 2) + b, 0:TH], slice(P + b * TH, P + (b + 1) * TH)) for b in range(2)]
                            if j >= 2:
                                pe.wait_ge(ex_ready, 5 * h + j - 1)
                        for out, e in outs:
                            pe.matmul(out, qs[:, s, j * P:(j + 1) * P], kn_raw[:, h, e], start=True, stop=False)
                            last = pe.matmul(out, qrs[:, s, j * P:(j + 1) * P], krs[:, hp, e], start=False, stop=True)
                        last.then_inc(sc_mm, 1)

                    def turns(j):
                        pe.wait_ge(pn_ready, 5 * h + j + 1)
                        if j == 0:
                            pe.wait_ge(vh_ev, h + 1)
                        else:
                            pe.wait_ge(tr_ev, 5 * h + j)
                        for b in range(1 if j == 0 else 5):
                            last = pe.transpose(psum[:, 4 + b // 4, (b % 4) * P:(b % 4 + 1) * P],
                                                prob[:, j % 2, b * P:(b + 1) * P], ident)
                        last.then_inc(tr_mm, 1)

                    pe.wait_ge(q_copied, h + 1)
                    scores(0)
                    scores(1)
                    for j in range(TK // P):
                        e = slice(j * P, (j + 1) * P)
                        out = psum[:, 4 + j // 4, (j % 4) * P:(j % 4 + 1) * P]
                        col = bass.ds(h * P, P)
                        pe.matmul(out, ent_hi[:, e], w_hi[:, 1, col], start=True, stop=False)
                        pe.matmul(out, ent_lo[:, e], w_hi[:, 1, col], start=False, stop=False)
                        last = pe.matmul(out, ent_hi[:, e], w_lo[:, 1, col], start=False, stop=True)
                    last.then_inc(vh_mm, 1)
                    turns(0)
                    scores(2)
                    turns(1)
                    scores(3)
                    turns(2)
                    scores(4)
                    turns(3)
                    turns(4)
                    pe.wait_ge(tr_ev, 5 * h + 5)
                    pe.wait_ge(o_ready, h + 1)
                    pe.matmul(psum[:, 7, 0:P], v_h[:, 0, :], pt0[:], start=True, stop=True)
                    for b in range(5):
                        last = pe.matmul(psum[:, 6, :], v_h[:, b + 1, :], pt[:, b, :], start=(b == 0), stop=(b == 4))
                    last.then_inc(pv_mm, 1)
            pe.wait_ge(o_ready, AH + 1)
            pe.sem_inc(used, 1)

        def act_attn_in(act, ph):
            q = ph["q"]
            act_hi(act, q + 1, PIECE, 1, ph["off"])
            act.wait_ge(used, q + 1)
            nc.scalar.activation(two(cq[:, 0, :]), bank2(0), ACT.Copy)
            nc.scalar.activation(two(cq[:, 1, :]), bank2(2), ACT.Copy).then_inc(freed, 1)
            act_hi(act, q + 2, ph["next"], 0, ph["off"])
            act.wait_ge(freed, q + 1)
            nc.scalar.activation(c_sq[:, 0, :], cq[:, 0, :], ACT.Square).then_inc(in_step_a, 1)
            nc.scalar.activation(c_sq[:, 1, :], cq[:, 1, :], ACT.Square).then_inc(in_step_a, 1)
            act.wait_ge(in_step_p, 2)
            nc.scalar.activation(two(c_root[:, 0, :]), bank2(0), ACT.Sqrt, bias=eps_v[:], scale=1.0 / QL).then_inc(in_step_a, 1)
            act.wait_ge(used, q + 2)
            nc.scalar.activation(two(ent[:, 0:T]), bank2(4), ACT.Copy)
            nc.scalar.activation(two(kr[:, 0:T]), bank2(6), ACT.Copy).then_inc(freed, 1)
            act.wait_ge(freed, q + 2)
            nc.scalar.activation(c_sq[:, 0, :], ent[:, 0:T], ACT.Square).then_inc(in_step_a, 1)
            act.wait_ge(in_step_p, 3)
            nc.scalar.activation(two(c_root[:, 1, :]), bank2(6), ACT.Sqrt, bias=eps_v[:], scale=1.0 / KV).then_inc(in_step_a, 1)

        def act_attn_q(act, ph):
            q = ph["q"]
            act_hi(act, q + 1, 12 * P, 1, ph["off"])
            for n in range(12):
                act.wait_ge(*q_count(q_mm, used, n))
                p, tile = n // 6, n % 6
                dst = qn_raw[:, 4 * p + tile, :] if tile < 4 else qr_raw[:, 2 * p + tile - 4, :]
                if n == 4:
                    act.wait_ge(in_step_d, 5)
                nc.scalar.activation(two(dst), bank2(2 * (n % 4)), ACT.Copy).then_inc(q_ev if tile < 5 else freed, 1)
                if n == 5:
                    act_hi(act, q + 2, 8 * P, 0, ph["off"])

        def act_attn_kv(act, ph):
            q = ph["q"]
            act_hi(act, q + 1, 8 * P, 1, ph["off"])
            act_hi(act, q + 2, PIECE, 0, ph["off"])

        def act_attn(act, ph):
            act.wait_ge(in_step_d, 7)
            act.wait_ge(cache_in, 32)
            nc.scalar.activation(kr_sq[:], kr[:], ACT.Square).then_inc(in_step_a, 1)
            act.wait_ge(freed, ph["q"] - 1)
            act.wait_ge(in_step_d, 8)
            act.wait_ge(in_ropes, 16)

            def squares(hp):
                for s in range(2):
                    h = 2 * hp + s
                    r = slice(64 * s, 64 * s + 64)
                    act.wait_ge(sums_mm, h + 1)
                    nc.scalar.activation(sq_q[:, s, :], qn_raw[:, h, :], ACT.Square)
                    nc.scalar.activation(sq_r[r, s, :], qr_raw[r, hp, :], ACT.Square)
                    nc.scalar.activation(sq_k[:, s, :], kn_raw[:, h, :], ACT.Square).then_inc(sq_in, 1)

            def roots(hp):
                act.wait_ge(inv_step, 4 * hp + 1)
                pair = r_in[:, bass.ds(2 * NC_ * hp, 2 * NC_)]
                nc.scalar.activation(pair, pair, ACT.Sqrt, bias=eps_v[:], scale=1.0 / QK).then_inc(inv_step, 1)
            squares(0)
            with act.Fori(1, AH // 2) as hp:
                squares(hp)
                roots(hp - 1)
            roots(AH // 2 - 1)
            act.wait_ge(keys_ready, AH + 3)

            def copy_q(h, s):
                nc.scalar.activation(qs[:, s, :], qn_raw[:, h, :], ACT.Copy).then_inc(q_copied, 1)
            with act.Fori(0, AH // 2) as hp:
                for s in range(2):
                    r = slice(64 * s, 64 * s + 64)
                    nc.scalar.activation(qrs[r, s, :], qr_raw[r, hp, :], ACT.Copy)
                copy_q(2 * hp, 0)
                for s in range(2):
                    h = 2 * hp + s

                    def ex(j):
                        act.wait_ge(nb_ready, 5 * h + j + 1)
                        if j >= 2:
                            act.wait_ge(tr_mm, 5 * h + j - 1)
                        k = slice(j % 2, j % 2 + 1)
                        src = psum[:, 2, 0:P] if j == 0 else bank2(2 * ((j + 1) % 2))
                        dst = prob[:, 0, 0:P] if j == 0 else two(prob[:, j % 2, :])
                        nc.scalar.activation(dst, src, ACT.Exp, bias=nb[:, k], scale=r_s[:, bass.ds(NC_ * h + TK // P + j, 1)],
                                             accum_out=sums[:, k]).then_inc(ex_ready, 1)

                    def turned(j):
                        act.wait_ge(tr_mm, 5 * h + j + 1)
                        if j == 0:
                            nc.scalar.activation(pt0[:], psum[:, 4, 0:P], ACT.Copy).then_inc(tr_ev, 1)
                        else:
                            c = slice((j - 1) * P, j * P)
                            nc.scalar.activation(pt[:, 0:4, c], psum[:, 4, :].rearrange("p (b n) -> p b n", b=4), ACT.Copy)
                            nc.scalar.activation(pt[:, 4, c], psum[:, 5, 0:P], ACT.Copy).then_inc(tr_ev, 1)

                    ex(0)
                    act.wait_ge(vh_mm, h + 1)
                    nc.scalar.activation(v_h[:, 0:4, :], psum[:, 4, :].rearrange("p (j n) -> p j n", j=4), ACT.Copy)
                    nc.scalar.activation(v_h[:, 4:6, :], psum[:, 5, 0:2 * P].rearrange("p (j n) -> p j n", j=2), ACT.Copy).then_inc(vh_ev, 1)
                    ex(1)
                    turned(0)
                    ex(2)
                    turned(1)
                    ex(3)
                    turned(2)
                    ex(4)
                    turned(3)
                    if s == 0:
                        copy_q(h + 1, 1)
                    turned(4)

        def dve_attn_in(dve, ph):
            q = ph["q"]
            dve_lo(dve, q + 1, PIECE, 1, ph["off"])
            dve_lo(dve, q + 2, ph["next"], 0, ph["off"])
            dve.wait_ge(in_step_a, 3)
            nc.vector.reciprocal(c_rstd[:, 0, :], c_root[:, 0, :]).then_inc(in_step_d, 1)
            dve.wait_ge(in_step_d, 1)
            for k in range(2):
                last = nc.vector.scalar_tensor_tensor(cq[:, k, :], cq[:, k, :], attn_g[:, 4 + k:5 + k], c_rstd[:, 0, :], ALU.mult, ALU.mult)
            last.then_inc(in_step_d, 1)
            dve.wait_ge(in_step_d, 2)
            nc.vector.tensor_copy(cq_hi[:], cq[:]).then_inc(in_step_d, 1)
            dve.wait_ge(in_step_d, 3)
            nc.vector.tensor_tensor(cq_lo[:], cq[:], cq_hi[:].bitcast(F32), ALU.subtract).then_inc(cq_ready, 1)
            dve.wait_ge(in_step_a, 5)
            nc.vector.reciprocal(c_rstd[:, 1, :], c_root[:, 1, :]).then_inc(in_step_d, 1)
            dve.wait_ge(in_step_d, 4)
            dve.wait_ge(cache_in, 32)
            nc.vector.scalar_tensor_tensor(ent[:, 0:T], ent[:, 0:T], attn_g[:, 6:7], c_rstd[:, 1, :], ALU.mult, ALU.mult).then_inc(in_step_d, 1)
            dve.wait_ge(in_step_d, 5)
            nc.vector.tensor_copy(ent_hi[:], ent[:]).then_inc(in_step_d, 1)
            dve.wait_ge(in_step_d, 6)
            nc.vector.tensor_tensor(ent_lo[:], ent[:], ent_hi[:].bitcast(F32), ALU.subtract).then_inc(in_step_d, 1)

        def dve_attn_q(dve, ph):
            q = ph["q"]
            dve_lo(dve, q + 1, 12 * P, 1, ph["off"])
            dve_lo(dve, q + 2, 8 * P, 0, ph["off"])

        def dve_attn_kv(dve, ph):
            q = ph["q"]
            dve_lo(dve, q + 1, 8 * P, 1, ph["off"])
            for n in range(AH):
                dve.wait_ge(kn_mm if n < AH - 1 else used, n + 1 if n < AH - 1 else q + 1)
                nc.vector.tensor_copy(kn_raw[:, n, :].rearrange("p (b n) -> p b n", b=2), wide(2 * (n % 4))).then_inc(
                    kn_ev if n < AH - 1 else freed, 1)
            dve_lo(dve, q + 2, PIECE, 0, ph["off"])

        def dve_attn(dve, ph):
            dve.wait_ge(cache_in, 32)
            nc.vector.tensor_scalar(k_rot[:], kr[:], attn_g[:, 3:4], None, ALU.mult).then_inc(in_step_d, 1)
            dve.wait_ge(in_step_p, 4)
            dve.wait_ge(in_ropes, 16)
            nc.vector.tensor_scalar(r_kr[:], psum[:, 7, 0:TK // P], 1.0, None, ALU.mult).then_inc(in_step_d, 1)
            nc.vector.tensor_tensor(rope_t[:], psum[:, 2, :], ropes[:, 1, :], ALU.mult).then_inc(in_step_d, 1)
            nc.vector.tensor_tensor(k_rot[:, NP_:T], k_rot[:, NP_:T], ropes[:, 0, :], ALU.mult).then_inc(in_step_d, 1)
            dve.wait_ge(in_step_d, 11)
            nc.vector.tensor_tensor(k_rot[:, NP_:T], k_rot[:, NP_:T], rope_t[:], ALU.add).then_inc(o_ready, 1)
            dve.wait_ge(o_ready, 1)
            nc.vector.tensor_tensor(g_both[:], attn_g[:, 0:1], attn_g[:, 2:3], ALU.mult).then_inc(cols_ev, 1)
            dve.sem_inc(rope_step, 1)
            dve.sem_inc(keys_ready, 2)
            pair_of = lambda buf, hp: buf[:, bass.ds(2 * NC_ * hp, 2 * NC_)]
            halves = lambda a: a.rearrange("p (b n) -> p b n", b=2)

            def gather(hp):
                for s in range(2):
                    r = slice(64 * s, 64 * s + 64)
                    dve.wait_ge(sq_in, 2 * hp + (s + 1))
                    nc.vector.tensor_tensor(sq_q[r, s, :], sq_q[r, s, :], sq_r[r, s, :], ALU.add).then_inc(sq_sum, 1)
                nc.vector.tensor_scalar(qr_raw[:, hp, :], qr_raw[:, hp, :], attn_g[:, 1:2], None, ALU.mult).then_inc(rope_step, 1)

            def columns(hp):
                dve.wait_ge(sums_mm, 2 * hp + 4)
                nc.vector.tensor_scalar(pair_of(r_in, hp), psum[:, 6, 0:2 * NC_], 1.0, None, ALU.mult).then_inc(cols_ev, 1)
                dve.wait_ge(cols_ev, hp + 2)
                k_cols = pair_of(r_in, hp).rearrange("p (s c) -> p s c", s=2)[:, :, 0:TK // P]
                shared = r_kr[:].rearrange("p (a c) -> p a c", a=1).to_broadcast([P, 2, TK // P])
                nc.vector.tensor_tensor(k_cols, k_cols, shared, ALU.add).then_inc(inv_step, 1)
                lat_q = qr_raw[:, hp, NP_:T]
                dve.wait_ge(rot_mm, hp + 1)
                nc.vector.tensor_tensor(lat_q, lat_q, ropes[:, 0, :], ALU.mult)
                nc.vector.tensor_tensor(rope_t[:], psum[:, 4, :], ropes[:, 1, :], ALU.mult).then_inc(rope_step, 1)
                dve.wait_ge(rope_step, 2 * hp + 3)
                nc.vector.tensor_tensor(lat_q, lat_q, rope_t[:], ALU.add).then_inc(roped, 1)
                dve.wait_ge(roped, hp + 1)

            def invert(hp):
                dve.wait_ge(inv_step, 4 * hp + 2)
                nc.vector.reciprocal(pair_of(r_out, hp), pair_of(r_in, hp)).then_inc(inv_step, 1)
                dve.wait_ge(inv_step, 4 * hp + 3)
                nc.vector.tensor_scalar(pair_of(r_s, hp), pair_of(r_out, hp), S_AT, None, ALU.mult)
                nc.vector.tensor_scalar(pair_of(r_n, hp), pair_of(r_out, hp), -S_AT, None, ALU.mult).then_inc(inv_step, 1)
                for s in range(2):
                    col = r_out[:, bass.ds(2 * NC_ * hp + NC_ * s, TK // P)].rearrange("p (c a) -> p c a", a=1)
                    dve.wait_ge(keys_ready, 2 * hp + (s + 1))
                    nc.vector.tensor_tensor(dg[:, s, :, :], ident.rearrange("p (a n) -> p a n", a=1).to_broadcast([P, TK // P, P]),
                                            col.to_broadcast([P, TK // P, P]), ALU.mult).then_inc(dg_ready, 1)

            def keys(hp):
                for s in range(2):
                    h = 2 * hp + s
                    r = slice(64 * s, 64 * s + 64)
                    dve.wait_ge(rk_mm, h + 1)
                    nc.vector.scalar_tensor_tensor(halves(kn_raw[:, h, :]), halves(kn_raw[:, h, :]), g_both[:], wide(2 * s),
                                                   ALU.mult, ALU.mult)
                    nc.vector.tensor_tensor(halves(krs[r, hp, :]), halves(k_rot[r, :]), psum[r, 2 * s:2 * s + 2, 0:KH],
                                            ALU.mult).then_inc(keys_ready, 1)
            gather(0)
            columns(0)
            with dve.Fori(1, AH // 2) as hp:
                gather(hp)
                invert(hp - 1)
                columns(hp)
                keys(hp - 1)
            invert(AH // 2 - 1)
            keys(AH // 2 - 1)
            dve.wait_ge(rk_mm, AH)
            nc.vector.memset(qrs[64:P, 0, :], 0.0)
            nc.vector.memset(qrs[0:64, 1, :], 0.0).then_inc(keys_ready, 1)
            with dve.Fori(0, AH // 2) as hp:
                for s in range(2):
                    h = 2 * hp + s

                    def top(j):
                        k = 5 * h + j + 1
                        dve.wait_ge(sc_mm, k)
                        if j >= 2:
                            dve.wait_ge(ex_ready, k - 2)
                        src = psum[:, 2, 0:P] if j == 0 else bank2(2 * ((j + 1) % 2))
                        m = mx[:, j % 2:j % 2 + 1]
                        nc.vector.tensor_reduce(m, src, AX_X if j == 0 else mybir.AxisListType.XY, ALU.max).then_inc(mx_ready, 1)
                        dve.wait_ge(mx_ready, k)
                        nc.vector.tensor_scalar(nb[:, j % 2:j % 2 + 1], m, r_n[:, bass.ds(NC_ * h + TK // P + j, 1)], None,
                                                ALU.mult).then_inc(nb_ready, 1)

                    def normal(j):
                        k = 5 * h + j + 1
                        dve.wait_ge(ex_ready, k)
                        nc.vector.reciprocal(rsum[:, j % 2:j % 2 + 1], sums[:, j % 2:j % 2 + 1]).then_inc(rs_ready, 1)
                        dve.wait_ge(rs_ready, k)
                        p = prob[:, j % 2, 0:P if j == 0 else T]
                        nc.vector.tensor_scalar(p, p, rsum[:, j % 2:j % 2 + 1], None, ALU.mult).then_inc(pn_ready, 1)

                    top(0)
                    top(1)
                    normal(0)
                    normal(1)
                    top(2)
                    normal(2)
                    top(3)
                    normal(3)
                    top(4)
                    normal(4)
                    dve.wait_ge(pv_mm, h + 1)
                    for a, b, src in ((0, NP_, psum[:, 7, 0:P]), (NP_, T, psum[:, 6, :])):
                        last = nc.vector.tensor_scalar(o_hi[:, h, a:b], src, 1.0, None, ALU.mult)
                    last.then_inc(oh_ready, 1)
                    dve.wait_ge(oh_ready, h + 1)
                    for a, b, src in ((0, NP_, psum[:, 7, 0:P]), (NP_, T, psum[:, 6, :])):
                        last = nc.vector.tensor_tensor(o_lo[:, h, a:b], src, o_hi[:, h, a:b].bitcast(F32), ALU.subtract)
                    last.then_inc(o_ready, 1)
            dve.wait_ge(o_ready, AH + 1)
            dve.sem_inc(freed, 1)

        def pe_attn_out(pe, ph):
            for p in range(4):
                pe_out_piece(pe, ph["q"] + p, p % 2, AH, 2, o_hi, o_lo, (o_ready, 1))

        def act_attn_out(act, ph):
            for p in range(4):
                if p < 3:
                    act_hi(act, ph["q"] + p + 1, PIECE, (p + 1) % 2, ph["off"])
                act.wait_ge(freed, ph["q"] + p + 1)
                act_square(act, ph["stats"], 2 * p)
                act_square(act, ph["stats"], 2 * p + 1)

        def dve_attn_out(dve, ph):
            clear_acc(dve, ph["stats"])
            for p in range(4):
                if p < 3:
                    dve_lo(dve, ph["q"] + p + 1, PIECE, (p + 1) % 2, ph["off"])
                dve.wait_ge(used, ph["q"] + p + 1)
                add_gated(dve, 2 * p, 4 * (p % 2))
                add_gated(dve, 2 * p + 1, 4 * (p % 2) + 2).then_inc(freed, 1)
                add_square(dve, ph["stats"], 2 * p)
                add_square(dve, ph["stats"], 2 * p + 1)

        def pool_attn_in(pool, ph):
            pool.wait_ge(freed, ph["q"])
            pool.dma_start(ent[:, T:TK], t["cache_c"]).then_inc(cache_in, 16)
            pool.dma_start(kr[:, T:TK], t["cache_r"]).then_inc(cache_in, 16)
            pool.wait_ge(in_step_d, 5)
            pool.dma_start(t["new_kv"][0:KV], ent[:, 0:NP_]).then_inc(kv_out, 16)
            pool.dma_start(t["new_kv"][KV:KV + 64], kr[0:64, 0:NP_]).then_inc(kv_out, 16)
            pool.wait_ge(kv_out, 32)
            pool.wait_ge(freed, ph['q'] + 4)
            pool.dma_start(ropes[:], t["ropes"]).then_inc(in_ropes, 16)

        for name, pe_f, act_f, dve_f in (
                ("attn_in", pe_attn_in, act_attn_in, dve_attn_in), ("attn_q", pe_attn_q, act_attn_q, dve_attn_q),
                ("attn_kv", pe_attn_kv, act_attn_kv, dve_attn_kv), ("attn", pe_attn, act_attn, dve_attn),
                ("attn_out", pe_attn_out, act_attn_out, dve_attn_out)):
            pe_mixers[name], act_mixers[name], dve_mixers[name] = pe_f, act_f, dve_f
        pool_phases["attn_in"] = pool_attn_in

        block = ctx.enter_context(nc.Block())

        @block.sync
        def _(sp):
            def slot_free(c):
                if c >= 2:
                    kind, value = leaves[c - 2]
                    sp.wait_ge(lo_done if kind == "w" else mod_used, value)

            def chunk_at(q, c, src, columns):
                slot_free(c)
                if q:
                    sp.wait_ge(raw_in, 8 * q)
                sp.dma_start(raw[:, c % 2, :, 0:columns], src).then_inc(raw_in, 16)

            def chunk_in_row(n, c, src, columns):
                sp.wait_ge(raw_in, 16 * n)
                sp.wait_ge(lo_done, 2 * n - 2)
                sp.dma_start(raw[:, c % 2, :, 0:columns], src).then_inc(raw_in, 16)

            def mod_chunk_at(m, c):
                slot_free(c)
                if m:
                    sp.wait_ge(mod_in, 16 * m)
                sp.dma_start(raw[:, c % 2], t["w_mod"][m]).then_inc(mod_in, 16)

            for ph in seq:
                kind, q, c, n = ph["kind"], ph["q"], ph["c"], ph["n"] // 2
                if kind == "heads":
                    sp_heads(sp, ph, chunk_in_row)
                elif ph["mods"] and n:
                    w, m = t["w_in"][ph["f"]], ph["mod"]
                    chunk_at(q, c, w[ph["pair"]], PIECE)
                    mod_chunk_at(m, c + 1)
                    with sp.Fori(1, n) as i:
                        sp.wait_ge(lo_done, 2 * i + q)
                        sp.dma_start(raw[:, c % 2], w[i + ph["pair"]]).then_inc(raw_in, 16)
                        sp.wait_ge(mod_used, 2 * i + 2 * m)
                        sp.dma_start(raw[:, (c + 1) % 2], t["w_mod"][i + m]).then_inc(mod_in, 16)
                elif ph["mods"]:
                    for i in range(ph["mods"]):
                        mod_chunk_at(i, i)
                elif n:
                    if kind == "in":
                        w, first, columns = t["w_in"][ph["f"]], ph["pair"], PIECE
                    elif kind == "out":
                        w, first, columns = t[f"w_out{ph['half']}"][ph["f"]], 0, ph["tiles"] * P
                    else:
                        w, first, columns = t["w_" + kind], 0, size_of(ph)
                    for i in range(min(n, 2)):
                        chunk_at(q + 2 * i, c + i, w[first + i], columns)
                    if n > 2:
                        with sp.Fori(2, n) as i:
                            chunk_in_row(i + q // 2, i + c, w[i + first], columns)

        @block.gpsimd
        def _(pool):
            for dst, src in ((cst, "cst"), (bmod, "bmod"), (norm_g, "norm_g")):
                pool.dma_start(dst[:], t[src]).then_inc(in_bmod, 16)
            pool.wait_ge(mod_in, 16)
            for k in range(KD):
                pool.dma_start(x[:, k, :], t["x"][k]).then_inc(in_x, 16)
            for dst, src in ((mlp, "mlp"), (wq3, "wq3"), (bgate, "bgate"), (m0, "m0"),
                             (n0, "n0"), (m0row, "m0row"), (attn_g, "attn_g")):
                pool.dma_start(dst[:], t[src]).then_inc(in_cst, 16)
            pool_mixers(pool)
            for k in range(KD):
                pool.wait_ge(freed, seq[-1]["q"] + seq[-1]["n"] - KD + k + 1)
                pool.dma_start(t["y"][k], x[:, k, :]).then_inc(y_out, 16)
            pool.wait_ge(y_out, 16 * KD)

        def piece_ready(pe, q):
            pe.wait_ge(lo_done, q + 1)
            if not isinstance(q, int) or q >= 2:
                pe.wait_ge(freed, q - 1)

        def pe_mod(pe, m, slot, hi, bank):
            pe.wait_ge(mod_lo_done, m + 1)
            low = raw_lo[:, slot[0], slot[1], :]
            for k in range(KD):
                s = slice(k * 2 * P, (k + 1) * 2 * P)
                pe.matmul(psum[0:4, bank, 0:2 * P], c4[:, k, :], hi[:, s], start=(k == 0), stop=False)
                last = pe.matmul(psum[0:4, bank, 0:2 * P], c4[:, k, :], low[:, s], start=False, stop=(k == KD - 1))
            last.then_inc(mod_used, 1)

        def pe_mod_turn(pe, c):
            pe.wait_ge(mod_copied, 2 * c + 2)
            for n in range(2):
                last = pe.matmul(psum[:, 2, 4 * n:4 * n + 4], mod_rows[:, n * P:(n + 1) * P], sum_parts,
                                 start=True, stop=True)
            last.then_inc(mod_turned, 1)

        def pe_in_piece(pe, q, par, norm_at, copied, turned, between=None):
            piece_ready(pe, q)
            for step in range(KD + 4):
                if step == 6 and between is not None:
                    between()
                for ab, k in ((0, step), (1, step - 4)):
                    if not 0 <= k < KD:
                        continue
                    if ab == 0:
                        pe.wait_ge(xn_ready, KD * norm_at + k + 1)
                    elif k == 0:
                        pe.wait_ge(mod_copied, copied)
                        if par == 0:
                            pe.wait_ge(mod_freed, turned)
                    s = slice((k * 2 + ab) * P, (k * 2 + ab + 1) * P)
                    for n in range(2):
                        last = mm3(pe, psum[:, 4 * par + 2 * ab + n, 0:TH], w_hi[:, par, s], w_lo[:, par, s],
                                   half(xn_hi[:, k, :], n), half(xn_lo[:, k, :], n), k == 0, k == KD - 1)
            last.then_inc(used, 1)

        def pe_out_piece(pe, q, par, kt, outs, r_hi, r_lo, ready=None):
            piece_ready(pe, q)
            for m in range(outs):
                for k in range(kt):
                    if ready is not None and m == 0:
                        pe.wait_ge(ready[0], ready[1] + k + 1)
                    s = slice((m * kt + k) * P, (m * kt + k + 1) * P)
                    for n in range(2):
                        last = mm3(pe, psum[:, 4 * par + 2 * m + n, 0:TH], w_hi[:, par, s], w_lo[:, par, s],
                                   half(r_hi[:, k, :], n), half(r_lo[:, k, :], n), k == 0, k == kt - 1)
            last.then_inc(used, 1)

        @block.tensor
        def _(pe):
            for ph in seq:
                kind, q, c = ph["kind"], ph["q"], ph["c"]
                if kind == "mod":
                    pe.wait_ge(c_ready, 1)
                    pe.wait_ge(in_bmod, 48)
                    pe.wait_ge(rows_set, 1)
                    for m in range(2 * ph["mods"]):
                        if m >= 2:
                            pe.wait_ge(mod_copied, m - 1)
                        pe_mod(pe, m, (m // 2 % 2, m % 2), w_hi[:, m % 2, :], 3 + 4 * (m % 2))
                        if m % 2:
                            if m >= 2:
                                pe.wait_ge(mod_freed, m // 2)
                            pe_mod_turn(pe, m // 2)
                elif kind == "norm":
                    pe.wait_ge(ones_set, 1)
                    pe.wait_ge(freed, q) if q else None
                    pe.wait_ge(acc_ready, KD * ph["at"] + KD)
                    for n in range(2):
                        last = pe.matmul(psum[:, n, 0:TH], ones[:], half(acc, n), start=True, stop=True)
                    last.then_inc(ss_ready, 1)
                elif kind == "in":
                    mods = ph["mods"]

                    def body(i):
                        at_ = i + ph["mod"]
                        for par in range(2):
                            if mods:
                                if not isinstance(i, int) or q + par >= 2:
                                    pe.wait_ge(freed, 2 * i + (q + par - 1))
                                pe_mod(pe, 2 * i + (2 * ph["mod"] + par), ((c + 1) % 2, par), mod_hi, 3 + 4 * par)
                            pe_in_piece(pe, 2 * i + (q + par), par, ph["norm"],
                                        2 * i + (2 * ph["mod"] + par + 1) if mods else 2 * ph["mod"],
                                        at_ if mods else ph["mod"])
                        if mods:
                            pe.wait_ge(freed, 2 * i + (q + 1))
                            pe_mod_turn(pe, at_)
                    lead = 0 if q else 1
                    if lead:
                        body(0)
                    with pe.Fori(lead, ph["n"] // 2) as i:
                        body(i)
                elif kind == "out":
                    with pe.Fori(0, KD // 2) as i:
                        for par in range(2):
                            pe_out_piece(pe, 2 * i + (q + par), par, ph["tiles"], 1, hid_hi, hid_lo,
                                         (hid_ready, ph["hid"] - ph["tiles"]))
                else:
                    pe_mixers[kind](pe, ph)

        def act_hi(act, q, size, par, off=None, chunk=None):
            if chunk is None:
                chunk = (q - par) // 2 + off
            act.wait_ge(raw_in, 8 * (q - par) + 16)
            if not isinstance(q, int) or q >= 2:
                act.wait_ge(used, q - 1)
            nc.scalar.activation(w_hi[:, par, 0:size], raw[:, chunk % 2, par, 0:size], ACT.Copy).then_inc(hi_done, 1)

        def act_mod(act, m, slot, hi):
            act.wait_ge(mod_in, 8 * (m - slot[1]) + 16)
            nc.scalar.activation(hi, raw[:, slot[0], slot[1], :], ACT.Copy).then_inc(mod_hi_done, 1)

        def chunk_of(ph, i):
            return 2 * i + ph["c"] if ph["mods"] else i + ph["c"]

        def act_square(act, at_, k):
            n = k + KD * at_
            if not isinstance(n, int) or n >= 2:
                act.wait_ge(acc_ready, k + (KD * at_ - 1))
            nc.scalar.activation(sq[:, k % 2, :], x[:, k, :], ACT.Square).then_inc(sq_ready, 1)

        @block.scalar
        def _(act):
            act.dma_start(cvec[:], t["cvec"]).then_inc(in_c, 16)
            act.wait_ge(in_c, 16)
            nc.scalar.activation(csilu[:], cvec[:], ACT.Silu).then_inc(c_act, 1)
            act.wait_ge(c_act, 1)
            nc.scalar.activation(c4[:, :, 0:2], csilu[:], ACT.Copy).then_inc(c_act, 1)

            def silu_evac(q, par):
                act.wait_ge(used, q + 1)
                nc.scalar.activation(two(silu_s[:, par, :]), bank2(4 * par), ACT.Silu).then_inc(silu_ready, 1)

            for ph in seq:
                kind, q, nxt = ph["kind"], ph["q"], ph["next"]
                if kind == "mod":
                    for m in range(2 * ph["mods"]):
                        if m >= 2:
                            act.wait_ge(mod_used, m - 1)
                        act_mod(act, m, (m // 2 % 2, m % 2), w_hi[:, m % 2, :])
                        if m == 2:
                            act.wait_ge(in_x, 16 * KD)
                        if m >= 2:
                            act_square(act, 0, m - 2)
                elif kind == "norm":
                    n0_ = KD * ph["at"]
                    if not ph["early"]:
                        act.wait_ge(freed, q)
                        for k in range(KD):
                            act_square(act, ph["at"], k)
                    if nxt:
                        if q == 0:
                            act.wait_ge(mod_used, 2 * N_FIRST)
                        act_hi(act, q, nxt, 0, chunk=ph["next_c"])
                        if ph["next_mod"] is not None:
                            act.wait_ge(mod_used, 2 * ph["next_mod"])
                            act_mod(act, 2 * ph["next_mod"], ((ph["next_c"] + 1) % 2, 0), mod_hi[:])
                    act.wait_ge(eps_set, 1)
                    act.wait_ge(ss_ready, ph["at"] + 1)
                    nc.scalar.activation(two(root[:]), bank2(0), ACT.Sqrt, bias=eps_v[:],
                                         scale=1.0 / D).then_inc(root_ready, 1)
                    shift = ph["sub"] * 24
                    for k in range(KD):
                        act.wait_ge(nrm_ready, n0_ + k + 1)
                        for a, b, g in SEG:
                            last = nc.scalar.activation(xn_hi[:, k, a:b], nrm[:, k % 2, a:b], ACT.Identity,
                                                        bias=mod[:, shift + k, g:g + 1])
                        last.then_inc(xhi_ready, 1)
                elif kind == "in":
                    pairs, c, mods = ph["n"] // 2, ph["c"], ph["mods"]
                    slot = (c + 1) % 2

                    def mod_piece(i, par):
                        m = 2 * i + (2 * ph["mod"] + par)
                        act.wait_ge(mod_used, m)
                        act_mod(act, m, (slot, par), mod_hi[:])

                    def body(i, final):
                        act_hi(act, 2 * i + (q + 1), PIECE, 1, chunk=chunk_of(ph, i))
                        if mods:
                            mod_piece(i, 1)
                        silu_evac(2 * i + q, 0)
                        size = nxt if final else PIECE
                        if size:
                            act_hi(act, 2 * i + (q + 2), size, 0, chunk=ph["next_c"] if final else chunk_of(ph, i + 1))
                        if mods and not final:
                            mod_piece(i + 1, 0)
                        silu_evac(2 * i + (q + 1), 1)
                    if mods and not ph["after_norm"]:
                        mod_piece(0, 0)
                    with act.Fori(0, pairs - 1) as i:
                        body(i, False)
                    body(pairs - 1, True)
                elif kind == "out":
                    size, stats = size_of(ph), ph["stats"]

                    def square(i, par):
                        if stats is not None:
                            act.wait_ge(freed, 2 * i + (q + par + 1))
                            act_square(act, stats, 2 * i + par)

                    def body(i, final):
                        act_hi(act, 2 * i + (q + 1), size, 1, chunk=i + ph["c"])
                        square(i, 0)
                        if not final or nxt:
                            act_hi(act, 2 * i + (q + 2), nxt if final else size, 0,
                                   chunk=ph["next_c"] if final else i + (ph["c"] + 1))
                        square(i, 1)
                    with act.Fori(0, KD // 2 - 1) as i:
                        body(i, False)
                    body(KD // 2 - 1, True)
                elif kind != "mod":
                    act_mixers[kind](act, ph)

        def dve_lo(dve, q, size, par, off=None, chunk=None):
            if chunk is None:
                chunk = (q - par) // 2 + off
            dve.wait_ge(hi_done, q + 1)
            nc.vector.tensor_tensor(w_lo[:, par, 0:size], raw[:, chunk % 2, par, 0:size],
                                    w_hi[:, par, 0:size].bitcast(F32), ALU.subtract).then_inc(lo_done, 1)

        def add_gated(dve, m, bank):
            for b, a0, a1, g in PARTS:
                tok = slice(b * TH + a0, b * TH + a1)
                last = nc.vector.scalar_tensor_tensor(x[:, m, tok], psum[:, bank + b, a0:a1],
                                                      gate_v[:, m, g:g + 1], x[:, m, tok], ALU.mult, ALU.add)
            return last

        def clear_acc(dve, at_):
            nc.vector.memset(acc[:], 0.0).then_inc(acc_set, 1)
            dve.wait_ge(acc_set, at_ + 1)

        def add_square(dve, at_, k):
            dve.wait_ge(sq_ready, k + (KD * at_ + 1))
            n = k + KD * at_
            if not isinstance(n, int) or n:
                dve.wait_ge(acc_ready, n)
            nc.vector.tensor_tensor(acc[:], acc[:], sq[:, k % 2, :], ALU.add).then_inc(acc_ready, 1)

        def gate_of(dve, sub):
            dve.wait_ge(mod_freed, 6 * sub + 6)
            nc.vector.tensor_scalar(gate_v[:], mod[:, 24 * sub + 16:24 * sub + 24, :], 1.0 if sub in (1, 4) else 0.5,
                                    None, ALU.mult).then_inc(gate_ready, 1)
            dve.wait_ge(gate_ready, sub + 1)

        @block.vector
        def _(dve):
            nc.vector.memset(eps_v[:], EPS).then_inc(eps_set, 1)
            nc.vector.memset(ones[:], 1.0).then_inc(ones_set, 1)
            nc.vector.memset(mod_rows[:], 0.0).then_inc(rows_set, 1)
            dve.wait_ge(c_act, 2)
            nc.vector.tensor_tensor(c4[:, :, 2:4], csilu[:], c4[:, :, 0:2].bitcast(F32), ALU.subtract).then_inc(c_ready, 1)
            dve.wait_ge(in_bmod, 48)

            def dve_mod(m, slot, hi):
                dve.wait_ge(mod_hi_done, m + 1)
                nc.vector.tensor_tensor(raw_lo[:, slot[0], slot[1], :], raw[:, slot[0], slot[1], :], hi.bitcast(F32), ALU.subtract).then_inc(mod_lo_done, 1)

            def mod_copy(m, par):
                dve.wait_ge(mod_used, m + 1)
                nc.vector.tensor_scalar(mod_rows[32 * par:32 * par + 4, :], psum[0:4, 3 + 4 * par, 0:2 * P], 1.0, None,
                                        ALU.mult).then_inc(mod_copied, 1)

            def mod_evac(c):
                dve.wait_ge(mod_turned, c + 1)
                tiles = bass.ds(4 * c, 4)
                four = lambda buf: buf[:, tiles, :].rearrange("p (j n) g -> p j n g", j=2)
                nc.vector.tensor_tensor(four(mod), psum[:, 2, 0:8].rearrange("p (n j g) -> p j n g", n=2, j=2),
                                        four(bmod), ALU.add).then_inc(mod_freed, 1)

            def hid_evac(q, par, n, m):
                dve.wait_ge(silu_ready, n + 1)
                product = hid_f[:, m, :]
                nc.vector.tensor_tensor(two(product), two(silu_s[:, par, :]), bank2(4 * par + 2),
                                        ALU.mult).then_inc(freed, 1)
                dve.wait_ge(freed, q + 1)
                nc.vector.tensor_scalar(hid_hi[:, m, :], product, 1.0, None, ALU.mult).then_inc(mul_ready, 1)
                dve.wait_ge(mul_ready, n + 1)
                nc.vector.tensor_tensor(hid_lo[:, m, :], product, hid_hi[:, m, :].bitcast(F32),
                                        ALU.subtract).then_inc(hid_ready, 1)

            for ph in seq:
                kind, q, nxt = ph["kind"], ph["q"], ph["next"]
                if kind == "mod":
                    last = 2 * ph["mods"] - 1
                    dve_mod(0, (0, 0), w_hi[:, 0, :])
                    for m in range(last + 1):
                        if m < last:
                            dve_mod(m + 1, ((m + 1) // 2 % 2, (m + 1) % 2), w_hi[:, (m + 1) % 2, :])
                        mod_copy(m, m % 2)
                        if m % 2:
                            mod_evac(m // 2)
                        if m == 1:
                            clear_acc(dve, 0)
                        if m >= 2:
                            add_square(dve, 0, m - 2)
                elif kind == "norm":
                    n0_, sub = KD * ph["at"], ph["sub"]
                    tile0 = 24 * sub
                    if not ph["early"]:
                        dve.wait_ge(freed, q)
                        clear_acc(dve, ph["at"])
                        for k in range(KD):
                            add_square(dve, ph["at"], k)
                    if nxt:
                        dve_lo(dve, q, nxt, 0, chunk=ph["next_c"])
                        if ph["next_mod"] is not None:
                            dve_mod(2 * ph["next_mod"], ((ph["next_c"] + 1) % 2, 0), mod_hi[:])
                    dve.wait_ge(mod_freed, 6 * sub + 4)
                    if q:
                        dve.wait_ge(freed, q)
                    nc.vector.scalar_tensor_tensor(scale_v[:], mod[:, tile0 + 8:tile0 + 16, :], 1.0,
                                                   norm_g[:, 8 * sub:8 * sub + 8, :], ALU.add, ALU.mult).then_inc(vec_ready, 1)
                    if sub in (1, 4):
                        gate_of(dve, sub)
                    dve.wait_ge(vec_ready, ph["at"] + 1)
                    dve.wait_ge(root_ready, ph["at"] + 1)
                    nc.vector.reciprocal(rstd[:], root[:]).then_inc(rstd_ready, 1)
                    dve.wait_ge(rstd_ready, ph["at"] + 1)

                    def low(k):
                        dve.wait_ge(xhi_ready, n0_ + k + 1)
                        for a, b, g in SEG:
                            last = nc.vector.scalar_tensor_tensor(xn_lo[:, k, a:b], nrm[:, k % 2, a:b],
                                                                  mod[:, tile0 + k, g:g + 1],
                                                                  xn_hi[:, k, a:b].bitcast(F32), ALU.add, ALU.subtract)
                        last.then_inc(xn_ready, 1)
                    for k in range(KD):
                        if n0_ + k >= 2:
                            dve.wait_ge(xn_ready, n0_ + k - 1)
                        for a, b, g in SEG:
                            last = nc.vector.scalar_tensor_tensor(nrm[:, k % 2, a:b], x[:, k, a:b], scale_v[:, k, g:g + 1],
                                                                  rstd[:, a:b], ALU.mult, ALU.mult)
                        last.then_inc(nrm_ready, 1)
                        if k >= 1:
                            low(k - 1)
                    low(KD - 1)
                    if ph["at"] == 0:
                        dve.wait_ge(in_cst, 112)
                elif kind == "in":
                    pairs, mods = ph["n"] // 2, ph["mods"]
                    slot = (ph["c"] + 1) % 2

                    def body(i, final):
                        m = 2 * i + 2 * ph["mod"]
                        if mods:
                            mod_copy(m, 0)
                        dve_lo(dve, 2 * i + (q + 1), PIECE, 1, chunk=chunk_of(ph, i))
                        if mods:
                            dve_mod(m + 1, (slot, 1), mod_hi[:])
                        hid_evac(2 * i + q, 0, 2 * i + ph["hid"], 2 * i + ph["k0"])
                        if mods:
                            mod_copy(m + 1, 1)
                        size = nxt if final else PIECE
                        if size:
                            dve_lo(dve, 2 * i + (q + 2), size, 0, chunk=ph["next_c"] if final else chunk_of(ph, i + 1))
                        if mods and not final:
                            dve_mod(m + 2, (slot, 0), mod_hi[:])
                        hid_evac(2 * i + (q + 1), 1, 2 * i + (ph["hid"] + 1), 2 * i + (ph["k0"] + 1))
                        if mods:
                            mod_evac(i + ph["mod"])
                    if mods and not ph["after_norm"]:
                        dve_mod(2 * ph["mod"], (slot, 0), mod_hi[:])
                    with dve.Fori(0, pairs - 1) as i:
                        body(i, False)
                    body(pairs - 1, True)
                elif kind == "out":
                    size, stats = size_of(ph), ph["stats"]
                    if ph["half"] == 0:
                        gate_of(dve, ph["sub"])
                    if stats is not None:
                        clear_acc(dve, stats)

                    def body(i, final):
                        for par in range(2):
                            nsize = size if par == 0 or not final else nxt
                            if nsize:
                                chunk = i + ph["c"] + par if not final or par == 0 else ph["next_c"]
                                dve_lo(dve, 2 * i + (q + par + 1), nsize, 1 - par, chunk=chunk)
                            dve.wait_ge(used, 2 * i + (q + par + 1))
                            add_gated(dve, 2 * i + par, 4 * par).then_inc(freed, 1)
                            if stats is not None:
                                add_square(dve, stats, 2 * i + par)
                    with dve.Fori(0, KD // 2 - 1) as i:
                        body(i, False)
                    body(KD // 2 - 1, True)
                else:
                    dve_mixers[kind](dve, ph)


def layout(a):
    f = lambda v: np.ascontiguousarray(v, dtype=np.float32)
    a = {k: np.asarray(v) for k, v in a.items()}

    def cols(v):
        return np.moveaxis(v.reshape(v.shape[:-1] + (-1, P)), -1, 0)

    o = {}
    tokens = np.concatenate([a["x_prompt"][0], a["x_sample"][0]], 0)
    o["x"] = tokens.T.reshape(KD, P, T)
    o["cvec"] = np.stack([cols(a["c_ctx"]), cols(a["c"][0])], -1)
    twice = lambda v: np.repeat(v[..., None], 2, -1)
    o["bmod"] = twice(cols(a["b_mod"]).reshape(P, 144))
    o["norm_g"] = twice(cols(a["norm_g"]).reshape(P, 48))
    o["w_mod"] = a["w_mod"].reshape(2, KD, P, 18, 2, 2 * P).transpose(0, 3, 2, 4, 1, 5).reshape(36, P, 2, PIECE)
    w = a["ffn_w_in"].reshape(4, KD, P, 2, MF // 2, 2, P)
    o["w_in"] = w.transpose(0, 4, 2, 5, 1, 3, 6).reshape(4, MF // 2, P, 2, PIECE)
    w = a["ffn_w_out"].reshape(4, MF, P, KD // 2, 2, P)
    for n, (k0, kt) in enumerate(((0, HALVES[0]), HALVES)):
        o[f"w_out{n}"] = w[:, k0:k0 + kt].transpose(0, 3, 2, 4, 1, 5).reshape(4, KD // 2, P, 2, kt * P)
    w = a["ml_w_up"][0].reshape(KD, P, 2, NT // 2, 2, P)
    o["w_up"] = w.transpose(3, 1, 4, 0, 2, 5).reshape(NT // 2, P, 2, PIECE)
    w = a["ml_w_down"][0].reshape(NH, HT, P, 2, 4, P)
    o["w_heads"] = w.transpose(0, 2, 3, 4, 1, 5).reshape(NH, P, 2, PIECE)
    params = np.concatenate([a["ml_conv_w"][0].T.reshape(NT, P, CONV).transpose(1, 0, 2).reshape(P, -1),
                             cols(a["ml_conv_b"][0]), cols(a["ml_head_g"][0]), cols(a["ml_skip"][0])], 1)
    o["mlp"] = params
    o["wq3"] = a["ml_w_qkv"][0].reshape(3, NT, P // 4, 4, 4).transpose(2, 3, 0, 1, 4).reshape(P, 3, NT, 4)
    w = a["ml_w_gate"][0].reshape(2, 3, NT, P // 4, 4 * 8).transpose(3, 1, 0, 2, 4)
    o["wgr"] = np.repeat(w, 4, 0)
    o["bgate"] = np.broadcast_to(a["ml_b_gate"][0].reshape(1, 16), (P, 16))
    o["m0"] = np.broadcast_to(a["state_mlstm_m"][0, 0].reshape(1, 8), (P, 8))
    o["m0row"] = a["state_mlstm_m"][0, 0].T
    o["n0"] = cols(a["state_mlstm_n"][0, 0]).transpose(0, 2, 1, 3).reshape(P, NH, 8)
    o["c0"] = a["state_mlstm_C"][0, 0].reshape(2, NH, DH, HT, P).transpose(1, 4, 0, 3, 2)
    w = a["mla_w_in"][0]
    kr = w[:, QL + KV:]
    w = np.concatenate([w, kr], 1).reshape(KD, P, 2, 2, P)
    o["w_attn_in"] = w.transpose(1, 2, 0, 3, 4).reshape(1, P, 2, PIECE)
    w = a["mla_w_uq"][0].reshape(2, P, 2, 4, QK)
    nope = w[..., :128].reshape(2, P, 2, 4, P)
    rope = w[..., 128:].reshape(2, P, 2, 2, P)
    w = np.concatenate([nope, rope], 3)
    o["w_attn_q"] = w.transpose(1, 2, 3, 0, 4).reshape(1, P, 2, 12 * P)
    w = a["mla_w_ukv"][0].reshape(P, AH, 2, P).transpose(0, 2, 1, 3)
    o["w_attn_kv"] = w.reshape(1, P, 2, AH * P)
    w = a["mla_w_o"][0].reshape(AH, P, 2, 2, 2, P)
    o["w_attn_out"] = w.transpose(2, 1, 3, 4, 0, 5).reshape(2, P, 2, PIECE)
    g = a["mla_qk_g"][0]
    dup = lambda v: np.concatenate([v, v])
    o["attn_g"] = np.stack([g[0, :128], dup(g[0, 128:]), g[1, :128], dup(g[1, 128:]),
                            *cols(a["mla_q_norm_g"][0]).T, a["mla_kv_norm_g"][0], a["mla_kv_norm_g"][0]], 1)
    cache = a["cache_mla"][0, 0].T
    o["cache_c"] = cache[:KV]
    o["cache_r"] = np.concatenate([cache[KV:], cache[KV:]], 0)
    i = np.arange(P)
    low, high = (i[:, None] <= i[None, :]), (i[:, None] >= i[None, :])
    rot = np.zeros((P, P))
    for b in (0, 64):
        for n in range(32):
            rot[b + 32 + n, b + n] = -1.0
            rot[b + n, b + 32 + n] = 1.0
    o["cst"] = np.concatenate([np.eye(P), low, high, np.where(low, 0.0, -1e30), np.where(high, 0.0, -1e30),
                               np.repeat(i[:, None] < 64, P, 1), np.repeat(i[:, None] >= 64, P, 1), rot,
                               i[:, None] // 4 == np.arange(32)[None, :],
                               [[r % 32 < 4 and (r // 32, r % 2) == divmod(n, 2) for n in range(4)] for r in i]], 1)
    pos = np.arange(NL)
    freqs = 10000.0 ** -(np.arange(16) / 16.0)
    ang = np.concatenate([(pos // 64)[:, None] * freqs, (pos % 64)[:, None] * freqs], 1).T
    four = np.concatenate([ang] * 4, 0)
    o["ropes"] = np.stack([np.cos(four), np.sin(four)], 1)
    return {k: f(v) for k, v in o.items()}


OUTS = {"y": (KD, P, T), "new_c": (NH, 2, DH, DH), "new_n": (NH, 2, 1, DH), "new_m": (4, 2), "new_kv": (KV + 64, NP_)}


def kernel(**inputs):
    import concourse.bacc as bacc
    from concourse.bass_utils import run_bass_kernel_spmd

    nc = bacc.Bacc("TRN2", target_bir_lowering=False, num_devices=1)
    arrays = {"in_" + n: v for n, v in layout(inputs).items()}
    t = {n[3:]: nc.dram_tensor(n, v.shape, F32, kind="ExternalInput").ap() for n, v in arrays.items()}
    t.update({n: nc.dram_tensor("out_" + n, s, F32, kind="ExternalOutput").ap() for n, s in OUTS.items()})
    build(nc, t)
    r = run_bass_kernel_spmd(nc, [arrays], core_ids=[0]).results[0]
    y = r["out_y"].reshape(D, T).T
    return (np.ascontiguousarray(y[:NP_])[None], np.ascontiguousarray(y[NP_:])[None],
            np.ascontiguousarray(r["out_new_c"].transpose(1, 0, 2, 3))[None, None],
            np.ascontiguousarray(r["out_new_n"].reshape(NH, 2, DH).transpose(1, 0, 2))[None, None],
            np.ascontiguousarray(r["out_new_m"].T)[None, None],
            np.ascontiguousarray(r["out_new_kv"].T)[None, None])
```
